# Optimizing a Trainium2 kernel written in Bass

```python
import math
import jax
import jax.numpy as jnp
from jax import lax
import numpy as np

D_MODEL = 2048
BATCH = 1
SEQ = 512
DEPTH = 1

GRID_W = 64
CTX_LEN = 256

DIFF_HEADS = 8
DIFF_HALF = 64
DIFF_VDIM = 2 * DIFF_HALF
DIFF_W = DIFF_HEADS * DIFF_VDIM
MLSTM_HEADS = 8
MLSTM_DHEAD = 128
ML_W = MLSTM_HEADS * MLSTM_DHEAD
MLSTM_CONV = 5
MLSTM_CHUNK = 64
N_GATES = 4
MIX_W = DIFF_W + ML_W
IN_SPLITS = (DIFF_W, 2 * DIFF_W, 3 * DIFF_W, 3 * DIFF_W + 2 * ML_W,
             3 * DIFF_W + 3 * ML_W, 3 * DIFF_W + 4 * ML_W)
IN_COLS = 3 * DIFF_W + 4 * ML_W + N_GATES * MLSTM_HEADS
Q_BLOCK = 128
ROPE_BASE = 10000.0
PEER_HEADS = 8
PEER_NKEYS = 128
PEER_EXPERTS = PEER_NKEYS * PEER_NKEYS
PEER_DQ = 256
PEER_TOPK = 16
PEER_TOKEN_BLOCK = 128
DEEPNORM_ALPHA = (2.0 * DEPTH) ** 0.25
DEEPNORM_BETA = (8.0 * DEPTH) ** -0.25
LN_EPS = 1e-5
RMS_EPS = 1e-6

kernel_name = 'hybrid_diffattn_mlstm_peer_dit'

def layer_norm(h, g, b):
    hf = h.astype(jnp.float32)
    mu = jnp.mean(hf, -1, keepdims=True)
    var = jnp.mean(jnp.square(hf - mu), -1, keepdims=True)
    return ((hf - mu) * lax.rsqrt(var + LN_EPS) * g + b).astype(h.dtype)

def head_rms_norm(a, g):
    af = a.astype(jnp.float32)
    return af * lax.rsqrt(jnp.mean(jnp.square(af), -1, keepdims=True) + RMS_EPS) * g

def modulate(h, shift, scale):
    return h * (1.0 + scale) + shift

def to_heads(a, n_heads):
    b, t, _ = a.shape
    return a.reshape(b, t, n_heads, -1).transpose(0, 2, 1, 3)

def merge_heads(a):
    b, h, t, d = a.shape
    return a.transpose(0, 2, 1, 3).reshape(b, t, h * d)

def rope_1d(a, pos):
    nf = a.shape[-1] // 2
    inv = ROPE_BASE ** (-jnp.arange(nf, dtype=jnp.float32) / nf)
    ang = pos.astype(jnp.float32)[:, None] * inv
    cos = jnp.cos(ang).astype(a.dtype)
    sin = jnp.sin(ang).astype(a.dtype)
    a1, a2 = a[..., :nf], a[..., nf:]
    return jnp.concatenate([a1 * cos - a2 * sin, a1 * sin + a2 * cos], -1)

def axial_rope(a, row, col):
    half = a.shape[-1] // 2
    return jnp.concatenate([rope_1d(a[..., :half], row), rope_1d(a[..., half:], col)], -1)

def centred_dwconv(a, w, b):
    out = lax.conv_general_dilated(a, w[:, None, :], window_strides=(1,), padding='SAME',
                                   dimension_numbers=('NWC', 'WIO', 'NWC'),
                                   feature_group_count=a.shape[-1])
    return out + b

def in_projections(h, lp):
    b, t, _ = h.shape
    proj = h @ lp['w_in']
    dq, dk, dv, mqk, mv, mo, mg = jnp.split(proj, IN_SPLITS, axis=-1)
    mqk = jax.nn.silu(centred_dwconv(mqk, lp['conv_w'], lp['conv_b']))
    mq, mk = jnp.split(mqk, 2, axis=-1)
    gates = mg.reshape(b, t, N_GATES, MLSTM_HEADS).astype(jnp.float32) + lp['gate_b'].astype(jnp.float32)
    i_f, f_f, i_b, f_b = gates.transpose(2, 0, 3, 1)
    diff = (to_heads(dq, DIFF_HEADS), to_heads(dk, DIFF_HEADS), to_heads(dv, DIFF_HEADS))
    ml = (to_heads(mq, MLSTM_HEADS), to_heads(mk, MLSTM_HEADS) * MLSTM_DHEAD ** -0.5,
          to_heads(mv, MLSTM_HEADS), to_heads(mo, MLSTM_HEADS),
          i_f, jax.nn.log_sigmoid(f_f), i_b, jax.nn.log_sigmoid(f_b))
    return diff, ml

def diff_attention(q1, q2, k1, k2, v, lam):
    b, h, t, d = q1.shape
    nb = t // Q_BLOCK
    scale = d ** -0.5

    def blocks(a):
        return jnp.moveaxis(a.reshape(b, h, nb, Q_BLOCK, d), 2, 0)

    def one_block(qs):
        a1, a2 = qs
        s1 = jnp.einsum('bhqd,bhkd->bhqk', a1, k1).astype(jnp.float32) * scale
        s2 = jnp.einsum('bhqd,bhkd->bhqk', a2, k2).astype(jnp.float32) * scale
        w = jax.nn.softmax(s1, axis=-1) - lam * jax.nn.softmax(s2, axis=-1)
        return jnp.einsum('bhqk,bhkd->bhqd', w.astype(v.dtype), v)

    o = lax.map(one_block, (blocks(q1), blocks(q2)))
    return jnp.moveaxis(o, 0, 2).reshape(b, h, t, v.shape[-1])

def mlstm_chunkwise(q, k, v, i_pre, logf, state):
    b, h, t, d = q.shape
    nc = t // MLSTM_CHUNK
    lc = MLSTM_CHUNK

    def to_chunks(a):
        return jnp.moveaxis(a.reshape(b, h, nc, lc, *a.shape[3:]), 2, 0)

    tri = jnp.tril(jnp.ones((lc, lc), dtype=bool))

    def step(carry, inp):
        c_st, n_st, m_st = carry
        qc, kc, vc, ic, fc = inp
        bcum = jnp.cumsum(fc, axis=-1)
        log_d = bcum[..., :, None] - bcum[..., None, :] + ic[..., None, :]
        log_d = jnp.where(tri, log_d, -jnp.inf)
        inter = bcum + m_st[..., None]
        m_row = jnp.maximum(inter, jnp.max(log_d, axis=-1))
        dmat = jnp.exp(log_d - m_row[..., None])
        g_in = jnp.exp(inter - m_row)
        s = jnp.einsum('bhld,bhsd->bhls', qc, kc) * dmat
        num = jnp.einsum('bhls,bhsd->bhld', s, vc) + g_in[..., None] * jnp.einsum('bhld,bhde->bhle', qc, c_st)
        den = jnp.sum(s, axis=-1) + g_in * jnp.einsum('bhld,bhd->bhl', qc, n_st)
        h_out = num / jnp.maximum(jnp.abs(den), jnp.exp(-m_row))[..., None]
        b_last = bcum[..., -1]
        wlog = b_last[..., None] - bcum + ic
        m_new = jnp.maximum(b_last + m_st, jnp.max(wlog, axis=-1))
        wk = jnp.exp(wlog - m_new[..., None])
        decay = jnp.exp(b_last + m_st - m_new)
        c_new = decay[..., None, None] * c_st + jnp.einsum('bhl,bhld,bhle->bhde', wk, kc, vc)
        n_new = decay[..., None] * n_st + jnp.einsum('bhl,bhld->bhd', wk, kc)
        return (c_new, n_new, m_new), h_out

    state, hs = lax.scan(step, state, (to_chunks(q), to_chunks(k), to_chunks(v),
                                       to_chunks(i_pre), to_chunks(logf)))
    return jnp.moveaxis(hs, 0, 2).reshape(b, h, t, v.shape[-1]), state

def mlstm_bidir(q, k, v, i_f, lf_f, i_b, lf_b, state_f, state_b):
    h_f, st_f = mlstm_chunkwise(q, k, v, i_f, lf_f, state_f)
    flip = lambda a: jnp.flip(a, axis=2)
    h_b, st_b = mlstm_chunkwise(flip(q), flip(k), flip(v), flip(i_b), flip(lf_b), state_b)
    return h_f + flip(h_b), st_f, st_b

def zero_mlstm_state(b):
    return (jnp.zeros((b, MLSTM_HEADS, MLSTM_DHEAD, MLSTM_DHEAD), jnp.float32),
            jnp.zeros((b, MLSTM_HEADS, MLSTM_DHEAD), jnp.float32),
            jnp.zeros((b, MLSTM_HEADS), jnp.float32))

def diff_group_out(o, lp, lam_init, dtype):
    return merge_heads(head_rms_norm(o, lp['diff_norm_g']) * (1.0 - lam_init)).astype(dtype)

def mlstm_group_out(hm, mo, lp, dtype):
    out = head_rms_norm(hm, lp['mlstm_norm_g']) * jax.nn.sigmoid(mo.astype(jnp.float32))
    return merge_heads(out).astype(dtype)

def token_mixer(h, hc, lp, row, col, lam_init, need_ctx_out):
    (q, k, v), (mq, mk, mv, mo, i_f, lf_f, i_b, lf_b) = in_projections(h, lp)
    (qc, kc, vc), (mqc, mkc, mvc, moc, ic_f, lfc_f, ic_b, lfc_b) = in_projections(hc, lp)
    lq1, lk1, lq2, lk2 = lp['diff_lambda'].astype(jnp.float32)
    lam = jnp.exp(jnp.dot(lq1, lk1)) - jnp.exp(jnp.dot(lq2, lk2)) + lam_init
    q1 = axial_rope(q[..., :DIFF_HALF], row, col)
    q2 = axial_rope(q[..., DIFF_HALF:], row, col)
    k1 = axial_rope(k[..., :DIFF_HALF], row, col)
    k2 = axial_rope(k[..., DIFF_HALF:], row, col)
    kc1, kc2 = kc[..., :DIFF_HALF], kc[..., DIFF_HALF:]
    keys1 = jnp.concatenate([kc1, k1], axis=2)
    keys2 = jnp.concatenate([kc2, k2], axis=2)
    vals = jnp.concatenate([vc, v], axis=2)
    d_lat = diff_group_out(diff_attention(q1, q2, keys1, keys2, vals, lam), lp, lam_init, h.dtype)
    b = h.shape[0]
    hm_c, st_f, st_b = mlstm_bidir(mqc, mkc, mvc, ic_f, lfc_f, ic_b, lfc_b,
                                   zero_mlstm_state(b), zero_mlstm_state(b))
    hm, _, _ = mlstm_bidir(mq, mk, mv, i_f, lf_f, i_b, lf_b, st_f, st_b)
    m_lat = mlstm_group_out(hm, mo, lp, h.dtype)
    y = jnp.concatenate([d_lat, m_lat], axis=-1) @ lp['w_out']
    yc = None
    if need_ctx_out:
        qc1, qc2 = qc[..., :DIFF_HALF], qc[..., DIFF_HALF:]
        d_ctx = diff_group_out(diff_attention(qc1, qc2, kc1, kc2, vc, lam), lp, lam_init, hc.dtype)
        m_ctx = mlstm_group_out(hm_c, moc, lp, hc.dtype)
        yc = jnp.concatenate([d_ctx, m_ctx], axis=-1) @ lp['w_out']
    return y, yc

def peer_ffn(h, lp):
    b, t, d = h.shape
    half = PEER_DQ // 2
    q = (h @ lp['peer_wq']).reshape(b, t, PEER_HEADS, PEER_DQ)
    keys = lp['peer_keys']
    s1 = jnp.einsum('bthd,hkd->bthk', q[..., :half], keys[0]).astype(jnp.float32)
    s2 = jnp.einsum('bthd,hkd->bthk', q[..., half:], keys[1]).astype(jnp.float32)
    v1, i1 = lax.top_k(s1, PEER_TOPK)
    v2, i2 = lax.top_k(s2, PEER_TOPK)
    cand = (v1[..., :, None] + v2[..., None, :]).reshape(b, t, PEER_HEADS, PEER_TOPK * PEER_TOPK)
    cidx = (i1[..., :, None] * PEER_NKEYS + i2[..., None, :]).reshape(b, t, PEER_HEADS, PEER_TOPK * PEER_TOPK)
    top_s, pos = lax.top_k(cand, PEER_TOPK)
    eidx = jnp.take_along_axis(cidx, pos, axis=-1)
    gates = jax.nn.softmax(top_s, axis=-1)
    n_e = PEER_HEADS * PEER_TOPK
    nb = (b * t) // PEER_TOKEN_BLOCK
    xs = h.reshape(nb, PEER_TOKEN_BLOCK, d)
    es = eidx.reshape(nb, PEER_TOKEN_BLOCK, n_e)
    gs = gates.reshape(nb, PEER_TOKEN_BLOCK, n_e)
    u_tab, v_tab = lp['peer_u'], lp['peer_v']

    def one_block(args):
        xb, eb, gb = args
        act = jnp.einsum('td,ted->te', xb, u_tab[eb]).astype(jnp.float32)
        act = jax.nn.gelu(act, approximate=False) * gb
        return jnp.einsum('te,ted->td', act.astype(xb.dtype), v_tab[eb])

    return lax.map(one_block, (xs, es, gs)).reshape(b, t, d)

def trunk_layer(x, xc, c, c_ctx, lp, row, col, lam_init, need_ctx_out):
    sh1, sc1, g1, sh2, sc2, g2 = jnp.split((jax.nn.silu(c) @ lp['w_ada'] + lp['b_ada'])[:, None, :], 6, axis=-1)
    csh1, csc1, cg1, csh2, csc2, cg2 = jnp.split(jax.nn.silu(c_ctx) @ lp['w_ada'] + lp['b_ada'], 6, axis=-1)
    y, yc = token_mixer(modulate(x, sh1, sc1), modulate(xc, csh1, csc1), lp, row, col, lam_init, need_ctx_out)
    x = layer_norm(DEEPNORM_ALPHA * x + g1 * y, lp['ln1_g'], lp['ln1_b'])
    x = layer_norm(DEEPNORM_ALPHA * x + g2 * peer_ffn(modulate(x, sh2, sc2), lp), lp['ln2_g'], lp['ln2_b'])
    if need_ctx_out:
        xc = layer_norm(DEEPNORM_ALPHA * xc + cg1 * yc, lp['ln1_g'], lp['ln1_b'])
        xc = layer_norm(DEEPNORM_ALPHA * xc + cg2 * peer_ffn(modulate(xc, csh2, csc2), lp), lp['ln2_g'], lp['ln2_b'])
    return x, xc

def setup_inputs(seed: int = 0) -> dict:
    key = jax.random.key(seed)
    ks = jax.random.split(key, 26)
    f32 = jnp.float32
    D, L, H = D_MODEL, DEPTH, MLSTM_HEADS

    def nrm(k, shape, s):
        return s * jax.random.normal(k, shape, f32)

    fgate_bias = jnp.linspace(3.0, 6.0, H, dtype=f32)
    gate_b = jnp.stack([nrm(ks[10], (L, H), 0.1),
                        fgate_bias + nrm(ks[11], (L, H), 0.1),
                        nrm(ks[12], (L, H), 0.1),
                        fgate_bias + nrm(ks[13], (L, H), 0.1)], axis=1)
    return {
        'x': nrm(ks[0], (BATCH, SEQ, D), 1.0),
        'c': nrm(ks[1], (BATCH, D), 1.0),
        'ctx': nrm(ks[2], (BATCH, CTX_LEN, D), 1.0),
        'c_ctx': nrm(ks[3], (D,), 1.0),
        'w_ada': nrm(ks[4], (L, D, 6 * D), 0.5 * D ** -0.5),
        'b_ada': nrm(ks[5], (L, 6 * D), 0.02),
        'w_in': nrm(ks[6], (L, D, IN_COLS), D ** -0.5),
        'conv_w': nrm(ks[7], (L, MLSTM_CONV, 2 * ML_W), MLSTM_CONV ** -0.5),
        'conv_b': nrm(ks[8], (L, 2 * ML_W), 0.02),
        'gate_b': gate_b,
        'diff_lambda': nrm(ks[9], (L, 4, DIFF_HALF), 0.1),
        'diff_norm_g': 1.0 + nrm(ks[14], (L, DIFF_VDIM), 0.02),
        'mlstm_norm_g': 1.0 + nrm(ks[15], (L, MLSTM_DHEAD), 0.02),
        'w_out': nrm(ks[16], (L, MIX_W, D), DEEPNORM_BETA * MIX_W ** -0.5),
        'ln1_g': 1.0 + nrm(ks[17], (L, D), 0.02),
        'ln1_b': nrm(ks[18], (L, D), 0.02),
        'ln2_g': 1.0 + nrm(ks[19], (L, D), 0.02),
        'ln2_b': nrm(ks[20], (L, D), 0.02),
        'peer_wq': nrm(ks[21], (L, D, PEER_HEADS * PEER_DQ), D ** -0.5),
        'peer_keys': nrm(ks[22], (L, 2, PEER_HEADS, PEER_NKEYS, PEER_DQ // 2), (PEER_DQ // 2) ** -0.5),
        'peer_u': nrm(ks[23], (L, PEER_EXPERTS, D), D ** -0.5),
        'peer_v': nrm(ks[24], (L, PEER_EXPERTS, D), DEEPNORM_BETA * (PEER_HEADS * PEER_TOPK) ** -0.5),
    }

def reference(x, c, ctx, c_ctx, w_ada, b_ada, w_in, conv_w, conv_b, gate_b, diff_lambda,
              diff_norm_g, mlstm_norm_g, w_out, ln1_g, ln1_b, ln2_g, ln2_b,
              peer_wq, peer_keys, peer_u, peer_v):
    n_lat = x.shape[1]
    rows = n_lat // GRID_W
    row = jnp.repeat(jnp.arange(rows, dtype=jnp.int32), GRID_W)
    col = jnp.tile(jnp.arange(GRID_W, dtype=jnp.int32), rows)
    xc = ctx
    for l in range(DEPTH):
        lp = {'w_ada': w_ada[l], 'b_ada': b_ada[l], 'w_in': w_in[l], 'conv_w': conv_w[l],
              'conv_b': conv_b[l], 'gate_b': gate_b[l], 'diff_lambda': diff_lambda[l],
              'diff_norm_g': diff_norm_g[l], 'mlstm_norm_g': mlstm_norm_g[l], 'w_out': w_out[l],
              'ln1_g': ln1_g[l], 'ln1_b': ln1_b[l], 'ln2_g': ln2_g[l], 'ln2_b': ln2_b[l],
              'peer_wq': peer_wq[l], 'peer_keys': peer_keys[l], 'peer_u': peer_u[l], 'peer_v': peer_v[l]}
        lam_init = 0.8 - 0.6 * math.exp(-0.3 * l)
        x, xc = trunk_layer(x, xc, c, c_ctx, lp, row, col, lam_init, l < DEPTH - 1)
    return x


_drawn_inputs = setup_inputs


def setup_inputs(seed=0):
    import zlib

    import numpy as np

    out = dict(_drawn_inputs(seed))
    spreads = {}
    factors = {'ctx': 3.04,
     'b_ada': 5.445,
     'conv_w': 3.541,
     'conv_b': 8.0,
     'diff_lambda': 8.0,
     'diff_norm_g': 8.0,
     'mlstm_norm_g': 8.0,
     'ln1_g': 2.82,
     'ln1_b': 2.84,
     'ln2_g': 2.919,
     'ln2_b': 2.871,
     'peer_wq': 7.441,
     'peer_keys': 7.458,
     'peer_u': 8.0,
     'peer_v': 7.443}
    for name, (base, spread) in spreads.items():
        noise = np.random.default_rng([zlib.crc32(name.encode()), seed]).standard_normal(out[name].shape)
        drawn = base * np.exp(spread * noise) if base else spread * noise
        out[name] = jnp.asarray(drawn.astype(out[name].dtype))
    for name, factor in factors.items():
        out[name] = (out[name] * factor).astype(out[name].dtype)
    return out
```

```python
import numpy as np
from contextlib import ExitStack

import concourse.bass as bass
from concourse import mybir

P = 128
D = 2048
KT = D // P
SEQ, CTX = 512, 256
T = SEQ + CTX
LT, CT = SEQ // P, CTX // P
H = 8
HD = 128
HALF = 64
NGATES = 4
CONV = 5
PAD = CONV // 2
GRID_W = 64
TOPK = 16
NKEYS = 128
PH = 8
NEXP = PH * TOPK
ALPHA = 2.0 ** 0.25
LAM_INIT = 0.2
LN_EPS, RMS_EPS = 1e-5, 1e-6
CHUNK = 512
SH_CHUNKS = 2 * D // CHUNK
REST_CHUNKS = 4 * D // CHUNK
OUT_CHUNKS = D // CHUNK
WBUF = 7
HALVES = H * 7 * 2
NEG = -3.0e38


def program(nc, xT, x, cxT, ccol, wada, bcol, brow, wseq, wgate, gbias, convw, convb, lamv, gcol,
            wout, lnv, wq, keysT, peer_u, peer_v, consts, rope, out):
    f32, u32 = mybir.dt.float32, mybir.dt.uint32
    ALU, ACT, AX = mybir.AluOpType, mybir.ActivationFunctionType, mybir.AxisListType
    with ExitStack() as top:
        def sb(name, shape, dt=f32, ctx=top):
            return ctx.enter_context(nc.sbuf_tensor(name, shape, dt))

        def sem(name):
            return top.enter_context(nc.semaphore(name))

        PS = top.enter_context(nc.psum_tensor("PS", [P, 8, 512], f32))
        cst = sb("cst", [P, 272])
        ident, rotm, iota16 = cst[:, 0:128], cst[:, 128:256], cst[:, 256:272]
        s_passed = sem("gpsimd_waits_passed")
        silc = sb("silc", [P, 2, KT])
        neglam = sb("neglam", [P, 1])
        gains = sb("gains", [P, 2])
        mixT = sb("mixT", [P, KT, SEQ])

        phase_a = ExitStack()
        hT = sb("hT", [P, KT, T], ctx=phase_a)
        colv = sb("colv", [P, 20, H], ctx=phase_a)
        m0b = sb("m0b", [P, 2, H], ctx=phase_a)
        Mrow = sb("Mrow", [H, 2, SEQ], ctx=phase_a)

        s_small = sem("small_loaded")
        s_x = sem("inputs_loaded")
        s_wa = [sem("ada_loaded0"), sem("ada_loaded1")]
        s_sil = sem("silu_done")
        s_silrep = sem("silu_spread")
        s_ada_pe = sem("ada_summed")
        s_ada_ev = sem("ada_row_kept")
        s_modT = sem("mod_turned")
        s_mod = sem("inputs_modulated")
        s_gate_pe = sem("gates_summed")
        s_gate_ev = sem("gates_kept")
        s_gate_mv = sem("gates_moved")
        s_abs = sem("gate_abs")
        s_lf1 = sem("log1p_done")
        s_scan = sem("scans_done")
        s_ex = sem("gate_exps")
        s_dm = sem("state_max_spread_ready")
        s_col = sem("columns_turned")
        s_lamd = sem("lambda_dots")
        s_lame = sem("lambda_exps")

        b1 = ExitStack()
        wr = sb("wr", [P, 2, KT, CHUNK], ctx=b1)
        adar = wr[:, 0, 0:8, :].rearrange("p k c -> p (k c)")
        with b1:
            silA = mixT[:, 0:4, :].rearrange("p k t -> p (k t)").rearrange("p (k m) -> p k m", k=KT)
            R = mixT[:, 4:12, :].rearrange("p k t -> p (k t)")
            cc = sb("cc", [P, 2, KT], ctx=b1)
            bc = sb("bc", [P, 2 * KT], ctx=b1)
            mods = sb("mods", [P, 2 * KT, 2], ctx=b1)
            wg = mixT[:, 12:13, :].rearrange("p k t -> p (k t)").rearrange("p (k m) -> p k m", k=KT)
            gb = sb("gb", [NGATES * H, 1], ctx=b1)
            gts = sb("gts", [NGATES * H, T], ctx=b1)
            lam4 = sb("lam4", [P, 4, HALF], ctx=b1)
            lamp = sb("lamp", [P, 2, HALF], ctx=b1)
            lamd = sb("lamd", [P, 2], ctx=b1)
            lame = sb("lame", [P, 2], ctx=b1)
            gI = sb("gI", [H, 2, T], ctx=b1)
            gF = sb("gF", [H, 2, T], ctx=b1)
            gA = mixT[0:H, 13:16, :].rearrange("p k t -> p (k t)").rearrange("p (d t) -> p d t", d=2)
            gE = sb("gE", [H, 2, T], ctx=b1)
            ones8 = sb("ones8", [H, T], ctx=b1)
            m0 = sb("m0", [H, 2], ctx=b1)
            mc = sb("mc", [H, 2], ctx=b1)
            dm0 = sb("dm0", [H, 2, H], ctx=b1)

            with nc.Block() as block:
                @block.sync
                def _(sp):
                    sp.dma_start(cc[:].rearrange("p a k -> p (a k)"), ccol).then_inc(s_small, 16)
                    sp.dma_start(cst[:], consts).then_inc(s_small, 16)
                    wv = wada.rearrange("(k p) n -> p k n", p=P)
                    sp.dma_start(wr[:, 0, :, :], wv[:, :, 0:CHUNK]).then_inc(s_wa[0], 16)
                    sp.dma_start(wr[:, 1, :, :], wv[:, :, CHUNK:2 * CHUNK]).then_inc(s_wa[1], 16)
                    sp.dma_start(bc[:], bcol).then_inc(s_small, 16)
                    sp.dma_start(gb[:], gbias).then_inc(s_small, 16)
                    sp.dma_start(gains[:], gcol).then_inc(s_small, 16)
                    sp.dma_start(lam4[:].rearrange("p a d -> p (a d)"), lamv.partition_broadcast(P)).then_inc(s_small, 16)
                    sp.dma_start(wg, wgate.rearrange("(k p) g -> p k g", p=P)).then_inc(s_small, 16)
                    sp.dma_start(hT[:, :, 0:SEQ], xT.rearrange("(k p) t -> p k t", p=P)).then_inc(s_x, 16)
                    sp.dma_start(hT[:, :, SEQ:T], cxT.rearrange("(k p) t -> p k t", p=P)).then_inc(s_x, 16)
                    wv4 = wada.rearrange("(k p) (n c) -> p k n c", p=P, c=CHUNK)
                    with sp.Fori(1, SH_CHUNKS // 2) as n:
                        for j in range(2):
                            sp.wait_ge(s_ada_pe, 2 * n + j - 1)
                            sp.dma_start(wr[:, j, :, :], wv4[:, :, 2 * n + j, :]).then_inc(s_wa[j], 16)
                    sp.wait_ge(s_gate_ev, 1)
                    for g, dst in enumerate((gI[:, 0, :], gF[:, 0, :], gI[:, 1, :], gF[:, 1, :])):
                        sp.dma_start(dst, gts[g * H:(g + 1) * H, :]).then_inc(s_gate_mv, 16)

                @block.scalar
                def _(act):
                    act.wait_ge(s_small, 16 * 7)
                    act.activation(silc[:], cc[:], ACT.Silu).then_inc(s_sil, 1)
                    with act.Fori(0, SH_CHUNKS // 2) as n:
                        for j in range(2):
                            act.wait_ge(s_ada_pe, 2 * n + j + 1)
                            act.activation(R[:, bass.ds((2 * n + j) * CHUNK, CHUNK)], PS[:, j, :], ACT.Copy).then_inc(s_ada_ev, 1)
                    act.wait_ge(s_lamd, 1)
                    act.activation(lame[:], lamd[:], ACT.Exp).then_inc(s_lame, 1)
                    act.wait_ge(s_abs, 1)
                    act.activation(gE[:], gE[:], ACT.Exp, scale=-1.0)
                    act.drain()
                    act.activation(gE[:], gE[:], ACT.Ln, bias=1.0).then_inc(s_lf1, 1)
                    act.wait_ge(s_scan, 1)
                    act.activation(gE[:], gA, ACT.Exp).then_inc(s_ex, 1)

                @block.tensor
                def _(pe):
                    pe.wait_ge(s_silrep, 1)
                    with pe.Fori(0, SH_CHUNKS // 2) as n:
                        for j in range(2):
                            pe.wait_ge(s_wa[j], 16 * n + 16)
                            pe.wait_ge(s_ada_ev, 2 * n + j + 1)
                            for k in range(KT):
                                last = pe.matmul(PS[:, j, :], silA[:, k, :], wr[:, j, k, :], start=(k == 0), stop=(k == KT - 1))
                            last.then_inc(s_ada_pe, 1)
                    pe.wait_ge(s_ada_ev, SH_CHUNKS + 2)
                    for j in range(2 * KT):
                        last = pe.matmul(PS[:, 2, 2 * j:2 * j + 2], R[:, j * P:(j + 1) * P], ident[:, 0:65:64], start=True, stop=True)
                    last.then_inc(s_modT, 1)
                    for k in range(KT):
                        if k % 4 == 0:
                            pe.wait_ge(s_mod, k // 4 + 1)
                        pe.matmul(PS[0:32, 3, :], wg[:, k, :], hT[:, k, 0:SEQ], start=(k == 0), stop=(k == KT - 1))
                        last = pe.matmul(PS[0:32, 4, 0:CTX], wg[:, k, :], hT[:, k, SEQ:T], start=(k == 0), stop=(k == KT - 1))
                    last.then_inc(s_gate_pe, 1)
                    pe.wait_ge(s_ex, 1)
                    for d in range(2):
                        for t in range(LT):
                            pe.transpose(PS[:, 5, (d * LT + t) * H:(d * LT + t + 1) * H], gI[:, d, t * P:(t + 1) * P], ident[0:H, 0:H])
                            pe.transpose(PS[:, 5, (8 + d * LT + t) * H:(9 + d * LT + t) * H], gE[:, d, t * P:(t + 1) * P], ident[0:H, 0:H])
                        for t in range(CT):
                            pe.transpose(PS[:, 5, (16 + d * CT + t) * H:(17 + d * CT + t) * H],
                                         gE[:, d, SEQ + t * P:SEQ + (t + 1) * P], ident[0:H, 0:H])
                    pe.wait_ge(s_dm, 1)
                    pe.matmul(PS[:, 6, 0:2 * H], ones8[:, 0:P], dm0[:].rearrange("p a b -> p (a b)"), start=True, stop=True).then_inc(s_col, 1)

                @block.vector
                def _(dve):
                    dve.memset(ones8[:], 1.0)
                    for _ in range(2):
                        dve.drain().then_inc(s_ada_ev, 1)
                    dve.wait_ge(s_sil, 1)
                    for a in range(2):
                        last = dve.tensor_copy(silA[:, :, 64 * a:64 * a + 64], silc[:, a, :].unsqueeze(2).to_broadcast([P, KT, 64]))
                    last.then_inc(s_silrep, 1)
                    dve.tensor_tensor(lamp[:], lam4[:, 0:4:2, :], lam4[:, 1:4:2, :], ALU.mult)
                    dve.drain()
                    dve.tensor_reduce(lamd[:], lamp[:], AX.X, ALU.add).then_inc(s_lamd, 1)
                    dve.wait_ge(s_lame, 1)
                    dve.tensor_tensor(neglam[:], lame[:, 1:2], lame[:, 0:1], ALU.subtract)
                    dve.tensor_scalar(gains[:, 0:1], gains[:, 0:1], 1.0 - LAM_INIT, None, ALU.mult)
                    dve.drain()
                    dve.tensor_scalar(neglam[:], neglam[:], -LAM_INIT, None, ALU.add)
                    dve.wait_ge(s_modT, 1)
                    dve.tensor_tensor(mods[:], PS[:, 2, 0:4 * KT].rearrange("p (k a) -> p k a", a=2),
                                      bc[:].unsqueeze(2).to_broadcast([P, 2 * KT, 2]), ALU.add)
                    dve.drain()
                    dve.tensor_scalar(mods[:, KT:2 * KT, :], mods[:, KT:2 * KT, :], 1.0, None, ALU.add)
                    dve.drain()
                    dve.wait_ge(s_x, 32)
                    for k in range(KT):
                        for a, (t0, t1) in enumerate(((0, SEQ), (SEQ, T))):
                            last = dve.tensor_scalar(hT[:, k, t0:t1], hT[:, k, t0:t1], mods[:, KT + k, a:a + 1],
                                                     mods[:, k, a:a + 1], ALU.mult, ALU.add)
                        if k % 4 == 3:
                            last.then_inc(s_mod, 1)
                    dve.wait_ge(s_gate_pe, 1)
                    dve.tensor_scalar(gts[:, 0:SEQ], PS[0:32, 3, :], gb[:, 0:1], None, ALU.add)
                    dve.tensor_scalar(gts[:, SEQ:T], PS[0:32, 4, 0:CTX], gb[:, 0:1], None, ALU.add).then_inc(s_gate_ev, 1)
                    dve.wait_ge(s_gate_mv, 64)
                    dve.scalar_tensor_tensor(gE[:], gF[:], -1.0, gF[:], ALU.mult, ALU.max).then_inc(s_abs, 1)
                    dve.tensor_scalar(gF[:], gF[:], 0.0, None, ALU.min)
                    dve.drain()
                    dve.wait_ge(s_lf1, 1)
                    dve.tensor_tensor(gF[:], gF[:], gE[:], ALU.subtract)
                    dve.drain()
                    for d in range(2):
                        for t0, t1 in ((0, SEQ), (SEQ, T)):
                            o, i = gA[:, d, t0:t1], gF[:, d, t0:t1]
                            if d:
                                o, i = o[:, ::-1], i[:, ::-1]
                            dve.tensor_tensor_scan(out=o, data0=ones8[:, 0:t1 - t0], data1=i, initial=0.0, op0=ALU.mult, op1=ALU.add)
                    dve.drain()
                    dve.tensor_tensor(gI[:], gI[:], gA, ALU.subtract)
                    dve.drain()
                    dve.tensor_reduce(mc[:], gI[:, :, SEQ:T], AX.X, ALU.max)
                    dve.drain()
                    dve.tensor_scalar(mc[:], mc[:], 0.0, None, ALU.max)
                    dve.drain()
                    dve.tensor_tensor(m0[:, 0:1], mc[:, 0:1], gA[:, 0, T - 1:T], ALU.add)
                    dve.tensor_tensor(m0[:, 1:2], mc[:, 1:2], gA[:, 1, SEQ:SEQ + 1], ALU.add)
                    dve.drain()
                    for d in range(2):
                        dve.tensor_scalar(dm0[:, d, :], ident[0:H, 0:H], m0[:, d:d + 1], None, ALU.mult)
                        o, i = Mrow[:, d, :], gI[:, d, 0:SEQ]
                        if d:
                            o, i = o[:, ::-1], i[:, ::-1]
                        dve.tensor_tensor_scan(out=o, data0=i, data1=i, initial=m0[:, d:d + 1], op0=ALU.max, op1=ALU.max)
                        dve.tensor_scalar(gA[:, d, SEQ:T], gI[:, d, SEQ:T], mc[:, d:d + 1], None, ALU.subtract)
                    dve.drain().then_inc(s_dm, 1)
                    dve.scalar_tensor_tensor(gA[:, :, 0:SEQ], gA[:, :, 0:SEQ], -1.0, Mrow[:], ALU.mult, ALU.subtract).then_inc(s_scan, 1)
                    dve.wait_ge(s_col, 1)
                    dve.tensor_copy(colv[:].rearrange("p a h -> p (a h)"), PS[:, 5, 0:20 * H])
                    dve.tensor_copy(m0b[:].rearrange("p a h -> p (a h)"), PS[:, 6, 0:2 * H])

        w_loaded = [sem(f"proj_weights_loaded{i}") for i in range(WBUF)]
        s_tab = sem("tables_loaded")
        pe_half, act_evac = sem("proj_halves_summed"), sem("proj_kept")
        dve_conv, act_silu = sem("conv_done"), sem("conv_silu_done")
        pe_m1, act_m1, dve_m1 = sem("ml_v_turned"), sem("ml_v_kept"), sem("ml_ctx_keys_weighted")
        pe_m2, act_g, act_d = sem("ml_state_and_max_summed"), sem("ml_state_decay"), sem("ml_decay")
        pool_d, pe_st, dve_sd = sem("ml_decay_masked"), sem("ml_scores"), sem("ml_scores_decayed")
        dve_qg, pe_n, dve_n = sem("ml_queries_decayed"), sem("ml_sums"), sem("ml_divided")
        dve_ss, act_rs, dve_hn = sem("ml_squares"), sem("ml_rms"), sem("ml_normed")
        pe_m5, dve_mlout = sem("ml_out_turned"), sem("ml_out_kept")
        pe_rot, act_v = sem("rotated"), sem("values_kept")
        dve_rope, pe_s, dve_max = sem("rope_done"), sem("scores"), sem("scores_max")
        act_exp, dve_w, pe_t = sem("scores_exp"), sem("weights"), sem("weights_turned")
        act_wt, pe_p, dve_pn = sem("weights_kept"), sem("values_summed"), sem("attention_kept")
        dve_as, act_as, dve_an = sem("at_squares"), sem("at_rms"), sem("at_normed")
        pe_o, dve_dout = sem("at_out_turned"), sem("at_out_kept")

        with phase_a:
            W = sb("W", [P, WBUF, 8, P], ctx=phase_a)
            rp = sb("rp", [P, 2, SEQ], ctx=phase_a)
            cw = sb("cw", [P, 2 * H, CONV], ctx=phase_a)
            cb = sb("cb", [P, 2 * H], ctx=phase_a)
            rawq = sb("rawq", [P, SEQ + 2 * PAD], ctx=phase_a)
            rawk = sb("rawk", [P, SEQ + 2 * PAD], ctx=phase_a)
            rawc = sb("rawc", [P, CTX + 2 * PAD], ctx=phase_a)
            mq = sb("mq", [P, SEQ], ctx=phase_a)
            mk = sb("mk", [P, T], ctx=phase_a)
            mvT = sb("mvT", [P, T], ctx=phase_a)
            sig = sb("sig", [P, SEQ], ctx=phase_a)
            vaug = sb("vaug", [P, LT + CT, HD + 2], ctx=phase_a)
            kw = sb("kw", [P, 2, CT, HD], ctx=phase_a)
            onesH = sb("onesH", [H, P], ctx=phase_a)
            C0 = sb("C0", [P, 2, HD + 1], ctx=phase_a)
            Mh = sb("Mh", [H, 2, SEQ], ctx=phase_a)
            G = sb("G", [P, 2, SEQ], ctx=phase_a)
            DM = sb("DM", [P, 2, 2, SEQ], ctx=phase_a)
            SD = sb("SD", [P, 2, LT, SEQ], ctx=phase_a)
            den = sb("den", [P, 2], ctx=phase_a)
            hf = sb("hf", [P, HD], ctx=phase_a)
            hn = sb("hn", [P, LT, HD], ctx=phase_a)
            sqd = sb("sqd", [P, HD], ctx=phase_a)
            ss = sb("ss", [P, 2, LT], ctx=phase_a)
            rawdq = sb("rawdq", [P, SEQ], ctx=phase_a)
            rawdk = sb("rawdk", [P, SEQ], ctx=phase_a)
            qz = sb("qz", [P, 2, SEQ], ctx=phase_a)
            kk = sb("kk", [P, T], ctx=phase_a)
            dvT = mvT
            V = sb("V", [P, LT + CT, HD], ctx=phase_a)
            dmflat = DM[:].rearrange("p a b t -> p (a b t)")
            E = dmflat[:, 0:2 * T].rearrange("p (a t) -> p a t", a=2)
            Wt = sb("Wt", [P, T], ctx=phase_a)
            WT = sb("WT", [P, LT + CT, P], ctx=phase_a)
            tq, tr = E[:, 0, 0:SEQ], E[:, 1, 0:SEQ]
            mx = sb("mx", [P, 4], ctx=phase_a)
            nm = sb("nm", [P, 2], ctx=phase_a)
            Z = sb("Z", [P, 2, 2], ctx=phase_a)
            rz = sb("rz", [P, 2], ctx=phase_a)
            on = sb("on", [P, LT, HD], ctx=phase_a)

            MLK, DFK = ("mq", "mk", "mv", "mo"), ("dq", "dk", "dv")
            HAS_CTX = {"mk", "mv", "dk", "dv"}
            BANK = {"mq": 0, "mk": 1, "mv": 0, "mo": 1, "dq": 0, "dk": 1, "dv": 0}
            TILE = {k: i for i, k in enumerate(MLK + DFK)}
            CTXBANK = 2

            def spans(d, st):
                return (st * P, SEQ) if d == 0 else (0, (st + 1) * P)

            with nc.Block() as block:
                @block.sync
                def _(sp):
                    sp.dma_start(rp[:].rearrange("p a t -> p (a t)"), rope).then_inc(s_tab, 16)
                    sp.dma_start(cw[:].rearrange("p a t -> p (a t)"), convw).then_inc(s_tab, 16)
                    sp.dma_start(cb[:], convb).then_inc(s_tab, 16)
                    for b in range(WBUF):
                        sp.dma_start(W[:, b, :, :], wseq[b]).then_inc(w_loaded[b], 16)
                    with sp.Fori(1, HALVES // WBUF) as r:
                        for b in range(WBUF):
                            sp.wait_ge(pe_half, WBUF * r + b - WBUF + 1)
                            sp.dma_start(W[:, b, :, :], wseq[WBUF * r + b]).then_inc(w_loaded[b], 16)

                @block.tensor
                def _(pe):
                    B = lambda i: PS[:, i, :]

                    def half(h, kind, j):
                        ml = kind in MLK
                        i = 2 * (MLK.index(kind) if ml else DFK.index(kind)) + j
                        s = i if ml else 8 + i
                        b = s % WBUF
                        pe.wait_ge(w_loaded[b], 16 * (2 * h + s // WBUF + 1))
                        bank = BANK[kind]
                        if j == 0:
                            before = {"mq": 0, "mk": 0, "mv": 1, "mo": 2, "dq": 3, "dk": 4, "dv": 5}[kind]
                            if before or not isinstance(h, int):
                                pe.wait_ge(act_evac, 7 * h + before)
                        for k in range(8):
                            last = pe.matmul(B(bank), W[:, b, k, :], hT[:, 8 * j + k, 0:SEQ], start=(j + k == 0), stop=(j * k == 7))
                        if kind in HAS_CTX:
                            if j == 0 and kind in ("mv", "dv"):
                                pe.wait_ge(act_evac, 7 * h + TILE[kind])
                            for k in range(8):
                                last = pe.matmul(PS[:, CTXBANK, 0:CTX], W[:, b, k, :], hT[:, 8 * j + k, SEQ:T],
                                                 start=(j + k == 0), stop=(j * k == 7))
                        last.then_inc(pe_half, 1)

                    def m1(h):
                        pe.wait_ge(dve_dout, h + 1)
                        pe.wait_ge(act_evac, 7 * h + 3)
                        pe.wait_ge(act_silu, 2 * h + 2)
                        for t in range(LT):
                            pe.transpose(PS[:, 6, t * P:(t + 1) * P], mvT[:, t * P:(t + 1) * P], ident)
                        for t in range(CT):
                            pe.transpose(PS[:, 7, t * P:(t + 1) * P], mvT[:, SEQ + t * P:SEQ + (t + 1) * P], ident)
                            last = pe.transpose(PS[:, 7, (2 + t) * P:(3 + t) * P], mk[:, SEQ + t * P:SEQ + (t + 1) * P], ident)
                        last.then_inc(pe_m1, 1)

                    def m2(h):
                        pe.wait_ge(dve_m1, h + 1)
                        for d in range(2):
                            for t in range(CT):
                                pe.matmul(PS[:, 5, 256 * d:256 * d + HD + 1], kw[:, d, t, :], vaug[:, LT + t, 0:HD + 1],
                                          start=(t == 0), stop=(t == CT - 1))
                        for d in range(2):
                            last = pe.matmul(B(3 + d), onesH[:], Mh[:, d, :], start=True, stop=True)
                        last.then_inc(pe_m2, 1)

                    def st(h, t):
                        if t == 0:
                            pe.wait_ge(act_m1, h + 1)
                        elif t >= 2:
                            pe.wait_ge(dve_sd, 4 * h + t - 1)
                        pe.matmul(B(6 + t % 2), mk[:, t * P:(t + 1) * P], mq[:], start=True, stop=True).then_inc(pe_st, 1)

                    def nsum(h, t):
                        if t == 0:
                            pe.wait_ge(dve_sd, 4 * h + 4)
                            pe.wait_ge(dve_qg, h + 1)
                        elif t == 1:
                            pe.wait_ge(act_d, 4 * h + 4)
                        else:
                            pe.wait_ge(dve_n, 4 * h + t - 1)
                        bank = 5 if t % 2 == 0 else 3
                        for d in range(2):
                            o = PS[:, bank, 256 * d:256 * d + HD + 1]
                            for n, s in enumerate(range(0, t + 1) if d == 0 else range(t, LT)):
                                pe.matmul(o, SD[:, d, s, t * P:(t + 1) * P], vaug[:, s, 0:HD + 1], start=(n == 0), stop=False)
                            last = pe.matmul(o, G[:, d, t * P:(t + 1) * P], C0[:, d, :], start=False, stop=True)
                        last.then_inc(pe_n, 1)

                    def m5(h):
                        pe.wait_ge(dve_hn, h + 1)
                        for t in range(LT):
                            last = pe.transpose(PS[:, 4, t * P:(t + 1) * P], hn[:, t, :], ident)
                        last.then_inc(pe_m5, 1)

                    def rot(h):
                        pe.wait_ge(dve_mlout, h + 1)
                        pe.wait_ge(act_evac, 7 * h + 7)
                        pe.matmul(B(3), rotm, rawdq[:], start=True, stop=True)
                        pe.matmul(B(4), rotm, rawdk[:], start=True, stop=True)
                        for t in range(LT):
                            pe.transpose(PS[:, 6, t * P:(t + 1) * P], dvT[:, t * P:(t + 1) * P], ident)
                        for t in range(CT):
                            last = pe.transpose(PS[:, 7, t * P:(t + 1) * P], dvT[:, SEQ + t * P:SEQ + (t + 1) * P], ident)
                        last.then_inc(pe_rot, 1)

                    def scores(h, q):
                        if q == 0:
                            pe.wait_ge(dve_rope, h + 1)
                        else:
                            pe.wait_ge(act_exp, 4 * h + q)
                        for a in range(2):
                            pe.matmul(B(3 + a), qz[:, a, q * P:(q + 1) * P], kk[:, 0:SEQ], start=True, stop=True)
                            last = pe.matmul(PS[:, 5, a * CTX:(a + 1) * CTX], qz[:, a, q * P:(q + 1) * P], kk[:, SEQ:T], start=True, stop=True)
                        last.then_inc(pe_s, 1)

                    def turn(h, q):
                        pe.wait_ge(dve_w, 4 * h + q + 1)
                        if q == 0:
                            pe.wait_ge(act_v, h + 1)
                        else:
                            pe.wait_ge(dve_pn, 4 * h + q)
                        for t in range(LT + CT):
                            last = pe.transpose(PS[:, 6 + t // 4, (t % 4) * P:(t % 4 + 1) * P], Wt[:, t * P:(t + 1) * P], ident)
                        last.then_inc(pe_t, 1)

                    def pv(h, q):
                        pe.wait_ge(act_wt, 4 * h + q + 1)
                        for t in range(LT + CT):
                            last = pe.matmul(PS[:, 7, 256:384], WT[:, t, :], V[:, t, :], start=(t == 0), stop=(t == LT + CT - 1))
                        last.then_inc(pe_p, 1)

                    def outT(h):
                        pe.wait_ge(dve_an, h + 1)
                        for t in range(LT):
                            last = pe.transpose(PS[:, 6, t * P:(t + 1) * P], on[:, t, :], ident)
                        last.then_inc(pe_o, 1)

                    def stage_a(h):
                        half(h, "dq", 0); m1(h); half(h, "dq", 1); m2(h)
                        half(h, "dk", 0); st(h, 0); st(h, 1); half(h, "dk", 1); st(h, 2); st(h, 3)
                        half(h, "dv", 0); nsum(h, 0); nsum(h, 1); half(h, "dv", 1); nsum(h, 2); nsum(h, 3)
                        m5(h)

                    def stage_b(h, proj):
                        g = h + 1
                        if proj: half(g, "mq", 0)
                        rot(h)
                        if proj: half(g, "mq", 1)
                        scores(h, 0)
                        if proj: half(g, "mk", 0)
                        turn(h, 0); scores(h, 1)
                        if proj: half(g, "mk", 1)
                        pv(h, 0)
                        if proj: half(g, "mv", 0)
                        turn(h, 1); scores(h, 2)
                        if proj: half(g, "mv", 1)
                        pv(h, 1)
                        if proj: half(g, "mo", 0)
                        turn(h, 2); scores(h, 3)
                        if proj: half(g, "mo", 1)
                        pv(h, 2); turn(h, 3); pv(h, 3); outT(h)

                    pe.wait_ge(s_tab, 48 + 1)
                    for kind in MLK:
                        half(0, kind, 0)
                        half(0, kind, 1)
                    with pe.Fori(0, H - 1) as h:
                        stage_a(h)
                        stage_b(h, True)
                    stage_a(H - 1)
                    stage_b(H - 1, False)

                @block.scalar
                def _(act):
                    def keep_mq(h):
                        act.wait_ge(pe_half, 14 * h + 2)
                        if not (isinstance(h, int) and h == 0):
                            act.wait_ge(dve_mlout, h)
                        else:
                            act.wait_ge(s_tab, 48 + 1)
                        act.activation(rawq[:, PAD:PAD + SEQ], PS[:, 0, :], ACT.Copy).then_inc(act_evac, 1)

                    def keep_mk(h):
                        act.wait_ge(pe_half, 14 * h + 4)
                        act.activation(rawk[:, PAD:PAD + SEQ], PS[:, 1, :], ACT.Copy)
                        act.activation(rawc[:, PAD:PAD + CTX], PS[:, 2, 0:CTX], ACT.Copy).then_inc(act_evac, 1)

                    def keep_mv(h):
                        act.wait_ge(pe_half, 14 * h + 6)
                        act.activation(mvT[:, 0:SEQ], PS[:, 0, :], ACT.Copy)
                        act.activation(mvT[:, SEQ:T], PS[:, 2, 0:CTX], ACT.Copy).then_inc(act_evac, 1)

                    def keep_mo(h):
                        act.wait_ge(pe_half, 14 * h + 8)
                        act.activation(sig[:], PS[:, 1, :], ACT.Sigmoid).then_inc(act_evac, 1)

                    def silu_q(h):
                        act.wait_ge(dve_conv, 2 * h + 1)
                        act.activation(mq[:], mq[:], ACT.Silu).then_inc(act_silu, 1)

                    def silu_k(h):
                        act.wait_ge(dve_conv, 2 * h + 2)
                        act.activation(mk[:], mk[:], ACT.Silu).then_inc(act_silu, 1)

                    def keep_v(h):
                        act.wait_ge(pe_m1, h + 1)
                        act.activation(vaug[:, 0:LT, 0:HD], PS[:, 6, :].rearrange("p (t c) -> p t c", c=HD), ACT.Copy).then_inc(act_m1, 1)

                    def state_decay(h):
                        act.wait_ge(pe_m2, h + 1)
                        act.activation(C0[:], PS[:, 5, :].rearrange("p (d c) -> p d c", d=2)[:, :, 0:HD + 1], ACT.Copy)
                        for d in range(2):
                            last = act.activation(G[:, d, :], PS[:, 3 + d, :], ACT.Exp, scale=-1.0, bias=m0b[:, d, bass.ds(h, 1)])
                        last.then_inc(act_g, 1)

                    def decay(h, t):
                        if t >= 2:
                            act.wait_ge(dve_sd, 4 * h + t - 1)
                        for d in range(2):
                            l0, l1 = spans(d, t)
                            last = act.activation(DM[:, t % 2, d, l0:l1], PS[:, 3 + d, l0:l1], ACT.Exp, scale=-1.0,
                                                  bias=colv[:, d * LT + t, bass.ds(h, 1)])
                        last.then_inc(act_d, 1)

                    def rms(i, ready, n, done):
                        act.wait_ge(ready, n)
                        act.activation(ss[:, i, :], ss[:, i, :], ACT.Ln)
                        act.drain()
                        act.activation(ss[:, i, :], ss[:, i, :], ACT.Exp, scale=-0.5).then_inc(done, 1)

                    def keep_dq(h):
                        act.wait_ge(pe_half, 14 * h + 10)
                        act.wait_ge(dve_dout, h + 1)
                        act.activation(rawdq[:], PS[:, 0, :], ACT.Copy).then_inc(act_evac, 1)

                    def keep_dk(h):
                        act.wait_ge(pe_half, 14 * h + 12)
                        act.activation(rawdk[:], PS[:, 1, :], ACT.Copy)
                        act.activation(kk[:, SEQ:T], PS[:, 2, 0:CTX], ACT.Copy).then_inc(act_evac, 1)

                    def keep_dv(h):
                        act.wait_ge(pe_half, 14 * h + 14)
                        act.activation(dvT[:, 0:SEQ], PS[:, 0, :], ACT.Copy)
                        act.activation(dvT[:, SEQ:T], PS[:, 2, 0:CTX], ACT.Copy).then_inc(act_evac, 1)

                    def keep_values(h):
                        act.wait_ge(pe_rot, h + 1)
                        act.activation(V[:, 0:LT, :], PS[:, 6, :].rearrange("p (t c) -> p t c", c=HD), ACT.Copy)
                        act.activation(V[:, LT:LT + CT, :], PS[:, 7, 0:CTX].rearrange("p (t c) -> p t c", c=HD), ACT.Copy).then_inc(act_v, 1)

                    def exps(h, q):
                        act.wait_ge(dve_max, 4 * h + q + 1)
                        for a in range(2):
                            act.activation(E[:, a, 0:SEQ], PS[:, 3 + a, :], ACT.Exp, scale=HALF ** -0.5, bias=nm[:, a:a + 1],
                                           accum_out=Z[:, 0, a:a + 1])
                            last = act.activation(E[:, a, SEQ:T], PS[:, 5, a * CTX:(a + 1) * CTX], ACT.Exp, scale=HALF ** -0.5,
                                                  bias=nm[:, a:a + 1], accum_out=Z[:, 1, a:a + 1])
                        last.then_inc(act_exp, 1)

                    def keep_wt(h, q):
                        act.wait_ge(pe_t, 4 * h + q + 1)
                        act.activation(WT[:].rearrange("p t c -> p (t c)"), PS[:, 6:8, :].rearrange("p b c -> p (b c)")[:, 0:T], ACT.Copy).then_inc(act_wt, 1)

                    def stage_a(h):
                        keep_v(h); keep_dq(h); state_decay(h); decay(h, 0); decay(h, 1); decay(h, 2); decay(h, 3)
                        keep_dk(h); keep_dv(h); rms(0, dve_ss, h + 1, act_rs)

                    def stage_b(h, proj):
                        g = h + 1
                        keep_values(h)
                        if proj: keep_mq(g)
                        exps(h, 0)
                        keep_wt(h, 0)
                        exps(h, 1)
                        if proj: keep_mk(g); silu_q(g)
                        keep_wt(h, 1)
                        exps(h, 2)
                        if proj: keep_mv(g)
                        keep_wt(h, 2)
                        exps(h, 3)
                        if proj: silu_k(g); keep_mo(g)
                        keep_wt(h, 3)
                        rms(1, dve_as, h + 1, act_as)

                    keep_mq(0); keep_mk(0); silu_q(0); keep_mv(0); silu_k(0); keep_mo(0)
                    with act.Fori(0, H - 1) as h:
                        stage_a(h)
                        stage_b(h, True)
                    stage_a(H - 1)
                    stage_b(H - 1, False)

                @block.gpsimd
                def _(pool):
                    def mask(h):
                        for t in range(LT):
                            pool.wait_ge(act_d, 4 * h + t + 1)
                            pool.sem_inc(s_passed)
                            for d, sign in ((0, 1), (1, -1)):
                                blk = DM[:, t % 2, d, t * P:(t + 1) * P]
                                last = pool.affine_select(out=blk, in_=blk, pattern=[[sign, P]], compare_op=ALU.is_ge, fill=0.0,
                                                          base=0, channel_multiplier=-sign)
                            last.then_inc(pool_d, 1)
                    with pool.Fori(0, H) as h:
                        mask(h)

                @block.vector
                def _(dve):
                    def conv(o, raw, n, c):
                        dve.tensor_scalar(o, raw[:, 0:n], cw[:, c, 0:1], cb[:, bass.ds(c, 1)], ALU.mult, ALU.add)
                        for j in range(1, CONV):
                            dve.drain()
                            last = dve.scalar_tensor_tensor(o, raw[:, j:j + n], cw[:, c, j:j + 1], o, ALU.mult, ALU.add)
                        return last

                    def conv_q(h):
                        dve.wait_ge(act_evac, 7 * h + 1)
                        conv(mq[:], rawq, SEQ, h).then_inc(dve_conv, 1)

                    def conv_k(h):
                        dve.wait_ge(act_evac, 7 * h + 2)
                        conv(mk[:, 0:SEQ], rawk, SEQ, h + H)
                        conv(mk[:, SEQ:T], rawc, CTX, h + H).then_inc(dve_conv, 1)

                    def ctx_keys(h):
                        dve.tensor_scalar(Mh[:].rearrange("p d t -> p (d t)"), Mrow[:].rearrange("p d t -> p (d t)"),
                                          ident[0:H, bass.ds(h, 1)], None, ALU.mult)
                        dve.wait_ge(pe_m1, h + 1)
                        dve.tensor_copy(vaug[:, LT:LT + CT, 0:HD], PS[:, 7, 0:CTX].rearrange("p (t c) -> p t c", c=HD))
                        for d in range(2):
                            for t in range(CT):
                                last = dve.tensor_scalar(kw[:, d, t, :], PS[:, 7, (2 + t) * P:(3 + t) * P],
                                                         colv[:, 16 + d * CT + t, bass.ds(h, 1)], HD ** -0.5, ALU.mult, ALU.mult)
                        last.then_inc(dve_m1, 1)

                    def decayed_queries(h):
                        dve.wait_ge(act_g, h + 1)
                        for d in range(2):
                            last = dve.tensor_tensor(G[:, d, :], G[:, d, :], mq[:], ALU.mult)
                        last.then_inc(dve_qg, 1)

                    def decayed_scores(h, t):
                        dve.wait_ge(pool_d, 4 * h + t + 1)
                        dve.wait_ge(pe_st, 4 * h + t + 1)
                        for d in range(2):
                            l0, l1 = spans(d, t)
                            last = dve.scalar_tensor_tensor(SD[:, d, t, l0:l1], PS[:, 6 + t % 2, l0:l1], HD ** -0.5, DM[:, t % 2, d, l0:l1],
                                                            ALU.mult, ALU.mult)
                        last.then_inc(dve_sd, 1)

                    def squares(o, src):
                        dve.scalar_tensor_tensor(sqd[:], src, 1.0, src, ALU.mult, ALU.mult, accum_out=o)

                    def mean_eps(i):
                        dve.drain()
                        dve.tensor_scalar(ss[:, i, :], ss[:, i, :], 1.0 / HD, RMS_EPS, ALU.mult, ALU.add)

                    def divide(h, t):
                        dve.wait_ge(pe_n, 4 * h + t + 1)
                        bank = PS[:, 5 if t % 2 == 0 else 3, :].rearrange("p (d c) -> p d c", d=2)
                        dsum = bank[:, :, HD:HD + 1].rearrange("p d c -> p (d c)")
                        floor = colv[:, 8 + t:8 + t + LT + 1:LT, bass.ds(h, 1)].rearrange("p d c -> p (d c)")
                        dve.scalar_tensor_tensor(den[:], dsum, -1.0, floor, ALU.mult, ALU.max)
                        dve.drain()
                        dve.tensor_tensor(den[:], dsum, den[:], ALU.max)
                        dve.drain()
                        dve.reciprocal(den[:], den[:])
                        dve.drain()
                        dve.tensor_scalar(hf[:], bank[:, 0, 0:HD], den[:, 0:1], None, ALU.mult)
                        dve.drain()
                        dve.scalar_tensor_tensor(hn[:, t, :], bank[:, 1, 0:HD], den[:, 1:2], hf[:], ALU.mult, ALU.add).then_inc(dve_n, 1)
                        dve.drain()
                        squares(ss[:, 0, t:t + 1], hn[:, t, :])

                    def ml_norm(h):
                        mean_eps(0)
                        dve.drain().then_inc(dve_ss, 1)
                        dve.wait_ge(act_rs, h + 1)
                        dve.tensor_tensor(hn[:], hn[:], ss[:, 0, :].unsqueeze(2).to_broadcast([P, LT, HD]), ALU.mult).then_inc(dve_hn, 1)
                        dve.wait_ge(pe_m5, h + 1)
                        dve.scalar_tensor_tensor(mixT[:, bass.ds(h + H, 1), :].rearrange("p a t -> p (a t)"), PS[:, 4, :], gains[:, 1:2], sig[:], ALU.mult, ALU.mult).then_inc(dve_mlout, 1)

                    def rope_qk(h):
                        dve.wait_ge(pe_rot, h + 1)
                        for raw, bank in ((rawdq, 3), (rawdk, 4)):
                            dve.tensor_tensor(tq, raw[:], rp[:, 0, :], ALU.mult)
                            dve.tensor_tensor(tr, PS[:, bank, :], rp[:, 1, :], ALU.mult)
                            dve.drain()
                            if bank == 3:
                                for a in range(2):
                                    r = slice(HALF * a, HALF * (a + 1))
                                    last = dve.tensor_tensor(qz[r, a, :], tq[r, :], tr[r, :], ALU.add)
                            else:
                                last = dve.tensor_tensor(kk[:, 0:SEQ], tq, tr, ALU.add)
                            dve.drain()
                        dve.drain().then_inc(dve_rope, 1)

                    def maxima(h, q):
                        dve.wait_ge(pe_s, 4 * h + q + 1)
                        dve.tensor_reduce(mx[:, 0:2], PS[:, 3:5, :], AX.X, ALU.max)
                        dve.tensor_reduce(mx[:, 2:4], PS[:, 5, :].rearrange("p (a c) -> p a c", a=2), AX.X, ALU.max)
                        dve.drain()
                        dve.tensor_tensor(nm[:], mx[:, 0:2], mx[:, 2:4], ALU.max)
                        dve.drain()
                        dve.tensor_scalar(nm[:], nm[:], -HALF ** -0.5, None, ALU.mult).then_inc(dve_max, 1)

                    def weights(h, q):
                        dve.wait_ge(act_exp, 4 * h + q + 1)
                        dve.tensor_tensor(rz[:], Z[:, 0, :], Z[:, 1, :], ALU.add)
                        dve.drain()
                        dve.reciprocal(rz[:], rz[:])
                        dve.drain()
                        dve.tensor_tensor(rz[:, 1:2], rz[:, 1:2], neglam[:], ALU.mult)
                        if q:
                            dve.wait_ge(pe_t, 4 * h + q)
                        dve.tensor_scalar(Wt[:], E[:, 0, :], rz[:, 0:1], None, ALU.mult)
                        dve.drain()
                        dve.scalar_tensor_tensor(Wt[:], E[:, 1, :], rz[:, 1:2], Wt[:], ALU.mult, ALU.add).then_inc(dve_w, 1)

                    def keep_att(h, q):
                        dve.wait_ge(pe_p, 4 * h + q + 1)
                        dve.tensor_copy(on[:, q, :], PS[:, 7, 256:384]).then_inc(dve_pn, 1)
                        dve.drain()
                        squares(ss[:, 1, q:q + 1], on[:, q, :])

                    def att_norm(h):
                        mean_eps(1)
                        dve.drain().then_inc(dve_as, 1)
                        dve.wait_ge(act_as, h + 1)
                        dve.tensor_tensor(on[:], on[:], ss[:, 1, :].unsqueeze(2).to_broadcast([P, LT, HD]), ALU.mult).then_inc(dve_an, 1)
                        dve.wait_ge(pe_o, h + 1)
                        dve.tensor_scalar(mixT[:, bass.ds(h, 1), :].rearrange("p a t -> p (a t)"), PS[:, 6, :], gains[:, 0:1], None, ALU.mult).then_inc(dve_dout, 1)

                    def stage_a(h):
                        ctx_keys(h); decayed_queries(h)
                        for t in range(LT):
                            decayed_scores(h, t)
                        for t in range(LT):
                            divide(h, t)
                        ml_norm(h)

                    def stage_b(h, proj):
                        g = h + 1
                        rope_qk(h); maxima(h, 0)
                        if proj: conv_q(g)
                        weights(h, 0); maxima(h, 1); weights(h, 1); keep_att(h, 0)
                        if proj: conv_k(g)
                        maxima(h, 2); weights(h, 2); keep_att(h, 1)
                        maxima(h, 3); weights(h, 3); keep_att(h, 2); keep_att(h, 3)
                        att_norm(h)

                    for pad in (rawq[:, 0:PAD], rawq[:, PAD + SEQ:], rawk[:, 0:PAD], rawk[:, PAD + SEQ:], rawc[:, 0:PAD], rawc[:, PAD + CTX:]):
                        dve.memset(pad, 0.0)
                    dve.memset(vaug[:, :, HD:HD + 2], 1.0)
                    dve.memset(onesH[:], 1.0)
                    dve.memset(qz[HALF:P, 0, :], 0.0)
                    dve.memset(qz[0:HALF, 1, :], 0.0)
                    dve.drain().then_inc(s_tab, 1)
                    dve.drain().then_inc(dve_dout, 1)
                    dve.wait_ge(s_tab, 49)
                    conv_q(0); conv_k(0)
                    with dve.Fori(0, H - 1) as h:
                        stage_a(h)
                        stage_b(h, True)
                    stage_a(H - 1)
                    stage_b(H - 1, False)

        x1 = sb("x1", [P, LT, D])
        vecs = sb("vecs", [P, 4, D])
        lng = sb("lng", [P, 2, D])
        eidx = sb("eidx", [P, LT * NEXP // 8, 8], u32)
        gate = sb("gate", [P, LT * NEXP // 4, 4])
        st6 = sb("st6", [P, 4, 6])
        mv2 = sb("mv2", [P, 2])
        rsd = sb("rsd", [P, 1])
        h2 = mixT[:].rearrange("p k t -> p (k t)").rearrange("p (t d) -> p t d", t=LT)

        s_ld3 = sem("residual_and_vectors_loaded")
        s_rep = sem("silu_spread3")
        s_wb = [sem("chunk_loaded0"), sem("chunk_loaded1")]
        s_cpe, s_cev = sem("chunk_summed"), sem("chunk_kept")
        s_keys = sem("keys_loaded")
        s_wq = [sem("query_weights_loaded0"), sem("query_weights_loaded1")]
        s_stat, s_std = sem("ln_stats"), sem("ln_std")
        s_h2, s_hTpe, s_hTev = sem("peer_input"), sem("peer_input_turned"), sem("peer_input_turned_kept")
        s_qpe, s_qev = sem("queries_summed"), sem("queries_kept")
        s_spe, s_sev = sem("key_scores"), sem("key_scores_kept")
        s_top, s_gex = sem("chosen"), sem("chosen_exps")

        def layer_norm(dve, src, sem_stat, sem_std, n):
            for i in range(4):
                dve.bn_stats(st6[:, i, :], src[:, i * 512:(i + 1) * 512])
            dve.drain()
            dve.bn_aggr(mv2[:], st6[:].rearrange("p a b -> p (a b)"))
            dve.drain()
            dve.tensor_scalar(rsd[:], mv2[:, 1:2], LN_EPS, None, ALU.add).then_inc(sem_stat, 1)
            dve.wait_ge(sem_std, n)
            dve.reciprocal(rsd[:], rsd[:])
            dve.drain()
            dve.tensor_scalar(src, src, mv2[:, 0:1], rsd[:, 0:1], ALU.subtract, ALU.mult)
            dve.drain()
            dve.tensor_tensor(src, src, lng[:, 0, :], ALU.mult)
            dve.drain()
            return dve.tensor_tensor(src, src, lng[:, 1, :], ALU.add)

        b3 = ExitStack()
        with b3:
            ring = sb("ring", [P, 2, KT, CHUNK], ctx=b3)
            wqb = sb("wqb", [P, 2, KT, P], ctx=b3)
            kys = sb("kys", [P, 2 * PH, NKEYS], ctx=b3)
            silB = wqb[:, 0, :, :]
            h2T = ring[:, 0, :, :]
            rest = ring[:, 1, :, :].rearrange("p k c -> p (k c)")
            def carve(at, shape, dt=f32):
                n = int(np.prod(shape[1:]))
                v = rest[:, at:at + n]
                if dt is not f32:
                    v = v.bitcast(dt)
                if len(shape) == 2:
                    return v
                names = "abcd"[:len(shape) - 1]
                return v.rearrange(f"p ({' '.join(names)}) -> p {' '.join(names)}", **dict(zip(names, shape[1:])))
            qT = carve(0, [P, 2, SEQ])
            sc = carve(1024, [P, LT, 2, NKEYS])
            s2 = carve(2048, [P, LT, 2, NKEYS])
            cand = carve(3072, [P, LT, TOPK * TOPK])
            cand2 = carve(4096, [P, LT, TOPK * TOPK])
            oh = carve(5120, [P, LT, TOPK, TOPK])
            vv = carve(6144, [P, LT, 2, TOPK])
            ii = carve(6272, [P, LT, 2, TOPK], u32)
            iif = carve(6400, [P, LT, 2, TOPK])
            tv = carve(6528, [P, LT, TOPK])
            tp = carve(6592, [P, LT, TOPK], u32)
            ab = carve(6656, [P, 2, LT, TOPK], u32)
            abf = carve(6784, [P, 2, LT, TOPK])
            sel = carve(6912, [P, 2, LT, TOPK])
            ef = carve(7040, [P, LT, TOPK])
            gx = carve(7104, [P, LT, TOPK])
            gs = carve(7168, [P, LT])
            yg = gate[:].rearrange("p a b -> p (a b)")

            with nc.Block() as block:
                @block.sync
                def _(sp):
                    wv = wada.rearrange("(k p) (n c) -> p k n c", p=P, c=CHUNK)
                    ov = wout.rearrange("(k p) (n c) -> p k n c", p=P, c=CHUNK)
                    for j in range(2):
                        sp.dma_start(ring[:, j, :, :], wv[:, :, SH_CHUNKS + j, :]).then_inc(s_wb[j], 16)
                    for i in range(4):
                        sp.dma_start(vecs[:, i, :], brow[i:i + 1, :].partition_broadcast(P)).then_inc(s_ld3, 16)
                    sp.dma_start(x1[:], x.rearrange("(t p) d -> p t d", p=P)).then_inc(s_ld3, 16)
                    for i in range(2):
                        sp.dma_start(lng[:, i, :], lnv[i:i + 1, :].partition_broadcast(P)).then_inc(s_ld3, 16)
                    sp.dma_start(kys[:].rearrange("p a k -> p (a k)"), keysT).then_inc(s_keys, 16)
                    with sp.Fori(1, REST_CHUNKS // 2) as n:
                        for j in range(2):
                            sp.wait_ge(s_cpe, 2 * n + j - 1)
                            sp.dma_start(ring[:, j, :, :], wv[:, :, SH_CHUNKS + 2 * n + j, :]).then_inc(s_wb[j], 16)
                    with sp.Fori(0, OUT_CHUNKS // 2) as n:
                        for j in range(2):
                            sp.wait_ge(s_cpe, 2 * n + j + REST_CHUNKS - 1)
                            sp.dma_start(ring[:, j, :, :], ov[:, :, 2 * n + j, :]).then_inc(s_wb[j], 16)
                    sp.wait_ge(s_cpe, REST_CHUNKS)
                    for j in range(2):
                        sp.dma_start(wqb[:, j, :, :], wq[j]).then_inc(s_wq[j], 16)
                    with sp.Fori(1, PH) as n:
                        for j in range(2):
                            sp.wait_ge(s_qpe, 2 * n + j - 1)
                            sp.dma_start(wqb[:, j, :, :], wq[2 * n + j]).then_inc(s_wq[j], 16)

                @block.tensor
                def _(pe):
                    pe.wait_ge(s_rep, 1)
                    with pe.Fori(0, REST_CHUNKS // 2) as n:
                        for j in range(2):
                            pe.wait_ge(s_wb[j], 16 * n + 16)
                            pe.wait_ge(s_cev, 2 * n + j + 1)
                            for k in range(KT):
                                last = pe.matmul(PS[:, j, :], silB[:, k, :], ring[:, j, k, :], start=(k == 0), stop=(k == KT - 1))
                            last.then_inc(s_cpe, 1)
                    pe.wait_ge(s_cev, REST_CHUNKS + 2)
                    with pe.Fori(0, OUT_CHUNKS // 2) as n:
                        for j in range(2):
                            pe.wait_ge(s_wb[j], 16 * n + 16 * (REST_CHUNKS // 2) + 16)
                            pe.wait_ge(s_cev, 2 * n + j + REST_CHUNKS + 1)
                            for t in range(LT):
                                for k in range(KT):
                                    last = pe.matmul(PS[:, 4 * j + t, :], mixT[:, k, t * P:(t + 1) * P], ring[:, j, k, :],
                                                     start=(k == 0), stop=(k == KT - 1))
                            last.then_inc(s_cpe, 1)
                    for t in range(LT):
                        pe.wait_ge(s_h2, t + 1)
                        for q in range(4):
                            n = 4 * t + q
                            if n >= 4:
                                pe.wait_ge(s_hTev, n - 3)
                            for i in range(4):
                                k = 4 * q + i
                                last = pe.transpose(PS[:, n % 4, i * P:(i + 1) * P], h2[:, t, k * P:(k + 1) * P], ident)
                            last.then_inc(s_hTpe, 1)
                    pe.wait_ge(s_hTev, 16)
                    pe.wait_ge(s_keys, 16)

                    def queries(m, j):
                        pe.wait_ge(s_wq[j], 16 * m + 16)
                        pe.wait_ge(s_qev, 2 * m + j + 1)
                        for k in range(KT):
                            last = pe.matmul(PS[:, j, :], wqb[:, j, k, :], h2T[:, k, :], start=(k == 0), stop=(k == KT - 1))
                        last.then_inc(s_qpe, 1)

                    def key_scores(m, j):
                        pe.wait_ge(s_qev, 2 * m + j + 3)
                        pe.wait_ge(s_sev, 2 * m + j + 1)
                        for t in range(LT):
                            last = pe.matmul(PS[:, 2 + j, t * NKEYS:(t + 1) * NKEYS], qT[:, j, t * P:(t + 1) * P],
                                             kys[:, bass.ds(2 * m + j, 1), :].rearrange("p a k -> p (a k)"), start=True, stop=True)
                        last.then_inc(s_spe, 1)

                    queries(0, 0)
                    with pe.Fori(0, PH - 1) as m:
                        queries(m, 1); key_scores(m, 0); queries(m + 1, 0); key_scores(m, 1)
                    queries(PH - 1, 1); key_scores(PH - 1, 0); key_scores(PH - 1, 1)

                @block.scalar
                def _(act):
                    for t in range(LT):
                        act.wait_ge(s_stat, t + 1)
                        act.activation(rsd[:], rsd[:], ACT.Sqrt).then_inc(s_std, 1)
                        for q in range(4):
                            n = 4 * t + q
                            act.wait_ge(s_hTpe, n + 1)
                            act.activation(h2T[:, 4 * q:4 * q + 4, t * P:(t + 1) * P],
                                           PS[:, n % 4, :].rearrange("p (i c) -> p i c", i=4), ACT.Copy).then_inc(s_hTev, 1)

                    def keep_queries(m):
                        for j in range(2):
                            act.wait_ge(s_qpe, 2 * m + j + 1)
                            act.wait_ge(s_spe, 2 * m + j + 1)
                            act.activation(qT[:, j, :], PS[:, j, :], ACT.Copy).then_inc(s_qev, 1)

                    def keep_scores(m):
                        act.wait_ge(s_top, m + 1)
                        for j in range(2):
                            act.wait_ge(s_spe, 2 * m + j + 3)
                            act.activation(sc[:, :, j, :], PS[:, 2 + j, :].rearrange("p (t k) -> p t k", k=NKEYS), ACT.Copy).then_inc(s_sev, 1)

                    def gate_exps(m):
                        act.wait_ge(s_top, m + 2)
                        act.activation(gx, gx, ACT.Exp).then_inc(s_gex, 1)

                    keep_queries(0); keep_scores(0)
                    with act.Fori(1, PH) as m:
                        keep_queries(m); gate_exps(m - 1); keep_scores(m)
                    gate_exps(PH - 1)

                @block.vector
                def _(dve):
                    for i in range(2):
                        for s in (s_cev, s_qev, s_sev, s_spe):
                            dve.drain().then_inc(s, 1)
                    dve.drain().then_inc(s_top, 1)
                    dve.tensor_copy(silB, silc[:, 0, :].unsqueeze(2).to_broadcast([P, KT, P])).then_inc(s_rep, 1)
                    dve.wait_ge(s_ld3, 7 * 16)
                    vflat = vecs[:].rearrange("p a d -> p (a d)")
                    with dve.Fori(0, REST_CHUNKS // 2) as n:
                        for j in range(2):
                            dve.wait_ge(s_cpe, 2 * n + j + 1)
                            part = vflat[:, bass.ds((2 * n + j) * CHUNK, CHUNK)]
                            dve.tensor_tensor(part, PS[:, j, :], part, ALU.add).then_inc(s_cev, 1)
                    dve.drain()
                    dve.tensor_scalar(vecs[:, 2, :], vecs[:, 2, :], 1.0, None, ALU.add)
                    with dve.Fori(0, OUT_CHUNKS // 2) as n:
                        for j in range(2):
                            dve.wait_ge(s_cpe, 2 * n + j + REST_CHUNKS + 1)
                            cols = bass.ds((2 * n + j) * CHUNK, CHUNK)
                            for t in range(LT):
                                last = dve.tensor_tensor(yg, PS[:, 4 * j + t, :], vecs[:, 0, cols], ALU.mult)
                                if t == LT - 1:
                                    last.then_inc(s_cev, 1)
                                dve.drain()
                                dve.scalar_tensor_tensor(x1[:, t, cols], x1[:, t, cols], ALPHA, yg, ALU.mult, ALU.add)
                                dve.drain()
                    for t in range(LT):
                        layer_norm(dve, x1[:, t, :], s_stat, s_std, t + 1)
                        dve.drain()
                        dve.tensor_tensor(h2[:, t, :], x1[:, t, :], vecs[:, 2, :], ALU.mult)
                        dve.drain()
                        dve.tensor_tensor(h2[:, t, :], h2[:, t, :], vecs[:, 1, :], ALU.add).then_inc(s_h2, 1)

                    def top16(groups):
                        for src, tmp, v, i in groups:
                            dve.max(v[:, 0:8], src)
                        dve.drain()
                        for src, tmp, v, i in groups:
                            dve.max_index(i[:, 0:8], v[:, 0:8], src)
                            dve.match_replace(out=tmp, in_to_replace=v[:, 0:8], in_values=src, imm_value=NEG)
                        dve.drain()
                        for src, tmp, v, i in groups:
                            dve.max(v[:, 8:16], tmp)
                        dve.drain()
                        for src, tmp, v, i in groups:
                            dve.max_index(i[:, 8:16], v[:, 8:16], tmp)
                        dve.drain()

                    eview = eidx[:].rearrange("p (t m a) b -> p t m (a b)", t=LT, m=PH)
                    gview = gate[:].rearrange("p (t m a) b -> p t m (a b)", t=LT, m=PH)
                    flat = lambda v: v.rearrange("p a b -> p (a b)")
                    with dve.Fori(0, PH) as m:
                        dve.wait_ge(s_sev, 2 * m + 4)
                        dve.memset(gs, 0.0)
                        top16([(sc[:, t, j, :], s2[:, t, j, :], vv[:, t, j, :], ii[:, t, j, :]) for t in range(LT) for j in range(2)])
                        for t in range(LT):
                            dve.tensor_tensor(cand[:, t, :].rearrange("p (a b) -> p a b", a=TOPK),
                                              vv[:, t, 0, :].unsqueeze(2).to_broadcast([P, TOPK, TOPK]),
                                              vv[:, t, 1, :].unsqueeze(1).to_broadcast([P, TOPK, TOPK]), ALU.add)
                        dve.tensor_copy(iif, ii)
                        dve.drain()
                        top16([(cand[:, t, :], cand2[:, t, :], tv[:, t, :], tp[:, t, :]) for t in range(LT)])
                        dve.tensor_tensor(gx, tv, tv[:, :, 0:1].to_broadcast([P, LT, TOPK]), ALU.subtract).then_inc(s_top, 1)
                        dve.tensor_scalar(flat(ab[:, 0, :, :]), flat(tp), 4, None, ALU.logical_shift_right)
                        dve.tensor_scalar(flat(ab[:, 1, :, :]), flat(tp), TOPK - 1, None, ALU.bitwise_and)
                        dve.drain()
                        dve.tensor_copy(abf, ab)
                        dve.drain()
                        for j in range(2):
                            dve.tensor_tensor(oh.rearrange("p t k i -> p (t k) i"), flat(abf[:, j, :, :]).unsqueeze(2).to_broadcast([P, LT * TOPK, TOPK]),
                                              iota16.unsqueeze(1).to_broadcast([P, LT * TOPK, TOPK]), ALU.is_equal)
                            dve.drain()
                            dve.tensor_tensor(oh, oh, iif[:, :, j, :].unsqueeze(2).to_broadcast([P, LT, TOPK, TOPK]), ALU.mult)
                            dve.drain()
                            dve.tensor_reduce(sel[:, j, :, :], oh, AX.X, ALU.add)
                            dve.drain()
                        dve.scalar_tensor_tensor(eview[:, :, bass.ds(m, 1), :].rearrange("p t m k -> p t (m k)"),
                                                 sel[:, 0, :, :], float(NKEYS), sel[:, 1, :, :], ALU.mult, ALU.add)
                        dve.wait_ge(s_gex, m + 1)
                        dve.tensor_reduce(gs, gx, AX.X, ALU.add)
                        dve.drain()
                        dve.reciprocal(gs, gs)
                        dve.drain()
                        dve.tensor_tensor(gview[:, :, bass.ds(m, 1), :].rearrange("p t m k -> p t (m k)"), gx,
                                          gs.unsqueeze(2).to_broadcast([P, LT, TOPK]), ALU.mult)
                        dve.drain()

        GROUP = 4
        NGROUP = NEXP // GROUP
        b4 = ExitStack()
        s_u = [sem(f"u_rows{i}") for i in range(GROUP)]
        s_v = [sem(f"v_rows{i}") for i in range(GROUP)]
        s_idx = sem("indices_staged")
        s_udone, s_vdone = sem("u_rows_used"), sem("v_rows_used")
        s_act, s_gelu = sem("dots_done"), sem("gelu_done")
        s_ln4 = sem("ln2_loaded")
        s_stat4, s_std4 = sem("ln2_stats"), sem("ln2_std")
        s_y, s_out = sem("rows_finished"), sem("rows_stored")
        with b4:
            Ub = sb("Ub", [P, GROUP, D], ctx=b4)
            Vb = sb("Vb", [P, GROUP, D], ctx=b4)
            stage = sb("stage", [P, 2, 8], u32, ctx=b4)
            dots = sb("dots", [P, GROUP], ctx=b4)
            coef = sb("coef", [P, GROUP], ctx=b4)
            acc, cur = vecs[:, 0, :], vecs[:, 1, :]
            with nc.Block() as block:
                @block.sync
                def _(sp):
                    for i in range(2):
                        sp.dma_start(lng[:, i, :], lnv[2 + i:3 + i, :].partition_broadcast(P)).then_inc(s_ln4, 16)
                    with sp.Fori(0, LT) as t:
                        sp.wait_ge(s_y, t + 1)
                        sp.dma_start(out.rearrange("(t p) d -> p t d", p=P)[:, bass.ds(t, 1), :], x1[:, bass.ds(t, 1), :]).then_inc(s_out, 16)
                    sp.wait_ge(s_out, 16 * LT)

                @block.gpsimd
                def _(pool):
                    with pool.Fori(0, LT * NGROUP // 4) as r:
                        for i in range(4):
                            n = 4 * r + i
                            if i % 2 == 0:
                                pool.wait_ge(s_vdone, 4 * n + 1)
                                pool.tensor_copy(stage[:, i // 2, :], eidx[:, bass.ds(2 * r + i // 2, 1), :].rearrange("p a b -> p (a b)")).then_inc(s_idx, 1)
                                pool.wait_ge(s_idx, 2 * r + i // 2 + 1)
                            for table, buf, ready, used in ((peer_u, Ub, s_u, s_udone), (peer_v, Vb, s_v, s_vdone)):
                                for e in range(GROUP):
                                    pool.wait_ge(used, 4 * n + e + 1)
                                    pool.sem_inc(s_passed)
                                    col = (i % 2) * GROUP + e
                                    pool.indirect_dma_start(out=buf[:, e, :], out_offset=None, in_=table,
                                                            in_offset=bass.IndirectOffsetOnAxis(ap=stage[:, i // 2, col:col + 1], axis=0)).then_inc(ready[e], 16)

                @block.scalar
                def _(act):
                    with act.Fori(0, LT) as t:
                        with act.Fori(0, NGROUP) as g:
                            act.wait_ge(s_act, t * NGROUP + g + 1)
                            act.activation(dots[:], dots[:], ACT.Gelu).then_inc(s_gelu, 1)
                        act.wait_ge(s_stat4, t + 1)
                        act.activation(rsd[:], rsd[:], ACT.Sqrt).then_inc(s_std4, 1)

                @block.vector
                def _(dve):
                    for i in range(GROUP):
                        dve.drain().then_inc(s_udone, 1)
                        dve.drain().then_inc(s_vdone, 1)
                    dve.wait_ge(s_ln4, 32)
                    with dve.Fori(0, LT) as t:
                        dve.tensor_copy(cur, h2[:, bass.ds(t, 1), :].rearrange("p a d -> p (a d)"))
                        dve.memset(acc, 0.0)
                        dve.drain()
                        with dve.Fori(0, NGROUP) as g:
                            n = t * NGROUP + g
                            for e in range(GROUP):
                                dve.wait_ge(s_u[e], 16 * n + 16)
                                dve.scalar_tensor_tensor(Ub[:, e, :], Ub[:, e, :], 1.0, cur, ALU.mult, ALU.mult,
                                                         accum_out=dots[:, e:e + 1]).then_inc(s_udone, 1)
                            dve.drain().then_inc(s_act, 1)
                            dve.wait_ge(s_gelu, n + 1)
                            dve.tensor_tensor(coef[:], dots[:], gate[:, bass.ds(n, 1), :].rearrange("p a b -> p (a b)"), ALU.mult)
                            for e in range(GROUP):
                                dve.drain()
                                dve.wait_ge(s_v[e], 16 * n + 16)
                                dve.scalar_tensor_tensor(acc, Vb[:, e, :], coef[:, e:e + 1], acc, ALU.mult, ALU.add).then_inc(s_vdone, 1)
                        dve.drain()
                        xt = x1[:, bass.ds(t, 1), :].rearrange("p a d -> p (a d)")
                        dve.tensor_tensor(acc, acc, vecs[:, 3, :], ALU.mult)
                        dve.drain()
                        dve.scalar_tensor_tensor(xt, xt, ALPHA, acc, ALU.mult, ALU.add)
                        dve.drain()
                        layer_norm(dve, xt, s_stat4, s_std4, t + 1).then_inc(s_y, 1)


def constants():
    turn = np.zeros((P, P), np.float32)
    nf = HALF // 4
    for m in range(P):
        if m % (2 * nf) < nf:
            turn[m + nf, m] = -1.0
        else:
            turn[m - nf, m] = 1.0
    iota = np.tile(np.arange(TOPK, dtype=np.float32), (P, 1))
    inv = (np.float32(10000.0) ** (-np.arange(nf, dtype=np.float32) / np.float32(nf))).astype(np.float32)
    tok = np.arange(SEQ)
    pos = np.stack([tok // GRID_W, tok % GRID_W]).astype(np.float32)
    f = np.arange(P)
    ang = pos[(f % HALF) // (HALF // 2)] * inv[f % nf][:, None]
    rope = np.concatenate([np.cos(ang), np.sin(ang)], 1).astype(np.float32)
    return np.concatenate([np.eye(P, dtype=np.float32), turn, iota], 1), rope


def kernel(x, c, ctx, c_ctx, w_ada, b_ada, w_in, conv_w, conv_b, gate_b, diff_lambda, diff_norm_g,
           mlstm_norm_g, w_out, ln1_g, ln1_b, ln2_g, ln2_b, peer_wq, peer_keys, peer_u, peer_v):
    import concourse.bacc as bacc
    from concourse.bass_utils import run_bass_kernel_spmd

    con = np.ascontiguousarray
    w_in = np.asarray(w_in)[0]
    b_ada = np.asarray(b_ada)[0]
    w = w_in[:, :7 * H * HD].reshape(2, 8, P, 7, H, HD)[:, :, :, [3, 4, 5, 6, 0, 1, 2]]
    consts, rope = constants()
    arrays = {
        "xT": con(np.asarray(x)[0].T), "x": con(np.asarray(x)[0]), "cxT": con(np.asarray(ctx)[0].T),
        "ccol": con(np.concatenate([np.asarray(c)[0].reshape(KT, P).T, np.asarray(c_ctx).reshape(KT, P).T], 1)),
        "wada": con(np.asarray(w_ada)[0]), "bcol": con(b_ada[:2 * D].reshape(2 * KT, P).T), "brow": con(b_ada[2 * D:].reshape(4, D)),
        "wseq": con(w.transpose(4, 3, 0, 2, 1, 5).reshape(HALVES, P, 8, P)),
        "wgate": con(w_in[:, 7 * H * HD:]), "gbias": con(np.asarray(gate_b)[0].reshape(NGATES * H, 1)),
        "convw": con(np.asarray(conv_w)[0].reshape(CONV, 2 * H, HD).transpose(2, 1, 0).reshape(P, 2 * H * CONV)),
        "convb": con(np.asarray(conv_b)[0].reshape(2 * H, HD).T),
        "lamv": con(np.asarray(diff_lambda)[0].reshape(1, 4 * HALF)),
        "gcol": con(np.stack([np.asarray(diff_norm_g)[0], np.asarray(mlstm_norm_g)[0]], 1)),
        "wout": con(np.asarray(w_out)[0]),
        "lnv": con(np.stack([np.asarray(a)[0] for a in (ln1_g, ln1_b, ln2_g, ln2_b)])),
        "wq": con(np.asarray(peer_wq)[0].reshape(KT, P, 2 * PH, P).transpose(2, 1, 0, 3)),
        "keysT": con(np.asarray(peer_keys)[0].transpose(3, 1, 0, 2).reshape(P, 2 * PH * NKEYS)),
        "peer_u": con(np.asarray(peer_u)[0]), "peer_v": con(np.asarray(peer_v)[0]),
        "consts": consts, "rope": rope,
    }
    nc = bacc.Bacc("TRN2", target_bir_lowering=False, num_devices=1)
    aps = {n: nc.dram_tensor(n, a.shape, mybir.dt.from_np(a.dtype), kind="ExternalInput").ap() for n, a in arrays.items()}
    aps["out"] = nc.dram_tensor("out", (SEQ, D), mybir.dt.float32, kind="ExternalOutput").ap()
    program(nc, **aps)
    r = run_bass_kernel_spmd(nc, [arrays], core_ids=[0])
    return r.results[0]["out"].reshape(1, SEQ, D)
```

```python
import numpy as np
from contextlib import ExitStack

import concourse.bass as bass
from concourse import mybir

P = 128
D = 2048
KT = D // P
SEQ, CTX = 512, 256
T = SEQ + CTX
LT, CT = SEQ // P, CTX // P
H = 8
HD = 128
HALF = 64
NGATES = 4
CONV = 5
PAD = CONV // 2
GRID_W = 64
TOPK = 16
NKEYS = 128
PH = 8
NEXP = PH * TOPK
ALPHA = 2.0 ** 0.25
LAM_INIT = 0.2
LN_EPS, RMS_EPS = 1e-5, 1e-6
CHUNK = 512
SH_CHUNKS = 2 * D // CHUNK
REST_CHUNKS = 4 * D // CHUNK
OUT_CHUNKS = D // CHUNK
WBUF = 7
HALVES = H * 7 * 2
NEG = -3.0e38
DT = 2
DTOK = DT * P
NEB = NKEYS * NKEYS // P
GROUP = 4
NG = (LT - DT) * NEXP // GROUP
assert 2 * NG == NEB


def program(nc, xT, x, cxT, ccol, wada, bcol, brow, wseq, wgate, gbias, convw, convb, lamv, gcol,
            wout, lnv, wq, keysT, peer_u, peer_v, peer_ut, consts, rope, out):
    f32, u32 = mybir.dt.float32, mybir.dt.uint32
    ALU, ACT, AX = mybir.AluOpType, mybir.ActivationFunctionType, mybir.AxisListType
    with ExitStack() as top:
        def sb(name, shape, dt=f32, ctx=top):
            return ctx.enter_context(nc.sbuf_tensor(name, shape, dt))

        def sem(name):
            return top.enter_context(nc.semaphore(name))

        PS = top.enter_context(nc.psum_tensor("PS", [P, 8, 512], f32))
        cst = sb("cst", [P, 272 + DT])
        ident, rotm, iota16 = cst[:, 0:128], cst[:, 128:256], cst[:, 256:272]
        tokid = cst[:, 272:272 + DT]
        gates_dram = nc.dram_tensor("gates_dram", (NKEYS * NKEYS, DTOK), f32, kind="Internal").ap()
        s_passed = sem("gpsimd_waits_passed")
        silc = sb("silc", [P, 2, KT])
        neglam = sb("neglam", [P, 1])
        gains = sb("gains", [P, 2])
        mixT = sb("mixT", [P, KT, SEQ])

        phase_a = ExitStack()
        hT = sb("hT", [P, KT, T], ctx=phase_a)
        colv = sb("colv", [P, 20, H], ctx=phase_a)
        m0b = sb("m0b", [P, 2, H], ctx=phase_a)
        Mrow = sb("Mrow", [H, 2, SEQ], ctx=phase_a)

        s_small = sem("small_loaded")
        s_x = sem("inputs_loaded")
        s_wa = [sem("ada_loaded0"), sem("ada_loaded1")]
        s_sil = sem("silu_done")
        s_silrep = sem("silu_spread")
        s_ada_pe = sem("ada_summed")
        s_ada_ev = sem("ada_row_kept")
        s_modT = sem("mod_turned")
        s_mod = sem("inputs_modulated")
        s_gate_pe = sem("gates_summed")
        s_gate_ev = sem("gates_kept")
        s_gate_mv = sem("gates_moved")
        s_abs = sem("gate_abs")
        s_lf1 = sem("log1p_done")
        s_scan = sem("scans_done")
        s_ex = sem("gate_exps")
        s_dm = sem("state_max_spread_ready")
        s_col = sem("columns_turned")
        s_lamd = sem("lambda_dots")
        s_lame = sem("lambda_exps")

        b1 = ExitStack()
        wr = sb("wr", [P, 2, KT, CHUNK], ctx=b1)
        adar = wr[:, 0, 0:8, :].rearrange("p k c -> p (k c)")
        with b1:
            silA = mixT[:, 0:4, :].rearrange("p k t -> p (k t)").rearrange("p (k m) -> p k m", k=KT)
            R = mixT[:, 4:12, :].rearrange("p k t -> p (k t)")
            cc = sb("cc", [P, 2, KT], ctx=b1)
            bc = sb("bc", [P, 2 * KT], ctx=b1)
            mods = sb("mods", [P, 2 * KT, 2], ctx=b1)
            wg = mixT[:, 12:13, :].rearrange("p k t -> p (k t)").rearrange("p (k m) -> p k m", k=KT)
            gb = sb("gb", [NGATES * H, 1], ctx=b1)
            gts = sb("gts", [NGATES * H, T], ctx=b1)
            lam4 = sb("lam4", [P, 4, HALF], ctx=b1)
            lamp = sb("lamp", [P, 2, HALF], ctx=b1)
            lamd = sb("lamd", [P, 2], ctx=b1)
            lame = sb("lame", [P, 2], ctx=b1)
            gI = sb("gI", [H, 2, T], ctx=b1)
            gF = sb("gF", [H, 2, T], ctx=b1)
            gA = mixT[0:H, 13:16, :].rearrange("p k t -> p (k t)").rearrange("p (d t) -> p d t", d=2)
            gE = sb("gE", [H, 2, T], ctx=b1)
            ones8 = sb("ones8", [H, T], ctx=b1)
            m0 = sb("m0", [H, 2], ctx=b1)
            mc = sb("mc", [H, 2], ctx=b1)
            dm0 = sb("dm0", [H, 2, H], ctx=b1)

            with nc.Block() as block:
                @block.sync
                def _(sp):
                    sp.dma_start(cc[:].rearrange("p a k -> p (a k)"), ccol).then_inc(s_small, 16)
                    sp.dma_start(cst[:], consts).then_inc(s_small, 16)
                    wv = wada.rearrange("(k p) n -> p k n", p=P)
                    sp.dma_start(wr[:, 0, :, :], wv[:, :, 0:CHUNK]).then_inc(s_wa[0], 16)
                    sp.dma_start(wr[:, 1, :, :], wv[:, :, CHUNK:2 * CHUNK]).then_inc(s_wa[1], 16)
                    sp.dma_start(bc[:], bcol).then_inc(s_small, 16)
                    sp.dma_start(gb[:], gbias).then_inc(s_small, 16)
                    sp.dma_start(gains[:], gcol).then_inc(s_small, 16)
                    sp.dma_start(lam4[:].rearrange("p a d -> p (a d)"), lamv.partition_broadcast(P)).then_inc(s_small, 16)
                    sp.dma_start(wg, wgate.rearrange("(k p) g -> p k g", p=P)).then_inc(s_small, 16)
                    sp.dma_start(hT[:, :, 0:SEQ], xT.rearrange("(k p) t -> p k t", p=P)).then_inc(s_x, 16)
                    sp.dma_start(hT[:, :, SEQ:T], cxT.rearrange("(k p) t -> p k t", p=P)).then_inc(s_x, 16)
                    wv4 = wada.rearrange("(k p) (n c) -> p k n c", p=P, c=CHUNK)
                    with sp.Fori(1, SH_CHUNKS // 2) as n:
                        for j in range(2):
                            sp.wait_ge(s_ada_pe, 2 * n + j - 1)
                            sp.dma_start(wr[:, j, :, :], wv4[:, :, 2 * n + j, :]).then_inc(s_wa[j], 16)
                    sp.wait_ge(s_gate_ev, 1)
                    for g, dst in enumerate((gI[:, 0, :], gF[:, 0, :], gI[:, 1, :], gF[:, 1, :])):
                        sp.dma_start(dst, gts[g * H:(g + 1) * H, :]).then_inc(s_gate_mv, 16)

                @block.scalar
                def _(act):
                    act.wait_ge(s_small, 16 * 7)
                    act.activation(silc[:], cc[:], ACT.Silu).then_inc(s_sil, 1)
                    with act.Fori(0, SH_CHUNKS // 2) as n:
                        for j in range(2):
                            act.wait_ge(s_ada_pe, 2 * n + j + 1)
                            act.activation(R[:, bass.ds((2 * n + j) * CHUNK, CHUNK)], PS[:, j, :], ACT.Copy).then_inc(s_ada_ev, 1)
                    act.wait_ge(s_lamd, 1)
                    act.activation(lame[:], lamd[:], ACT.Exp).then_inc(s_lame, 1)
                    act.wait_ge(s_abs, 1)
                    act.activation(gE[:], gE[:], ACT.Exp, scale=-1.0)
                    act.drain()
                    act.activation(gE[:], gE[:], ACT.Ln, bias=1.0).then_inc(s_lf1, 1)
                    act.wait_ge(s_scan, 1)
                    act.activation(gE[:], gA, ACT.Exp).then_inc(s_ex, 1)

                @block.tensor
                def _(pe):
                    pe.wait_ge(s_silrep, 1)
                    with pe.Fori(0, SH_CHUNKS // 2) as n:
                        for j in range(2):
                            pe.wait_ge(s_wa[j], 16 * n + 16)
                            pe.wait_ge(s_ada_ev, 2 * n + j + 1)
                            for k in range(KT):
                                last = pe.matmul(PS[:, j, :], silA[:, k, :], wr[:, j, k, :], start=(k == 0), stop=(k == KT - 1))
                            last.then_inc(s_ada_pe, 1)
                    pe.wait_ge(s_ada_ev, SH_CHUNKS + 2)
                    for j in range(2 * KT):
                        last = pe.matmul(PS[:, 2, 2 * j:2 * j + 2], R[:, j * P:(j + 1) * P], ident[:, 0:65:64], start=True, stop=True)
                    last.then_inc(s_modT, 1)
                    for k in range(KT):
                        if k % 4 == 0:
                            pe.wait_ge(s_mod, k // 4 + 1)
                        pe.matmul(PS[0:32, 3, :], wg[:, k, :], hT[:, k, 0:SEQ], start=(k == 0), stop=(k == KT - 1))
                        last = pe.matmul(PS[0:32, 4, 0:CTX], wg[:, k, :], hT[:, k, SEQ:T], start=(k == 0), stop=(k == KT - 1))
                    last.then_inc(s_gate_pe, 1)
                    pe.wait_ge(s_ex, 1)
                    for d in range(2):
                        for t in range(LT):
                            pe.transpose(PS[:, 5, (d * LT + t) * H:(d * LT + t + 1) * H], gI[:, d, t * P:(t + 1) * P], ident[0:H, 0:H])
                            pe.transpose(PS[:, 5, (8 + d * LT + t) * H:(9 + d * LT + t) * H], gE[:, d, t * P:(t + 1) * P], ident[0:H, 0:H])
                        for t in range(CT):
                            pe.transpose(PS[:, 5, (16 + d * CT + t) * H:(17 + d * CT + t) * H],
                                         gE[:, d, SEQ + t * P:SEQ + (t + 1) * P], ident[0:H, 0:H])
                    pe.wait_ge(s_dm, 1)
                    pe.matmul(PS[:, 6, 0:2 * H], ones8[:, 0:P], dm0[:].rearrange("p a b -> p (a b)"), start=True, stop=True).then_inc(s_col, 1)

                @block.vector
                def _(dve):
                    dve.memset(ones8[:], 1.0)
                    for _ in range(2):
                        dve.drain().then_inc(s_ada_ev, 1)
                    dve.wait_ge(s_sil, 1)
                    for a in range(2):
                        last = dve.tensor_copy(silA[:, :, 64 * a:64 * a + 64], silc[:, a, :].unsqueeze(2).to_broadcast([P, KT, 64]))
                    last.then_inc(s_silrep, 1)
                    dve.tensor_tensor(lamp[:], lam4[:, 0:4:2, :], lam4[:, 1:4:2, :], ALU.mult)
                    dve.drain()
                    dve.tensor_reduce(lamd[:], lamp[:], AX.X, ALU.add).then_inc(s_lamd, 1)
                    dve.wait_ge(s_lame, 1)
                    dve.tensor_tensor(neglam[:], lame[:, 1:2], lame[:, 0:1], ALU.subtract)
                    dve.tensor_scalar(gains[:, 0:1], gains[:, 0:1], 1.0 - LAM_INIT, None, ALU.mult)
                    dve.drain()
                    dve.tensor_scalar(neglam[:], neglam[:], -LAM_INIT, None, ALU.add)
                    dve.wait_ge(s_modT, 1)
                    dve.tensor_tensor(mods[:], PS[:, 2, 0:4 * KT].rearrange("p (k a) -> p k a", a=2),
                                      bc[:].unsqueeze(2).to_broadcast([P, 2 * KT, 2]), ALU.add)
                    dve.drain()
                    dve.tensor_scalar(mods[:, KT:2 * KT, :], mods[:, KT:2 * KT, :], 1.0, None, ALU.add)
                    dve.drain()
                    dve.wait_ge(s_x, 32)
                    for k in range(KT):
                        for a, (t0, t1) in enumerate(((0, SEQ), (SEQ, T))):
                            last = dve.tensor_scalar(hT[:, k, t0:t1], hT[:, k, t0:t1], mods[:, KT + k, a:a + 1],
                                                     mods[:, k, a:a + 1], ALU.mult, ALU.add)
                        if k % 4 == 3:
                            last.then_inc(s_mod, 1)
                    dve.wait_ge(s_gate_pe, 1)
                    dve.tensor_scalar(gts[:, 0:SEQ], PS[0:32, 3, :], gb[:, 0:1], None, ALU.add)
                    dve.tensor_scalar(gts[:, SEQ:T], PS[0:32, 4, 0:CTX], gb[:, 0:1], None, ALU.add).then_inc(s_gate_ev, 1)
                    dve.wait_ge(s_gate_mv, 64)
                    dve.scalar_tensor_tensor(gE[:], gF[:], -1.0, gF[:], ALU.mult, ALU.max).then_inc(s_abs, 1)
                    dve.tensor_scalar(gF[:], gF[:], 0.0, None, ALU.min)
                    dve.drain()
                    dve.wait_ge(s_lf1, 1)
                    dve.tensor_tensor(gF[:], gF[:], gE[:], ALU.subtract)
                    dve.drain()
                    for d in range(2):
                        for t0, t1 in ((0, SEQ), (SEQ, T)):
                            o, i = gA[:, d, t0:t1], gF[:, d, t0:t1]
                            if d:
                                o, i = o[:, ::-1], i[:, ::-1]
                            dve.tensor_tensor_scan(out=o, data0=ones8[:, 0:t1 - t0], data1=i, initial=0.0, op0=ALU.mult, op1=ALU.add)
                    dve.drain()
                    dve.tensor_tensor(gI[:], gI[:], gA, ALU.subtract)
                    dve.drain()
                    dve.tensor_reduce(mc[:], gI[:, :, SEQ:T], AX.X, ALU.max)
                    dve.drain()
                    dve.tensor_scalar(mc[:], mc[:], 0.0, None, ALU.max)
                    dve.drain()
                    dve.tensor_tensor(m0[:, 0:1], mc[:, 0:1], gA[:, 0, T - 1:T], ALU.add)
                    dve.tensor_tensor(m0[:, 1:2], mc[:, 1:2], gA[:, 1, SEQ:SEQ + 1], ALU.add)
                    dve.drain()
                    for d in range(2):
                        dve.tensor_scalar(dm0[:, d, :], ident[0:H, 0:H], m0[:, d:d + 1], None, ALU.mult)
                        o, i = Mrow[:, d, :], gI[:, d, 0:SEQ]
                        if d:
                            o, i = o[:, ::-1], i[:, ::-1]
                        dve.tensor_tensor_scan(out=o, data0=i, data1=i, initial=m0[:, d:d + 1], op0=ALU.max, op1=ALU.max)
                        dve.tensor_scalar(gA[:, d, SEQ:T], gI[:, d, SEQ:T], mc[:, d:d + 1], None, ALU.subtract)
                    dve.drain().then_inc(s_dm, 1)
                    dve.scalar_tensor_tensor(gA[:, :, 0:SEQ], gA[:, :, 0:SEQ], -1.0, Mrow[:], ALU.mult, ALU.subtract).then_inc(s_scan, 1)
                    dve.wait_ge(s_col, 1)
                    dve.tensor_copy(colv[:].rearrange("p a h -> p (a h)"), PS[:, 5, 0:20 * H])
                    dve.tensor_copy(m0b[:].rearrange("p a h -> p (a h)"), PS[:, 6, 0:2 * H])

        w_loaded = [sem(f"proj_weights_loaded{i}") for i in range(WBUF)]
        s_tab = sem("tables_loaded")
        pe_half, act_evac = sem("proj_halves_summed"), sem("proj_kept")
        dve_conv, act_silu = sem("conv_done"), sem("conv_silu_done")
        pe_m1, act_m1, dve_m1 = sem("ml_v_turned"), sem("ml_v_kept"), sem("ml_ctx_keys_weighted")
        pe_m2, act_g, act_d = sem("ml_state_and_max_summed"), sem("ml_state_decay"), sem("ml_decay")
        pool_d, pe_st, dve_sd = sem("ml_decay_masked"), sem("ml_scores"), sem("ml_scores_decayed")
        dve_qg, pe_n, dve_n = sem("ml_queries_decayed"), sem("ml_sums"), sem("ml_divided")
        dve_ss, act_rs, dve_hn = sem("ml_squares"), sem("ml_rms"), sem("ml_normed")
        pe_m5, dve_mlout = sem("ml_out_turned"), sem("ml_out_kept")
        pe_rot, act_v = sem("rotated"), sem("values_kept")
        dve_rope, pe_s, dve_max = sem("rope_done"), sem("scores"), sem("scores_max")
        act_exp, dve_w, pe_t = sem("scores_exp"), sem("weights"), sem("weights_turned")
        act_wt, pe_p, dve_pn = sem("weights_kept"), sem("values_summed"), sem("attention_kept")
        dve_as, act_as, dve_an = sem("at_squares"), sem("at_rms"), sem("at_normed")
        pe_o, dve_dout = sem("at_out_turned"), sem("at_out_kept")

        with phase_a:
            W = sb("W", [P, WBUF, 8, P], ctx=phase_a)
            rp = sb("rp", [P, 2, SEQ], ctx=phase_a)
            cw = sb("cw", [P, 2 * H, CONV], ctx=phase_a)
            cb = sb("cb", [P, 2 * H], ctx=phase_a)
            rawq = sb("rawq", [P, SEQ + 2 * PAD], ctx=phase_a)
            rawk = sb("rawk", [P, SEQ + 2 * PAD], ctx=phase_a)
            rawc = sb("rawc", [P, CTX + 2 * PAD], ctx=phase_a)
            mq = sb("mq", [P, SEQ], ctx=phase_a)
            mk = sb("mk", [P, T], ctx=phase_a)
            mvT = sb("mvT", [P, T], ctx=phase_a)
            sig = sb("sig", [P, SEQ], ctx=phase_a)
            vaug = sb("vaug", [P, LT + CT, HD + 2], ctx=phase_a)
            kw = sb("kw", [P, 2, CT, HD], ctx=phase_a)
            onesH = sb("onesH", [H, P], ctx=phase_a)
            C0 = sb("C0", [P, 2, HD + 1], ctx=phase_a)
            Mh = sb("Mh", [H, 2, SEQ], ctx=phase_a)
            G = sb("G", [P, 2, SEQ], ctx=phase_a)
            DM = sb("DM", [P, 2, 2, SEQ], ctx=phase_a)
            SD = sb("SD", [P, 2, LT, SEQ], ctx=phase_a)
            den = sb("den", [P, 2], ctx=phase_a)
            hf = sb("hf", [P, HD], ctx=phase_a)
            hn = sb("hn", [P, LT, HD], ctx=phase_a)
            sqd = sb("sqd", [P, HD], ctx=phase_a)
            ss = sb("ss", [P, 2, LT], ctx=phase_a)
            rawdq = sb("rawdq", [P, SEQ], ctx=phase_a)
            rawdk = sb("rawdk", [P, SEQ], ctx=phase_a)
            qz = sb("qz", [P, 2, SEQ], ctx=phase_a)
            kk = sb("kk", [P, T], ctx=phase_a)
            dvT = mvT
            V = sb("V", [P, LT + CT, HD], ctx=phase_a)
            dmflat = DM[:].rearrange("p a b t -> p (a b t)")
            E = dmflat[:, 0:2 * T].rearrange("p (a t) -> p a t", a=2)
            Wt = sb("Wt", [P, T], ctx=phase_a)
            WT = sb("WT", [P, LT + CT, P], ctx=phase_a)
            tq, tr = E[:, 0, 0:SEQ], E[:, 1, 0:SEQ]
            mx = sb("mx", [P, 4], ctx=phase_a)
            nm = sb("nm", [P, 2], ctx=phase_a)
            Z = sb("Z", [P, 2, 2], ctx=phase_a)
            rz = sb("rz", [P, 2], ctx=phase_a)
            on = sb("on", [P, LT, HD], ctx=phase_a)

            MLK, DFK = ("mq", "mk", "mv", "mo"), ("dq", "dk", "dv")
            HAS_CTX = {"mk", "mv", "dk", "dv"}
            BANK = {"mq": 0, "mk": 1, "mv": 0, "mo": 1, "dq": 0, "dk": 1, "dv": 0}
            TILE = {k: i for i, k in enumerate(MLK + DFK)}
            CTXBANK = 2

            def spans(d, st):
                return (st * P, SEQ) if d == 0 else (0, (st + 1) * P)

            with nc.Block() as block:
                @block.sync
                def _(sp):
                    sp.dma_start(rp[:].rearrange("p a t -> p (a t)"), rope).then_inc(s_tab, 16)
                    sp.dma_start(cw[:].rearrange("p a t -> p (a t)"), convw).then_inc(s_tab, 16)
                    sp.dma_start(cb[:], convb).then_inc(s_tab, 16)
                    for b in range(WBUF):
                        sp.dma_start(W[:, b, :, :], wseq[b]).then_inc(w_loaded[b], 16)
                    with sp.Fori(1, HALVES // WBUF) as r:
                        for b in range(WBUF):
                            sp.wait_ge(pe_half, WBUF * r + b - WBUF + 1)
                            sp.dma_start(W[:, b, :, :], wseq[WBUF * r + b]).then_inc(w_loaded[b], 16)

                @block.tensor
                def _(pe):
                    B = lambda i: PS[:, i, :]

                    def half(h, kind, j):
                        ml = kind in MLK
                        i = 2 * (MLK.index(kind) if ml else DFK.index(kind)) + j
                        s = i if ml else 8 + i
                        b = s % WBUF
                        pe.wait_ge(w_loaded[b], 16 * (2 * h + s // WBUF + 1))
                        bank = BANK[kind]
                        if j == 0:
                            before = {"mq": 0, "mk": 0, "mv": 1, "mo": 2, "dq": 3, "dk": 4, "dv": 5}[kind]
                            if before or not isinstance(h, int):
                                pe.wait_ge(act_evac, 7 * h + before)
                        for k in range(8):
                            last = pe.matmul(B(bank), W[:, b, k, :], hT[:, 8 * j + k, 0:SEQ], start=(j + k == 0), stop=(j * k == 7))
                        if kind in HAS_CTX:
                            if j == 0 and kind in ("mv", "dv"):
                                pe.wait_ge(act_evac, 7 * h + TILE[kind])
                            for k in range(8):
                                last = pe.matmul(PS[:, CTXBANK, 0:CTX], W[:, b, k, :], hT[:, 8 * j + k, SEQ:T],
                                                 start=(j + k == 0), stop=(j * k == 7))
                        last.then_inc(pe_half, 1)

                    def m1(h):
                        pe.wait_ge(dve_dout, h + 1)
                        pe.wait_ge(act_evac, 7 * h + 3)
                        pe.wait_ge(act_silu, 2 * h + 2)
                        for t in range(LT):
                            pe.transpose(PS[:, 6, t * P:(t + 1) * P], mvT[:, t * P:(t + 1) * P], ident)
                        for t in range(CT):
                            pe.transpose(PS[:, 7, t * P:(t + 1) * P], mvT[:, SEQ + t * P:SEQ + (t + 1) * P], ident)
                            last = pe.transpose(PS[:, 7, (2 + t) * P:(3 + t) * P], mk[:, SEQ + t * P:SEQ + (t + 1) * P], ident)
                        last.then_inc(pe_m1, 1)

                    def m2(h):
                        pe.wait_ge(dve_m1, h + 1)
                        for d in range(2):
                            for t in range(CT):
                                pe.matmul(PS[:, 5, 256 * d:256 * d + HD + 1], kw[:, d, t, :], vaug[:, LT + t, 0:HD + 1],
                                          start=(t == 0), stop=(t == CT - 1))
                        for d in range(2):
                            last = pe.matmul(B(3 + d), onesH[:], Mh[:, d, :], start=True, stop=True)
                        last.then_inc(pe_m2, 1)

                    def st(h, t):
                        if t == 0:
                            pe.wait_ge(act_m1, h + 1)
                        elif t >= 2:
                            pe.wait_ge(dve_sd, 4 * h + t - 1)
                        pe.matmul(B(6 + t % 2), mk[:, t * P:(t + 1) * P], mq[:], start=True, stop=True).then_inc(pe_st, 1)

                    def nsum(h, t):
                        if t == 0:
                            pe.wait_ge(dve_sd, 4 * h + 4)
                            pe.wait_ge(dve_qg, h + 1)
                        elif t == 1:
                            pe.wait_ge(act_d, 4 * h + 4)
                        else:
                            pe.wait_ge(dve_n, 4 * h + t - 1)
                        bank = 5 if t % 2 == 0 else 3
                        for d in range(2):
                            o = PS[:, bank, 256 * d:256 * d + HD + 1]
                            for n, s in enumerate(range(0, t + 1) if d == 0 else range(t, LT)):
                                pe.matmul(o, SD[:, d, s, t * P:(t + 1) * P], vaug[:, s, 0:HD + 1], start=(n == 0), stop=False)
                            last = pe.matmul(o, G[:, d, t * P:(t + 1) * P], C0[:, d, :], start=False, stop=True)
                        last.then_inc(pe_n, 1)

                    def m5(h):
                        pe.wait_ge(dve_hn, h + 1)
                        for t in range(LT):
                            last = pe.transpose(PS[:, 4, t * P:(t + 1) * P], hn[:, t, :], ident)
                        last.then_inc(pe_m5, 1)

                    def rot(h):
                        pe.wait_ge(dve_mlout, h + 1)
                        pe.wait_ge(act_evac, 7 * h + 7)
                        pe.matmul(B(3), rotm, rawdq[:], start=True, stop=True)
                        pe.matmul(B(4), rotm, rawdk[:], start=True, stop=True)
                        for t in range(LT):
                            pe.transpose(PS[:, 6, t * P:(t + 1) * P], dvT[:, t * P:(t + 1) * P], ident)
                        for t in range(CT):
                            last = pe.transpose(PS[:, 7, t * P:(t + 1) * P], dvT[:, SEQ + t * P:SEQ + (t + 1) * P], ident)
                        last.then_inc(pe_rot, 1)

                    def scores(h, q):
                        if q == 0:
                            pe.wait_ge(dve_rope, h + 1)
                        else:
                            pe.wait_ge(act_exp, 4 * h + q)
                        for a in range(2):
                            pe.matmul(B(3 + a), qz[:, a, q * P:(q + 1) * P], kk[:, 0:SEQ], start=True, stop=True)
                            last = pe.matmul(PS[:, 5, a * CTX:(a + 1) * CTX], qz[:, a, q * P:(q + 1) * P], kk[:, SEQ:T], start=True, stop=True)
                        last.then_inc(pe_s, 1)

                    def turn(h, q):
                        pe.wait_ge(dve_w, 4 * h + q + 1)
                        if q == 0:
                            pe.wait_ge(act_v, h + 1)
                        else:
                            pe.wait_ge(dve_pn, 4 * h + q)
                        for t in range(LT + CT):
                            last = pe.transpose(PS[:, 6 + t // 4, (t % 4) * P:(t % 4 + 1) * P], Wt[:, t * P:(t + 1) * P], ident)
                        last.then_inc(pe_t, 1)

                    def pv(h, q):
                        pe.wait_ge(act_wt, 4 * h + q + 1)
                        for t in range(LT + CT):
                            last = pe.matmul(PS[:, 7, 256:384], WT[:, t, :], V[:, t, :], start=(t == 0), stop=(t == LT + CT - 1))
                        last.then_inc(pe_p, 1)

                    def outT(h):
                        pe.wait_ge(dve_an, h + 1)
                        for t in range(LT):
                            last = pe.transpose(PS[:, 6, t * P:(t + 1) * P], on[:, t, :], ident)
                        last.then_inc(pe_o, 1)

                    def stage_a(h):
                        half(h, "dq", 0); m1(h); half(h, "dq", 1); m2(h)
                        half(h, "dk", 0); st(h, 0); st(h, 1); half(h, "dk", 1); st(h, 2); st(h, 3)
                        half(h, "dv", 0); nsum(h, 0); nsum(h, 1); half(h, "dv", 1); nsum(h, 2); nsum(h, 3)
                        m5(h)

                    def stage_b(h, proj):
                        g = h + 1
                        if proj: half(g, "mq", 0)
                        rot(h)
                        if proj: half(g, "mq", 1)
                        scores(h, 0)
                        if proj: half(g, "mk", 0)
                        turn(h, 0); scores(h, 1)
                        if proj: half(g, "mk", 1)
                        pv(h, 0)
                        if proj: half(g, "mv", 0)
                        turn(h, 1); scores(h, 2)
                        if proj: half(g, "mv", 1)
                        pv(h, 1)
                        if proj: half(g, "mo", 0)
                        turn(h, 2); scores(h, 3)
                        if proj: half(g, "mo", 1)
                        pv(h, 2); turn(h, 3); pv(h, 3); outT(h)

                    pe.wait_ge(s_tab, 48 + 1)
                    for kind in MLK:
                        half(0, kind, 0)
                        half(0, kind, 1)
                    with pe.Fori(0, H - 1) as h:
                        stage_a(h)
                        stage_b(h, True)
                    stage_a(H - 1)
                    stage_b(H - 1, False)

                @block.scalar
                def _(act):
                    def keep_mq(h):
                        act.wait_ge(pe_half, 14 * h + 2)
                        if not (isinstance(h, int) and h == 0):
                            act.wait_ge(dve_mlout, h)
                        else:
                            act.wait_ge(s_tab, 48 + 1)
                        act.activation(rawq[:, PAD:PAD + SEQ], PS[:, 0, :], ACT.Copy).then_inc(act_evac, 1)

                    def keep_mk(h):
                        act.wait_ge(pe_half, 14 * h + 4)
                        act.activation(rawk[:, PAD:PAD + SEQ], PS[:, 1, :], ACT.Copy)
                        act.activation(rawc[:, PAD:PAD + CTX], PS[:, 2, 0:CTX], ACT.Copy).then_inc(act_evac, 1)

                    def keep_mv(h):
                        act.wait_ge(pe_half, 14 * h + 6)
                        act.activation(mvT[:, 0:SEQ], PS[:, 0, :], ACT.Copy)
                        act.activation(mvT[:, SEQ:T], PS[:, 2, 0:CTX], ACT.Copy).then_inc(act_evac, 1)

                    def keep_mo(h):
                        act.wait_ge(pe_half, 14 * h + 8)
                        act.activation(sig[:], PS[:, 1, :], ACT.Sigmoid).then_inc(act_evac, 1)

                    def silu_q(h):
                        act.wait_ge(dve_conv, 2 * h + 1)
                        act.activation(mq[:], mq[:], ACT.Silu).then_inc(act_silu, 1)

                    def silu_k(h):
                        act.wait_ge(dve_conv, 2 * h + 2)
                        act.activation(mk[:], mk[:], ACT.Silu).then_inc(act_silu, 1)

                    def keep_v(h):
                        act.wait_ge(pe_m1, h + 1)
                        act.activation(vaug[:, 0:LT, 0:HD], PS[:, 6, :].rearrange("p (t c) -> p t c", c=HD), ACT.Copy).then_inc(act_m1, 1)

                    def state_decay(h):
                        act.wait_ge(pe_m2, h + 1)
                        act.activation(C0[:], PS[:, 5, :].rearrange("p (d c) -> p d c", d=2)[:, :, 0:HD + 1], ACT.Copy)
                        for d in range(2):
                            last = act.activation(G[:, d, :], PS[:, 3 + d, :], ACT.Exp, scale=-1.0, bias=m0b[:, d, bass.ds(h, 1)])
                        last.then_inc(act_g, 1)

                    def decay(h, t):
                        if t >= 2:
                            act.wait_ge(dve_sd, 4 * h + t - 1)
                        for d in range(2):
                            l0, l1 = spans(d, t)
                            last = act.activation(DM[:, t % 2, d, l0:l1], PS[:, 3 + d, l0:l1], ACT.Exp, scale=-1.0,
                                                  bias=colv[:, d * LT + t, bass.ds(h, 1)])
                        last.then_inc(act_d, 1)

                    def rms(i, ready, n, done):
                        act.wait_ge(ready, n)
                        act.activation(ss[:, i, :], ss[:, i, :], ACT.Ln)
                        act.drain()
                        act.activation(ss[:, i, :], ss[:, i, :], ACT.Exp, scale=-0.5).then_inc(done, 1)

                    def keep_dq(h):
                        act.wait_ge(pe_half, 14 * h + 10)
                        act.wait_ge(dve_dout, h + 1)
                        act.activation(rawdq[:], PS[:, 0, :], ACT.Copy).then_inc(act_evac, 1)

                    def keep_dk(h):
                        act.wait_ge(pe_half, 14 * h + 12)
                        act.activation(rawdk[:], PS[:, 1, :], ACT.Copy)
                        act.activation(kk[:, SEQ:T], PS[:, 2, 0:CTX], ACT.Copy).then_inc(act_evac, 1)

                    def keep_dv(h):
                        act.wait_ge(pe_half, 14 * h + 14)
                        act.activation(dvT[:, 0:SEQ], PS[:, 0, :], ACT.Copy)
                        act.activation(dvT[:, SEQ:T], PS[:, 2, 0:CTX], ACT.Copy).then_inc(act_evac, 1)

                    def keep_values(h):
                        act.wait_ge(pe_rot, h + 1)
                        act.activation(V[:, 0:LT, :], PS[:, 6, :].rearrange("p (t c) -> p t c", c=HD), ACT.Copy)
                        act.activation(V[:, LT:LT + CT, :], PS[:, 7, 0:CTX].rearrange("p (t c) -> p t c", c=HD), ACT.Copy).then_inc(act_v, 1)

                    def exps(h, q):
                        act.wait_ge(dve_max, 4 * h + q + 1)
                        for a in range(2):
                            act.activation(E[:, a, 0:SEQ], PS[:, 3 + a, :], ACT.Exp, scale=HALF ** -0.5, bias=nm[:, a:a + 1],
                                           accum_out=Z[:, 0, a:a + 1])
                            last = act.activation(E[:, a, SEQ:T], PS[:, 5, a * CTX:(a + 1) * CTX], ACT.Exp, scale=HALF ** -0.5,
                                                  bias=nm[:, a:a + 1], accum_out=Z[:, 1, a:a + 1])
                        last.then_inc(act_exp, 1)

                    def keep_wt(h, q):
                        act.wait_ge(pe_t, 4 * h + q + 1)
                        act.activation(WT[:].rearrange("p t c -> p (t c)"), PS[:, 6:8, :].rearrange("p b c -> p (b c)")[:, 0:T], ACT.Copy).then_inc(act_wt, 1)

                    def stage_a(h):
                        keep_v(h); keep_dq(h); state_decay(h); decay(h, 0); decay(h, 1); decay(h, 2); decay(h, 3)
                        keep_dk(h); keep_dv(h); rms(0, dve_ss, h + 1, act_rs)

                    def stage_b(h, proj):
                        g = h + 1
                        keep_values(h)
                        if proj: keep_mq(g)
                        exps(h, 0)
                        keep_wt(h, 0)
                        exps(h, 1)
                        if proj: keep_mk(g); silu_q(g)
                        keep_wt(h, 1)
                        exps(h, 2)
                        if proj: keep_mv(g)
                        keep_wt(h, 2)
                        exps(h, 3)
                        if proj: silu_k(g); keep_mo(g)
                        keep_wt(h, 3)
                        rms(1, dve_as, h + 1, act_as)

                    keep_mq(0); keep_mk(0); silu_q(0); keep_mv(0); silu_k(0); keep_mo(0)
                    with act.Fori(0, H - 1) as h:
                        stage_a(h)
                        stage_b(h, True)
                    stage_a(H - 1)
                    stage_b(H - 1, False)

                @block.gpsimd
                def _(pool):
                    def mask(h):
                        for t in range(LT):
                            pool.wait_ge(act_d, 4 * h + t + 1)
                            pool.sem_inc(s_passed)
                            for d, sign in ((0, 1), (1, -1)):
                                blk = DM[:, t % 2, d, t * P:(t + 1) * P]
                                last = pool.affine_select(out=blk, in_=blk, pattern=[[sign, P]], compare_op=ALU.is_ge, fill=0.0,
                                                          base=0, channel_multiplier=-sign)
                            last.then_inc(pool_d, 1)
                    with pool.Fori(0, H) as h:
                        mask(h)

                @block.vector
                def _(dve):
                    def conv(o, raw, n, c):
                        dve.tensor_scalar(o, raw[:, 0:n], cw[:, c, 0:1], cb[:, bass.ds(c, 1)], ALU.mult, ALU.add)
                        for j in range(1, CONV):
                            dve.drain()
                            last = dve.scalar_tensor_tensor(o, raw[:, j:j + n], cw[:, c, j:j + 1], o, ALU.mult, ALU.add)
                        return last

                    def conv_q(h):
                        dve.wait_ge(act_evac, 7 * h + 1)
                        conv(mq[:], rawq, SEQ, h).then_inc(dve_conv, 1)

                    def conv_k(h):
                        dve.wait_ge(act_evac, 7 * h + 2)
                        conv(mk[:, 0:SEQ], rawk, SEQ, h + H)
                        conv(mk[:, SEQ:T], rawc, CTX, h + H).then_inc(dve_conv, 1)

                    def ctx_keys(h):
                        dve.tensor_scalar(Mh[:].rearrange("p d t -> p (d t)"), Mrow[:].rearrange("p d t -> p (d t)"),
                                          ident[0:H, bass.ds(h, 1)], None, ALU.mult)
                        dve.wait_ge(pe_m1, h + 1)
                        dve.tensor_copy(vaug[:, LT:LT + CT, 0:HD], PS[:, 7, 0:CTX].rearrange("p (t c) -> p t c", c=HD))
                        for d in range(2):
                            for t in range(CT):
                                last = dve.tensor_scalar(kw[:, d, t, :], PS[:, 7, (2 + t) * P:(3 + t) * P],
                                                         colv[:, 16 + d * CT + t, bass.ds(h, 1)], HD ** -0.5, ALU.mult, ALU.mult)
                        last.then_inc(dve_m1, 1)

                    def decayed_queries(h):
                        dve.wait_ge(act_g, h + 1)
                        for d in range(2):
                            last = dve.tensor_tensor(G[:, d, :], G[:, d, :], mq[:], ALU.mult)
                        last.then_inc(dve_qg, 1)

                    def decayed_scores(h, t):
                        dve.wait_ge(pool_d, 4 * h + t + 1)
                        dve.wait_ge(pe_st, 4 * h + t + 1)
                        for d in range(2):
                            l0, l1 = spans(d, t)
                            last = dve.scalar_tensor_tensor(SD[:, d, t, l0:l1], PS[:, 6 + t % 2, l0:l1], HD ** -0.5, DM[:, t % 2, d, l0:l1],
                                                            ALU.mult, ALU.mult)
                        last.then_inc(dve_sd, 1)

                    def squares(o, src):
                        dve.scalar_tensor_tensor(sqd[:], src, 1.0, src, ALU.mult, ALU.mult, accum_out=o)

                    def mean_eps(i):
                        dve.drain()
                        dve.tensor_scalar(ss[:, i, :], ss[:, i, :], 1.0 / HD, RMS_EPS, ALU.mult, ALU.add)

                    def divide(h, t):
                        dve.wait_ge(pe_n, 4 * h + t + 1)
                        bank = PS[:, 5 if t % 2 == 0 else 3, :].rearrange("p (d c) -> p d c", d=2)
                        dsum = bank[:, :, HD:HD + 1].rearrange("p d c -> p (d c)")
                        floor = colv[:, 8 + t:8 + t + LT + 1:LT, bass.ds(h, 1)].rearrange("p d c -> p (d c)")
                        dve.scalar_tensor_tensor(den[:], dsum, -1.0, floor, ALU.mult, ALU.max)
                        dve.drain()
                        dve.tensor_tensor(den[:], dsum, den[:], ALU.max)
                        dve.drain()
                        dve.reciprocal(den[:], den[:])
                        dve.drain()
                        dve.tensor_scalar(hf[:], bank[:, 0, 0:HD], den[:, 0:1], None, ALU.mult)
                        dve.drain()
                        dve.scalar_tensor_tensor(hn[:, t, :], bank[:, 1, 0:HD], den[:, 1:2], hf[:], ALU.mult, ALU.add).then_inc(dve_n, 1)
                        dve.drain()
                        squares(ss[:, 0, t:t + 1], hn[:, t, :])

                    def ml_norm(h):
                        mean_eps(0)
                        dve.drain().then_inc(dve_ss, 1)
                        dve.wait_ge(act_rs, h + 1)
                        dve.tensor_tensor(hn[:], hn[:], ss[:, 0, :].unsqueeze(2).to_broadcast([P, LT, HD]), ALU.mult).then_inc(dve_hn, 1)
                        dve.wait_ge(pe_m5, h + 1)
                        dve.scalar_tensor_tensor(mixT[:, bass.ds(h + H, 1), :].rearrange("p a t -> p (a t)"), PS[:, 4, :], gains[:, 1:2], sig[:], ALU.mult, ALU.mult).then_inc(dve_mlout, 1)

                    def rope_qk(h):
                        dve.wait_ge(pe_rot, h + 1)
                        for raw, bank in ((rawdq, 3), (rawdk, 4)):
                            dve.tensor_tensor(tq, raw[:], rp[:, 0, :], ALU.mult)
                            dve.tensor_tensor(tr, PS[:, bank, :], rp[:, 1, :], ALU.mult)
                            dve.drain()
                            if bank == 3:
                                for a in range(2):
                                    r = slice(HALF * a, HALF * (a + 1))
                                    last = dve.tensor_tensor(qz[r, a, :], tq[r, :], tr[r, :], ALU.add)
                            else:
                                last = dve.tensor_tensor(kk[:, 0:SEQ], tq, tr, ALU.add)
                            dve.drain()
                        dve.drain().then_inc(dve_rope, 1)

                    def maxima(h, q):
                        dve.wait_ge(pe_s, 4 * h + q + 1)
                        dve.tensor_reduce(mx[:, 0:2], PS[:, 3:5, :], AX.X, ALU.max)
                        dve.tensor_reduce(mx[:, 2:4], PS[:, 5, :].rearrange("p (a c) -> p a c", a=2), AX.X, ALU.max)
                        dve.drain()
                        dve.tensor_tensor(nm[:], mx[:, 0:2], mx[:, 2:4], ALU.max)
                        dve.drain()
                        dve.tensor_scalar(nm[:], nm[:], -HALF ** -0.5, None, ALU.mult).then_inc(dve_max, 1)

                    def weights(h, q):
                        dve.wait_ge(act_exp, 4 * h + q + 1)
                        dve.tensor_tensor(rz[:], Z[:, 0, :], Z[:, 1, :], ALU.add)
                        dve.drain()
                        dve.reciprocal(rz[:], rz[:])
                        dve.drain()
                        dve.tensor_tensor(rz[:, 1:2], rz[:, 1:2], neglam[:], ALU.mult)
                        if q:
                            dve.wait_ge(pe_t, 4 * h + q)
                        dve.tensor_scalar(Wt[:], E[:, 0, :], rz[:, 0:1], None, ALU.mult)
                        dve.drain()
                        dve.scalar_tensor_tensor(Wt[:], E[:, 1, :], rz[:, 1:2], Wt[:], ALU.mult, ALU.add).then_inc(dve_w, 1)

                    def keep_att(h, q):
                        dve.wait_ge(pe_p, 4 * h + q + 1)
                        dve.tensor_copy(on[:, q, :], PS[:, 7, 256:384]).then_inc(dve_pn, 1)
                        dve.drain()
                        squares(ss[:, 1, q:q + 1], on[:, q, :])

                    def att_norm(h):
                        mean_eps(1)
                        dve.drain().then_inc(dve_as, 1)
                        dve.wait_ge(act_as, h + 1)
                        dve.tensor_tensor(on[:], on[:], ss[:, 1, :].unsqueeze(2).to_broadcast([P, LT, HD]), ALU.mult).then_inc(dve_an, 1)
                        dve.wait_ge(pe_o, h + 1)
                        dve.tensor_scalar(mixT[:, bass.ds(h, 1), :].rearrange("p a t -> p (a t)"), PS[:, 6, :], gains[:, 0:1], None, ALU.mult).then_inc(dve_dout, 1)

                    def stage_a(h):
                        ctx_keys(h); decayed_queries(h)
                        for t in range(LT):
                            decayed_scores(h, t)
                        for t in range(LT):
                            divide(h, t)
                        ml_norm(h)

                    def stage_b(h, proj):
                        g = h + 1
                        rope_qk(h); maxima(h, 0)
                        if proj: conv_q(g)
                        weights(h, 0); maxima(h, 1); weights(h, 1); keep_att(h, 0)
                        if proj: conv_k(g)
                        maxima(h, 2); weights(h, 2); keep_att(h, 1)
                        maxima(h, 3); weights(h, 3); keep_att(h, 2); keep_att(h, 3)
                        att_norm(h)

                    for pad in (rawq[:, 0:PAD], rawq[:, PAD + SEQ:], rawk[:, 0:PAD], rawk[:, PAD + SEQ:], rawc[:, 0:PAD], rawc[:, PAD + CTX:]):
                        dve.memset(pad, 0.0)
                    dve.memset(vaug[:, :, HD:HD + 2], 1.0)
                    dve.memset(onesH[:], 1.0)
                    dve.memset(qz[HALF:P, 0, :], 0.0)
                    dve.memset(qz[0:HALF, 1, :], 0.0)
                    dve.drain().then_inc(s_tab, 1)
                    dve.drain().then_inc(dve_dout, 1)
                    dve.wait_ge(s_tab, 49)
                    conv_q(0); conv_k(0)
                    with dve.Fori(0, H - 1) as h:
                        stage_a(h)
                        stage_b(h, True)
                    stage_a(H - 1)
                    stage_b(H - 1, False)

        x1 = sb("x1", [P, LT, D])
        vecs = sb("vecs", [P, 4, D])
        lng = sb("lng", [P, 2, D])
        eidx = sb("eidx", [P, 2 * NG, GROUP], u32)
        gate = sb("gate", [P, 2 * NG, GROUP])
        st6 = sb("st6", [P, 4, 6])
        mv2 = sb("mv2", [P, 2])
        rsd = sb("rsd", [P, 1])
        h2 = mixT[:].rearrange("p k t -> p (k t)").rearrange("p (t d) -> p t d", t=LT)

        s_ld3 = sem("residual_and_vectors_loaded")
        s_rep = sem("silu_spread3")
        s_wb = [sem("chunk_loaded0"), sem("chunk_loaded1")]
        s_cpe, s_cev = sem("chunk_summed"), sem("chunk_kept")
        s_keys = sem("keys_loaded")
        s_wq = [sem("query_weights_loaded0"), sem("query_weights_loaded1")]
        s_stat, s_std = sem("ln_stats"), sem("ln_std")
        s_h2, s_hTpe, s_hTev = sem("peer_input"), sem("peer_input_turned"), sem("peer_input_turned_kept")
        s_qpe, s_qev = sem("queries_summed"), sem("queries_kept")
        s_spe, s_sev = sem("key_scores"), sem("key_scores_kept")
        s_top, s_gex = sem("chosen"), sem("chosen_exps")
        s_zero, s_zeroed = sem("zeros_ready"), sem("gates_cleared")
        s_dense, s_scat = sem("dense_gates_ready"), sem("dense_gates_added")
        s_added = sem("heads_gates_added")
        s_h2Td = sem("dense_input_kept")

        def layer_norm(dve, src, sem_stat, sem_std, n):
            for i in range(4):
                dve.bn_stats(st6[:, i, :], src[:, i * 512:(i + 1) * 512])
            dve.drain()
            dve.bn_aggr(mv2[:], st6[:].rearrange("p a b -> p (a b)"))
            dve.drain()
            dve.tensor_scalar(rsd[:], mv2[:, 1:2], LN_EPS, None, ALU.add).then_inc(sem_stat, 1)
            dve.wait_ge(sem_std, n)
            dve.reciprocal(rsd[:], rsd[:])
            dve.drain()
            dve.tensor_scalar(src, src, mv2[:, 0:1], rsd[:, 0:1], ALU.subtract, ALU.mult)
            dve.drain()
            dve.tensor_tensor(src, src, lng[:, 0, :], ALU.mult)
            dve.drain()
            return dve.tensor_tensor(src, src, lng[:, 1, :], ALU.add)

        b3 = ExitStack()
        with b3:
            ring = sb("ring", [P, 2, KT, CHUNK], ctx=b3)
            wqb = sb("wqb", [P, 2, KT, P], ctx=b3)
            kys = sb("kys", [P, 2 * PH, NKEYS], ctx=b3)
            silB = wqb[:, 0, :, :]
            h2T = ring[:, 0, :, :]
            rest = ring[:, 1, :, :].rearrange("p k c -> p (k c)")
            def carve(at, shape, dt=f32):
                n = int(np.prod(shape[1:]))
                v = rest[:, at:at + n]
                if dt is not f32:
                    v = v.bitcast(dt)
                if len(shape) == 2:
                    return v
                names = "abcd"[:len(shape) - 1]
                return v.rearrange(f"p ({' '.join(names)}) -> p {' '.join(names)}", **dict(zip(names, shape[1:])))
            qT = carve(0, [P, 2, SEQ])
            sc = carve(1024, [P, LT, 2, NKEYS])
            s2 = carve(2048, [P, LT, 2, NKEYS])
            cand = carve(3072, [P, LT, TOPK * TOPK])
            cand2 = carve(4096, [P, LT, TOPK * TOPK])
            oh = carve(5120, [P, LT, TOPK, TOPK])
            vv = carve(6144, [P, LT, 2, TOPK])
            ii = carve(6272, [P, LT, 2, TOPK], u32)
            iif = carve(6400, [P, LT, 2, TOPK])
            tv = carve(6528, [P, LT, TOPK])
            tp = carve(6592, [P, LT, TOPK], u32)
            ab = carve(6656, [P, 2, LT, TOPK], u32)
            abf = carve(6784, [P, 2, LT, TOPK])
            sel = carve(6912, [P, 2, LT, TOPK])
            ef = carve(7040, [P, LT, TOPK])
            gx = carve(7104, [P, LT, TOPK])
            gs = carve(7168, [P, LT])
            dgate = carve(7172, [P, DT, TOPK])
            didx = carve(7204, [P, DT, TOPK], u32)
            h2Td = mixT[:].rearrange("p k t -> p (k t)")[:, 0:KT * DTOK].rearrange("p (k t) -> p k t", k=KT)
            yg = gate[:].rearrange("p a b -> p (a b)")

            with nc.Block() as block:
                @block.sync
                def _(sp):
                    wv = wada.rearrange("(k p) (n c) -> p k n c", p=P, c=CHUNK)
                    ov = wout.rearrange("(k p) (n c) -> p k n c", p=P, c=CHUNK)
                    for j in range(2):
                        sp.dma_start(ring[:, j, :, :], wv[:, :, SH_CHUNKS + j, :]).then_inc(s_wb[j], 16)
                    for i in range(4):
                        sp.dma_start(vecs[:, i, :], brow[i:i + 1, :].partition_broadcast(P)).then_inc(s_ld3, 16)
                    sp.dma_start(x1[:], x.rearrange("(t p) d -> p t d", p=P)).then_inc(s_ld3, 16)
                    for i in range(2):
                        sp.dma_start(lng[:, i, :], lnv[i:i + 1, :].partition_broadcast(P)).then_inc(s_ld3, 16)
                    sp.dma_start(kys[:].rearrange("p a k -> p (a k)"), keysT).then_inc(s_keys, 16)
                    with sp.Fori(1, REST_CHUNKS // 2) as n:
                        for j in range(2):
                            sp.wait_ge(s_cpe, 2 * n + j - 1)
                            sp.dma_start(ring[:, j, :, :], wv[:, :, SH_CHUNKS + 2 * n + j, :]).then_inc(s_wb[j], 16)
                    with sp.Fori(0, OUT_CHUNKS // 2) as n:
                        for j in range(2):
                            sp.wait_ge(s_cpe, 2 * n + j + REST_CHUNKS - 1)
                            sp.dma_start(ring[:, j, :, :], ov[:, :, 2 * n + j, :]).then_inc(s_wb[j], 16)
                    sp.wait_ge(s_cpe, REST_CHUNKS)
                    for j in range(2):
                        sp.dma_start(wqb[:, j, :, :], wq[j]).then_inc(s_wq[j], 16)
                    with sp.Fori(1, PH) as n:
                        for j in range(2):
                            sp.wait_ge(s_qpe, 2 * n + j - 1)
                            sp.dma_start(wqb[:, j, :, :], wq[2 * n + j]).then_inc(s_wq[j], 16)

                @block.tensor
                def _(pe):
                    pe.wait_ge(s_rep, 1)
                    with pe.Fori(0, REST_CHUNKS // 2) as n:
                        for j in range(2):
                            pe.wait_ge(s_wb[j], 16 * n + 16)
                            pe.wait_ge(s_cev, 2 * n + j + 1)
                            for k in range(KT):
                                last = pe.matmul(PS[:, j, :], silB[:, k, :], ring[:, j, k, :], start=(k == 0), stop=(k == KT - 1))
                            last.then_inc(s_cpe, 1)
                    pe.wait_ge(s_cev, REST_CHUNKS + 2)
                    with pe.Fori(0, OUT_CHUNKS // 2) as n:
                        for j in range(2):
                            pe.wait_ge(s_wb[j], 16 * n + 16 * (REST_CHUNKS // 2) + 16)
                            pe.wait_ge(s_cev, 2 * n + j + REST_CHUNKS + 1)
                            for t in range(LT):
                                for k in range(KT):
                                    last = pe.matmul(PS[:, 4 * j + t, :], mixT[:, k, t * P:(t + 1) * P], ring[:, j, k, :],
                                                     start=(k == 0), stop=(k == KT - 1))
                            last.then_inc(s_cpe, 1)
                    for t in range(LT):
                        pe.wait_ge(s_h2, t + 1)
                        for q in range(4):
                            n = 4 * t + q
                            if n >= 4:
                                pe.wait_ge(s_hTev, n - 3)
                            for i in range(4):
                                k = 4 * q + i
                                last = pe.transpose(PS[:, n % 4, i * P:(i + 1) * P], h2[:, t, k * P:(k + 1) * P], ident)
                            last.then_inc(s_hTpe, 1)
                    pe.wait_ge(s_hTev, 16)
                    pe.wait_ge(s_keys, 16)

                    def queries(m, j):
                        pe.wait_ge(s_wq[j], 16 * m + 16)
                        pe.wait_ge(s_qev, 2 * m + j + 1)
                        for k in range(KT):
                            last = pe.matmul(PS[:, j, :], wqb[:, j, k, :], h2T[:, k, :], start=(k == 0), stop=(k == KT - 1))
                        last.then_inc(s_qpe, 1)

                    def key_scores(m, j):
                        pe.wait_ge(s_qev, 2 * m + j + 3)
                        pe.wait_ge(s_sev, 2 * m + j + 1)
                        for t in range(LT):
                            last = pe.matmul(PS[:, 2 + j, t * NKEYS:(t + 1) * NKEYS], qT[:, j, t * P:(t + 1) * P],
                                             kys[:, bass.ds(2 * m + j, 1), :].rearrange("p a k -> p (a k)"), start=True, stop=True)
                        last.then_inc(s_spe, 1)

                    queries(0, 0)
                    with pe.Fori(0, PH - 1) as m:
                        queries(m, 1); key_scores(m, 0); queries(m + 1, 0); key_scores(m, 1)
                    queries(PH - 1, 1); key_scores(PH - 1, 0); key_scores(PH - 1, 1)

                @block.gpsimd
                def _(pool):
                    cells = gates_dram.rearrange("e (t o) -> (e t) o", o=1)
                    pool.wait_ge(s_zeroed, 16 * 8)
                    with pool.Fori(0, PH) as m:
                        pool.wait_ge(s_dense, m + 1)
                        pool.sem_inc(s_passed)
                        for t in range(DT):
                            for k in range(TOPK):
                                pool.indirect_dma_start(out=cells, out_offset=bass.IndirectOffsetOnAxis(ap=didx[:, t, k:k + 1], axis=0),
                                                        in_=dgate[:, t, k:k + 1], in_offset=None, compute_op=ALU.add).then_inc(s_scat, 16)
                        pool.wait_ge(s_scat, (16 * DT * TOPK) * m + 16 * DT * TOPK)
                        pool.sem_inc(s_added)

                @block.scalar
                def _(act):
                    act.wait_ge(s_zero, 1)
                    gz = gates_dram.rearrange("(p a) t -> p (a t)", p=P).rearrange("p (b r c) -> b p r c", b=8, c=512)
                    zsrc = eidx[:].rearrange("p a b -> p (a b)").bitcast(f32).unsqueeze(1).to_broadcast([P, 8, 512])
                    for b in range(8):
                        act.dma_start(gz[b], zsrc).then_inc(s_zeroed, 16)
                    for t in range(LT):
                        act.wait_ge(s_stat, t + 1)
                        act.activation(rsd[:], rsd[:], ACT.Sqrt).then_inc(s_std, 1)
                        for q in range(4):
                            n = 4 * t + q
                            act.wait_ge(s_hTpe, n + 1)
                            act.activation(h2T[:, 4 * q:4 * q + 4, t * P:(t + 1) * P],
                                           PS[:, n % 4, :].rearrange("p (i c) -> p i c", i=4), ACT.Copy).then_inc(s_hTev, 1)

                    def keep_queries(m):
                        for j in range(2):
                            act.wait_ge(s_qpe, 2 * m + j + 1)
                            act.wait_ge(s_spe, 2 * m + j + 1)
                            act.activation(qT[:, j, :], PS[:, j, :], ACT.Copy).then_inc(s_qev, 1)

                    def keep_scores(m):
                        act.wait_ge(s_top, m + 1)
                        for j in range(2):
                            act.wait_ge(s_spe, 2 * m + j + 3)
                            act.activation(sc[:, :, j, :], PS[:, 2 + j, :].rearrange("p (t k) -> p t k", k=NKEYS), ACT.Copy).then_inc(s_sev, 1)

                    def gate_exps(m):
                        act.wait_ge(s_top, m + 2)
                        act.activation(gx, gx, ACT.Exp).then_inc(s_gex, 1)

                    keep_queries(0); keep_scores(0)
                    with act.Fori(1, PH) as m:
                        keep_queries(m); gate_exps(m - 1); keep_scores(m)
                    act.activation(h2Td, h2T[:, :, 0:DTOK], ACT.Copy).then_inc(s_h2Td, 1)
                    gate_exps(PH - 1)

                @block.vector
                def _(dve):
                    for i in range(2):
                        for s in (s_cev, s_qev, s_sev, s_spe):
                            dve.drain().then_inc(s, 1)
                    dve.drain().then_inc(s_top, 1)
                    dve.memset(eidx[:], 0).then_inc(s_zero, 1)
                    dve.tensor_copy(silB, silc[:, 0, :].unsqueeze(2).to_broadcast([P, KT, P])).then_inc(s_rep, 1)
                    dve.wait_ge(s_ld3, 7 * 16)
                    vflat = vecs[:].rearrange("p a d -> p (a d)")
                    with dve.Fori(0, REST_CHUNKS // 2) as n:
                        for j in range(2):
                            dve.wait_ge(s_cpe, 2 * n + j + 1)
                            part = vflat[:, bass.ds((2 * n + j) * CHUNK, CHUNK)]
                            dve.tensor_tensor(part, PS[:, j, :], part, ALU.add).then_inc(s_cev, 1)
                    dve.drain()
                    dve.tensor_scalar(vecs[:, 2, :], vecs[:, 2, :], 1.0, None, ALU.add)
                    with dve.Fori(0, OUT_CHUNKS // 2) as n:
                        for j in range(2):
                            dve.wait_ge(s_cpe, 2 * n + j + REST_CHUNKS + 1)
                            cols = bass.ds((2 * n + j) * CHUNK, CHUNK)
                            for t in range(LT):
                                last = dve.tensor_tensor(yg, PS[:, 4 * j + t, :], vecs[:, 0, cols], ALU.mult)
                                if t == LT - 1:
                                    last.then_inc(s_cev, 1)
                                dve.drain()
                                dve.scalar_tensor_tensor(x1[:, t, cols], x1[:, t, cols], ALPHA, yg, ALU.mult, ALU.add)
                                dve.drain()
                    for t in range(LT):
                        layer_norm(dve, x1[:, t, :], s_stat, s_std, t + 1)
                        dve.drain()
                        dve.tensor_tensor(h2[:, t, :], x1[:, t, :], vecs[:, 2, :], ALU.mult)
                        dve.drain()
                        dve.tensor_tensor(h2[:, t, :], h2[:, t, :], vecs[:, 1, :], ALU.add).then_inc(s_h2, 1)

                    def top16(groups):
                        for src, tmp, v, i in groups:
                            dve.max(v[:, 0:8], src)
                        dve.drain()
                        for src, tmp, v, i in groups:
                            dve.max_index(i[:, 0:8], v[:, 0:8], src)
                            dve.match_replace(out=tmp, in_to_replace=v[:, 0:8], in_values=src, imm_value=NEG)
                        dve.drain()
                        for src, tmp, v, i in groups:
                            dve.max(v[:, 8:16], tmp)
                        dve.drain()
                        for src, tmp, v, i in groups:
                            dve.max_index(i[:, 8:16], v[:, 8:16], tmp)
                        dve.drain()

                    eview = eidx[:, 0:NG, :].rearrange("p (t m a) b -> p t m (a b)", t=LT - DT, m=PH)
                    gview = gate[:, 0:NG, :].rearrange("p (t m a) b -> p t m (a b)", t=LT - DT, m=PH)
                    flat = lambda v: v.rearrange("p a b -> p (a b)")
                    dve.wait_ge(s_zeroed, 16 * 8)
                    dve.drain().then_inc(s_added, 1)
                    with dve.Fori(0, PH) as m:
                        dve.wait_ge(s_sev, 2 * m + 4)
                        dve.memset(gs, 0.0)
                        top16([(sc[:, t, j, :], s2[:, t, j, :], vv[:, t, j, :], ii[:, t, j, :]) for t in range(LT) for j in range(2)])
                        for t in range(LT):
                            dve.tensor_tensor(cand[:, t, :].rearrange("p (a b) -> p a b", a=TOPK),
                                              vv[:, t, 0, :].unsqueeze(2).to_broadcast([P, TOPK, TOPK]),
                                              vv[:, t, 1, :].unsqueeze(1).to_broadcast([P, TOPK, TOPK]), ALU.add)
                        dve.tensor_copy(iif, ii)
                        dve.drain()
                        top16([(cand[:, t, :], cand2[:, t, :], tv[:, t, :], tp[:, t, :]) for t in range(LT)])
                        dve.tensor_tensor(gx, tv, tv[:, :, 0:1].to_broadcast([P, LT, TOPK]), ALU.subtract).then_inc(s_top, 1)
                        dve.tensor_scalar(flat(ab[:, 0, :, :]), flat(tp), 4, None, ALU.logical_shift_right)
                        dve.tensor_scalar(flat(ab[:, 1, :, :]), flat(tp), TOPK - 1, None, ALU.bitwise_and)
                        dve.drain()
                        dve.tensor_copy(abf, ab)
                        dve.drain()
                        for j in range(2):
                            dve.tensor_tensor(oh.rearrange("p t k i -> p (t k) i"), flat(abf[:, j, :, :]).unsqueeze(2).to_broadcast([P, LT * TOPK, TOPK]),
                                              iota16.unsqueeze(1).to_broadcast([P, LT * TOPK, TOPK]), ALU.is_equal)
                            dve.drain()
                            dve.tensor_tensor(oh, oh, iif[:, :, j, :].unsqueeze(2).to_broadcast([P, LT, TOPK, TOPK]), ALU.mult)
                            dve.drain()
                            dve.tensor_reduce(sel[:, j, :, :], oh, AX.X, ALU.add)
                            dve.drain()
                        dve.scalar_tensor_tensor(ef, sel[:, 0, :, :], float(NKEYS), sel[:, 1, :, :], ALU.mult, ALU.add)
                        dve.wait_ge(s_gex, m + 1)
                        dve.tensor_reduce(gs, gx, AX.X, ALU.add)
                        dve.drain()
                        dve.reciprocal(gs, gs)
                        dve.tensor_copy(eview[:, :, bass.ds(m, 1), :].rearrange("p t m k -> p t (m k)"), ef[:, DT:LT, :])
                        dve.drain()
                        dve.wait_ge(s_added, m + 1)
                        dve.scalar_tensor_tensor(didx, ef[:, 0:DT, :], float(DTOK), tokid.unsqueeze(2).to_broadcast([P, DT, TOPK]), ALU.mult, ALU.add)
                        dve.tensor_tensor(gview[:, :, bass.ds(m, 1), :].rearrange("p t m k -> p t (m k)"), gx[:, DT:LT, :],
                                          gs[:, DT:LT].unsqueeze(2).to_broadcast([P, LT - DT, TOPK]), ALU.mult)
                        dve.tensor_tensor(dgate, gx[:, 0:DT, :], gs[:, 0:DT].unsqueeze(2).to_broadcast([P, DT, TOPK]), ALU.mult)
                        dve.drain().then_inc(s_dense, 1)

        b4 = ExitStack()
        s_u = [sem(f"u_rows{i}") for i in range(GROUP)]
        s_v = [sem(f"v_rows{i}") for i in range(2)]
        s_idx = sem("indices_staged")
        s_udone, s_vdone = sem("u_rows_used"), sem("v_rows_used")
        s_act, s_dgelu = sem("dots_done"), sem("dots_gelu")
        s_ut = [sem("ut_block_loaded0"), sem("ut_block_loaded1")]
        s_vb = [sem("v_block_loaded0"), sem("v_block_loaded1")]
        s_gb = [sem("gate_block_loaded0"), sem("gate_block_loaded1")]
        s_pa, s_po = sem("dense_dots"), sem("dense_outputs")
        s_ge, s_m, s_add = sem("dense_gelu"), sem("dense_gated"), sem("dense_added")
        s_gdone = sem("sums_done")
        s_ln4 = sem("ln2_loaded")
        s_stat4, s_std4 = sem("ln2_stats"), sem("ln2_std")
        s_y, s_out = sem("rows_finished"), sem("rows_stored")
        h2Td = mixT[:].rearrange("p k t -> p (k t)")[:, 0:KT * DTOK].rearrange("p (k t) -> p k t", k=KT)
        with b4:
            Ub = sb("Ub", [P, GROUP, D], ctx=b4)
            Vb = lng
            UT = sb("UT", [P, 2, KT, P], ctx=b4)
            VB = sb("VB", [P, 2, D], ctx=b4)
            GB = sb("GB", [P, 2, 2, DTOK], ctx=b4)
            gl = sb("gl", [P, 2, 2, DTOK], ctx=b4)
            AT = sb("AT", [P, 2, 2, DTOK], ctx=b4)
            accx = sb("accx", [P, D], ctx=b4)
            stage = sb("stage", [P, 2, GROUP], u32, ctx=b4)
            dots = sb("dots", [P, GROUP], ctx=b4)
            coef = sb("coef", [P, GROUP], ctx=b4)
            dacc = [vecs[:, 2, :], accx[:]]
            NOUT = DT * OUT_CHUNKS

            with nc.Block() as block:
                @block.sync
                def _(sp):
                    gd = gates_dram.rearrange("(n b p) t -> p n b t", b=2, p=P)
                    vd = peer_v.rearrange("(n b p) d -> p n b d", b=2, p=P)

                    def u_block(n, j):
                        sp.dma_start(UT[:, j, :, :], peer_ut[2 * n + j]).then_inc(s_ut[j], 16)

                    def v_block(n, j):
                        sp.dma_start(VB[:, j, :], vd[:, bass.ds(n, 1), j, :]).then_inc(s_vb[j], 16)

                    def g_block(n, i):
                        sp.dma_start(GB[:, i, :, :], gd[:, bass.ds(n, 1), :, :].rearrange("p a b t -> p (a b) t")).then_inc(s_gb[i], 16)

                    def turn(n, i):
                        for j in range(2):
                            sp.wait_ge(s_pa, 2 * n + j + 1)
                            u_block(n + 1, j)
                        sp.wait_ge(s_m, n + 2)
                        g_block(n + 1, 1 - i)
                        sp.wait_ge(s_po, NOUT * n)
                        v_block(n, 0); v_block(n, 1)

                    u_block(0, 0); u_block(0, 1); g_block(0, 0); v_block(0, 0); v_block(0, 1)
                    for j in range(2):
                        sp.wait_ge(s_pa, j + 1)
                        u_block(1, j)
                    g_block(1, 1)
                    with sp.Fori(0, (NG - 2) // 2) as r:
                        turn(2 * r + 1, 1)
                        turn(2 * r + 2, 0)
                    sp.wait_ge(s_po, NOUT * (NG - 1))
                    v_block(NG - 1, 0); v_block(NG - 1, 1)
                    sp.wait_ge(s_gdone, 1)
                    for i in range(2):
                        sp.dma_start(lng[:, i, :], lnv[2 + i:3 + i, :].partition_broadcast(P)).then_inc(s_ln4, 16)
                    for t in range(LT):
                        sp.wait_ge(s_y, t + 1)
                        sp.dma_start(out[t * P:(t + 1) * P, :], x1[:, t, :]).then_inc(s_out, 16)
                    sp.wait_ge(s_out, 16 * LT)

                @block.gpsimd
                def _(pool):
                    def rows(table, buf, slot, ready, par, e):
                        pool.indirect_dma_start(out=buf[:, slot, :], out_offset=None, in_=table,
                                                in_offset=bass.IndirectOffsetOnAxis(ap=stage[:, par, e:e + 1], axis=0)).then_inc(ready[slot], 16)

                    def u_rows(n, par, e):
                        pool.wait_ge(s_udone, 4 * n + e + 1)
                        pool.sem_inc(s_passed)
                        rows(peer_u, Ub, e, s_u, par, e)

                    def v_rows(n, par, e):
                        pool.wait_ge(s_vdone, 4 * n + e + 1)
                        pool.sem_inc(s_passed)
                        rows(peer_v, Vb, e % 2, s_v, par, e)

                    def stage_in(n, par):
                        pool.tensor_copy(stage[:, par, :], eidx[:, bass.ds(n, 1), :].rearrange("p a b -> p (a b)")).then_inc(s_idx, 1)
                        pool.wait_ge(s_idx, n + 1)
                        pool.sem_inc(s_passed)

                    def turn(n, i, more):
                        v_rows(n, i, 0); v_rows(n, i, 1)
                        if more:
                            stage_in(n + 1, 1 - i)
                            u_rows(n + 1, 1 - i, 0); u_rows(n + 1, 1 - i, 1)
                        v_rows(n, i, 2); v_rows(n, i, 3)
                        if more:
                            u_rows(n + 1, 1 - i, 2); u_rows(n + 1, 1 - i, 3)

                    stage_in(0, 0)
                    for e in range(GROUP):
                        u_rows(0, 0, e)
                    with pool.Fori(0, NG // 2 - 1) as r:
                        turn(2 * r, 0, True)
                        turn(2 * r + 1, 1, True)
                    turn(NG - 2, 0, True)
                    turn(NG - 1, 1, False)

                @block.tensor
                def _(pe):
                    def dense_dots(n, i):
                        pe.wait_ge(s_ge, n + 1)
                        for j in range(2):
                            pe.wait_ge(s_ut[j], 16 * n + 16)
                            for k in range(KT):
                                last = pe.matmul(PS[:, i, j * DTOK:(j + 1) * DTOK], UT[:, j, k, :], h2Td[:, k, :], start=(k == 0), stop=(k == KT - 1))
                            last.then_inc(s_pa, 1)

                    def dense_out(n, i):
                        pe.wait_ge(s_m, n + 3)
                        for j in range(2):
                            pe.wait_ge(s_vb[j], 16 * n + 16)
                        for o in range(NOUT):
                            t, c = o // OUT_CHUNKS, o % OUT_CHUNKS
                            pe.wait_ge(s_add, NOUT * n + o + 1)
                            for j in range(2):
                                last = pe.matmul(PS[:, 2 + o % 4, :], AT[:, i, j, t * P:(t + 1) * P], VB[:, j, c * CHUNK:(c + 1) * CHUNK],
                                                 start=(j == 0), stop=(j == 1))
                            last.then_inc(s_po, 1)

                    dense_dots(0, 0)
                    with pe.Fori(0, NG // 2 - 1) as r:
                        dense_dots(2 * r + 1, 1); dense_out(2 * r, 0)
                        dense_dots(2 * r + 2, 0); dense_out(2 * r + 1, 1)
                    dense_dots(NG - 1, 1); dense_out(NG - 2, 0); dense_out(NG - 1, 1)

                @block.scalar
                def _(act):
                    with act.Fori(0, NG // 2) as r:
                        for i in range(2):
                            n = 2 * r + i
                            act.wait_ge(s_pa, 2 * n + 2)
                            act.wait_ge(s_m, n + 1)
                            act.activation(gl[:, i, :, :].rearrange("p j t -> p (j t)"), PS[:, i, :], ACT.Gelu).then_inc(s_ge, 1)
                            act.wait_ge(s_act, n + 1)
                            act.activation(dots[:], dots[:], ACT.Gelu).then_inc(s_dgelu, 1)
                    for t in range(LT):
                        act.wait_ge(s_stat4, t + 1)
                        act.activation(rsd[:], rsd[:], ACT.Sqrt).then_inc(s_std4, 1)

                @block.vector
                def _(dve):
                    for s, credits in ((s_udone, 4), (s_vdone, 2), (s_ge, 2), (s_m, 2), (s_add, 4)):
                        for _ in range(credits):
                            dve.drain().then_inc(s, 1)
                    for v in (vecs[:, 0, :], vecs[:, 1, :], vecs[:, 2, :], accx[:]):
                        dve.memset(v, 0.0)
                    dve.drain()

                    def add(n, o):
                        t, c = o // OUT_CHUNKS, o % OUT_CHUNKS
                        part = dacc[t][:, c * CHUNK:(c + 1) * CHUNK]
                        dve.wait_ge(s_po, NOUT * n + o + 1)
                        dve.tensor_tensor(part, PS[:, 2 + o % 4, :], part, ALU.add).then_inc(s_add, 1)

                    with dve.Fori(0, LT - DT) as t:
                        acc = vecs[:, bass.ds(t, 1), :].rearrange("p a d -> p (a d)")
                        cur = h2[:, bass.ds(t + DT, 1), :].rearrange("p a d -> p (a d)")
                        with dve.Fori(0, NEXP // GROUP // 2) as r:
                            for i in range(2):
                                n = t * (NEXP // GROUP) + 2 * r + i
                                dve.wait_ge(s_ge, n + 3)
                                dve.wait_ge(s_gb[i], 16 * (t * (NEXP // GROUP // 2) + r) + 16)
                                dve.tensor_tensor(AT[:, i, :, :], gl[:, i, :, :], GB[:, i, :, :], ALU.mult).then_inc(s_m, 1)
                                for e in range(GROUP):
                                    dve.wait_ge(s_u[e], 16 * n + 16)
                                    dve.scalar_tensor_tensor(Ub[:, e, :], Ub[:, e, :], 1.0, cur, ALU.mult, ALU.mult,
                                                             accum_out=dots[:, e:e + 1]).then_inc(s_udone, 1)
                                dve.drain().then_inc(s_act, 1)
                                dve.wait_ge(s_dgelu, n + 1)
                                dve.tensor_tensor(coef[:], dots[:], gate[:, bass.ds(n, 1), :].rearrange("p a b -> p (a b)"), ALU.mult)
                                for e in range(GROUP):
                                    dve.drain()
                                    dve.wait_ge(s_v[e % 2], 16 * (2 * n + e // 2) + 16)
                                    dve.scalar_tensor_tensor(acc, Vb[:, e % 2, :], coef[:, e:e + 1], acc, ALU.mult, ALU.add).then_inc(s_vdone, 1)
                                    add(n, 2 * e); add(n, 2 * e + 1)
                                dve.drain()
                    dve.drain().then_inc(s_gdone, 1)
                    dve.wait_ge(s_ln4, 32)
                    sums = dacc + [vecs[:, 0, :], vecs[:, 1, :]]
                    for t in range(LT):
                        dve.tensor_tensor(sums[t], sums[t], vecs[:, 3, :], ALU.mult)
                        dve.drain()
                        dve.scalar_tensor_tensor(x1[:, t, :], x1[:, t, :], ALPHA, sums[t], ALU.mult, ALU.add)
                        dve.drain()
                        layer_norm(dve, x1[:, t, :], s_stat4, s_std4, t + 1).then_inc(s_y, 1)


def constants():
    turn = np.zeros((P, P), np.float32)
    nf = HALF // 4
    for m in range(P):
        if m % (2 * nf) < nf:
            turn[m + nf, m] = -1.0
        else:
            turn[m - nf, m] = 1.0
    iota = np.tile(np.arange(TOPK, dtype=np.float32), (P, 1))
    inv = (np.float32(10000.0) ** (-np.arange(nf, dtype=np.float32) / np.float32(nf))).astype(np.float32)
    tok = np.arange(SEQ)
    pos = np.stack([tok // GRID_W, tok % GRID_W]).astype(np.float32)
    f = np.arange(P)
    ang = pos[(f % HALF) // (HALF // 2)] * inv[f % nf][:, None]
    rope = np.concatenate([np.cos(ang), np.sin(ang)], 1).astype(np.float32)
    token = (np.arange(P)[:, None] + P * np.arange(DT)[None, :]).astype(np.float32)
    return np.concatenate([np.eye(P, dtype=np.float32), turn, iota, token], 1), rope


def kernel(x, c, ctx, c_ctx, w_ada, b_ada, w_in, conv_w, conv_b, gate_b, diff_lambda, diff_norm_g,
           mlstm_norm_g, w_out, ln1_g, ln1_b, ln2_g, ln2_b, peer_wq, peer_keys, peer_u, peer_v):
    import concourse.bacc as bacc
    from concourse.bass_utils import run_bass_kernel_spmd

    con = np.ascontiguousarray
    w_in = np.asarray(w_in)[0]
    b_ada = np.asarray(b_ada)[0]
    w = w_in[:, :7 * H * HD].reshape(2, 8, P, 7, H, HD)[:, :, :, [3, 4, 5, 6, 0, 1, 2]]
    consts, rope = constants()
    arrays = {
        "xT": con(np.asarray(x)[0].T), "x": con(np.asarray(x)[0]), "cxT": con(np.asarray(ctx)[0].T),
        "ccol": con(np.concatenate([np.asarray(c)[0].reshape(KT, P).T, np.asarray(c_ctx).reshape(KT, P).T], 1)),
        "wada": con(np.asarray(w_ada)[0]), "bcol": con(b_ada[:2 * D].reshape(2 * KT, P).T), "brow": con(b_ada[2 * D:].reshape(4, D)),
        "wseq": con(w.transpose(4, 3, 0, 2, 1, 5).reshape(HALVES, P, 8, P)),
        "wgate": con(w_in[:, 7 * H * HD:]), "gbias": con(np.asarray(gate_b)[0].reshape(NGATES * H, 1)),
        "convw": con(np.asarray(conv_w)[0].reshape(CONV, 2 * H, HD).transpose(2, 1, 0).reshape(P, 2 * H * CONV)),
        "convb": con(np.asarray(conv_b)[0].reshape(2 * H, HD).T),
        "lamv": con(np.asarray(diff_lambda)[0].reshape(1, 4 * HALF)),
        "gcol": con(np.stack([np.asarray(diff_norm_g)[0], np.asarray(mlstm_norm_g)[0]], 1)),
        "wout": con(np.asarray(w_out)[0]),
        "lnv": con(np.stack([np.asarray(a)[0] for a in (ln1_g, ln1_b, ln2_g, ln2_b)])),
        "wq": con(np.asarray(peer_wq)[0].reshape(KT, P, 2 * PH, P).transpose(2, 1, 0, 3)),
        "keysT": con(np.asarray(peer_keys)[0].transpose(3, 1, 0, 2).reshape(P, 2 * PH * NKEYS)),
        "peer_u": con(np.asarray(peer_u)[0]), "peer_v": con(np.asarray(peer_v)[0]),
        "peer_ut": con(np.asarray(peer_u)[0].reshape(NEB, P, KT, P).transpose(0, 3, 2, 1)),
        "consts": consts, "rope": rope,
    }
    nc = bacc.Bacc("TRN2", target_bir_lowering=False, num_devices=1)
    aps = {n: nc.dram_tensor(n, a.shape, mybir.dt.from_np(a.dtype), kind="ExternalInput").ap() for n, a in arrays.items()}
    aps["out"] = nc.dram_tensor("out", (SEQ, D), mybir.dt.float32, kind="ExternalOutput").ap()
    program(nc, **aps)
    r = run_bass_kernel_spmd(nc, [arrays], core_ids=[0])
    return r.results[0]["out"].reshape(1, SEQ, D)
```

```python
import numpy as np
from contextlib import ExitStack

import concourse.bass as bass
from concourse import mybir

P = 128
D = 2048
KT = D // P
SEQ, CTX = 512, 256
T = SEQ + CTX
LT, CT = SEQ // P, CTX // P
H = 8
HD = 128
HALF = 64
NGATES = 4
CONV = 5
PAD = CONV // 2
GRID_W = 64
TOPK = 16
NKEYS = 128
PH = 8
NEXP = PH * TOPK
G2C = D // PH
ALPHA = 2.0 ** 0.25
LAM_INIT = 0.2
LN_EPS, RMS_EPS = 1e-5, 1e-6
CHUNK = 512
SH_CHUNKS = 2 * D // CHUNK
OUK = 2
OUNITS = KT // OUK
REST_CHUNKS = 3 * D // CHUNK
OUT_CHUNKS = D // CHUNK
NPROJ = 7
QK = KT // 4
WBUF = 4
QUARTERS = H * NPROJ * 4
ZPIECES = 48
NEG = -3.0e38
DT = 3
DTOK = DT * P
NEB = NKEYS * NKEYS // P
GROUP = 2
NG = NEB // GROUP
assert (LT - DT) * NEXP == NG * GROUP


def program(nc, xT, x, cxT, ccol, wada, bcol, brow, wseq, wgate, gbias, convw, convb, lamv, gcol,
            wout, lnv, wq, keysT, peer_u, peer_v, peer_ut, consts, rope, out):
    f32, f32r, u32 = mybir.dt.float32, mybir.dt.float32r, mybir.dt.uint32
    ALU, ACT, AX = mybir.AluOpType, mybir.ActivationFunctionType, mybir.AxisListType
    with ExitStack() as top:
        def sb(name, shape, dt=f32, ctx=top):
            return ctx.enter_context(nc.sbuf_tensor(name, shape, dt))

        at = {}

        def sb_at(name, shape, dt=f32, ctx=top):
            at[name] = -(-nc.sbuf_base // 32) * 32
            return sb(name, shape, dt, ctx)

        def over(name, under, shape, dt=f32, skip=0):
            return nc.alloc_sbuf_tensor_at(name, shape, dt, offset=at[under] + skip)

        def sem(name):
            return top.enter_context(nc.semaphore(name))

        PS = top.enter_context(nc.psum_tensor("PS", [P, 8, 512], f32))
        cst = sb("cst", [P, 272 + DT])
        ident, rotm, iota16 = cst[:, 0:128], cst[:, 128:256], cst[:, 256:272]
        tokid = cst[:, 272:272 + DT]
        gates_dram = nc.dram_tensor("gates_dram", (NKEYS * NKEYS, DTOK), f32, kind="Internal").ap()
        s_passed = sem("gpsimd_waits_passed")
        silc = sb("silc", [P, 2, KT])
        neglam = sb("neglam", [P, 1])
        gains = sb("gains", [P, 2])
        mix_dram = nc.dram_tensor("mix_dram", (D, SEQ), f32, kind="Internal").ap()

        phase_a = ExitStack()
        hH = sb_at("hH", [P, KT, T], f32r, ctx=phase_a)
        hL = sb("hL", [P, KT, T], f32r, ctx=phase_a)
        colv = sb("colv", [P, 20, H], ctx=phase_a)
        m0b = sb("m0b", [P, 2, H], ctx=phase_a)
        Mrow = sb("Mrow", [H, 2, SEQ], ctx=phase_a)

        s_small = sem("small_loaded")
        s_x = sem("inputs_loaded")
        s_wa = [sem("ada_loaded0"), sem("ada_loaded1")]
        s_sil = sem("silu_done")
        s_silrep = sem("silu_spread")
        s_ada_pe = sem("ada_summed")
        s_ada_ev = sem("ada_row_kept")
        s_modT = sem("mod_turned")
        s_mod = sem("inputs_modulated")
        s_gate_pe = sem("gates_summed")
        s_gate_ev = sem("gates_kept")
        s_gate_st, s_gate_mv = sem("gates_stored"), sem("gates_moved")
        gts_dram = nc.dram_tensor("gts_dram", (NGATES * H, T), f32, kind="Internal").ap()
        s_abs = sem("gate_abs")
        s_lf1 = sem("log1p_done")
        s_scan = sem("scans_done")
        s_ex = sem("gate_exps")
        s_dm = sem("state_max_spread_ready")
        s_col = sem("columns_turned")
        s_lamd = sem("lambda_dots")
        s_lame = sem("lambda_exps")

        b1 = ExitStack()
        wr = over("wr", "hH", [P, 2, KT, CHUNK])
        silA = over("silA", "hH", [P, KT, P], skip=2 * KT * CHUNK * 4)
        R = over("R", "hH", [P, SH_CHUNKS * CHUNK], skip=2 * KT * CHUNK * 4 + KT * P * 4)
        s_hh = sem("inputs_high")
        with b1:
            hT = sb("hT", [P, KT, T], ctx=b1)
            cc = sb("cc", [P, 2, KT], ctx=b1)
            bc = sb("bc", [P, 2 * KT], ctx=b1)
            mods = sb("mods", [P, 2 * KT, 2], ctx=b1)
            wg = sb("wg", [P, KT, NGATES * H], ctx=b1)
            gb = sb("gb", [NGATES * H, 1], ctx=b1)
            gts = sb("gts", [NGATES * H, T], ctx=b1)
            lam4 = sb("lam4", [P, 4, HALF], ctx=b1)
            lamp = sb("lamp", [P, 2, HALF], ctx=b1)
            lamd = sb("lamd", [P, 2], ctx=b1)
            lame = sb("lame", [P, 2], ctx=b1)

            with nc.Block() as block:
                @block.sync
                def _(sp):
                    sp.dma_start(cc[:].rearrange("p a k -> p (a k)"), ccol).then_inc(s_small, 16)
                    sp.dma_start(cst[:], consts).then_inc(s_small, 16)
                    sp.dma_start(bc[:], bcol).then_inc(s_small, 16)
                    sp.dma_start(gb[:], gbias).then_inc(s_small, 16)
                    sp.dma_start(gains[:], gcol).then_inc(s_small, 16)
                    sp.dma_start(lam4[:].rearrange("p a d -> p (a d)"), lamv.partition_broadcast(P)).then_inc(s_small, 16)
                    sp.dma_start(wg[:], wgate.rearrange("(k p) g -> p k g", p=P)).then_inc(s_small, 16)
                    wv = wada.rearrange("(k p) n -> p k n", p=P)
                    sp.dma_start(wr[:, 0, :, :], wv[:, :, 0:CHUNK]).then_inc(s_wa[0], 16)
                    sp.dma_start(wr[:, 1, :, :], wv[:, :, CHUNK:2 * CHUNK]).then_inc(s_wa[1], 16)
                    sp.dma_start(hT[:, :, 0:SEQ], xT.rearrange("(k p) t -> p k t", p=P)).then_inc(s_x, 16)
                    sp.dma_start(hT[:, :, SEQ:T], cxT.rearrange("(k p) t -> p k t", p=P)).then_inc(s_x, 16)
                    wv4 = wada.rearrange("(k p) (n c) -> p k n c", p=P, c=CHUNK)
                    with sp.Fori(1, SH_CHUNKS // 2) as n:
                        for j in range(2):
                            sp.wait_ge(s_ada_pe, 2 * n + j - 1)
                            sp.dma_start(wr[:, j, :, :], wv4[:, :, 2 * n + j, :]).then_inc(s_wa[j], 16)
                    sp.wait_ge(s_gate_ev, 1)
                    sp.dma_start(gts_dram, gts[:]).then_inc(s_gate_st, 16)
                    sp.wait_ge(s_gate_st, 16)

                @block.scalar
                def _(act):
                    act.wait_ge(s_small, 16 * 7)
                    act.activation(silc[:], cc[:], ACT.Silu).then_inc(s_sil, 1)
                    with act.Fori(0, SH_CHUNKS // 2) as n:
                        for j in range(2):
                            act.wait_ge(s_ada_pe, 2 * n + j + 1)
                            act.activation(R[:, bass.ds((2 * n + j) * CHUNK, CHUNK)], PS[:, j, :], ACT.Copy).then_inc(s_ada_ev, 1)
                    act.wait_ge(s_lamd, 1)
                    act.activation(lame[:], lamd[:], ACT.Exp).then_inc(s_lame, 1)
                    for q in range(4):
                        ks = slice(q * QK, (q + 1) * QK)
                        act.wait_ge(s_mod, q + 1)
                        act.activation(hH[:, ks, :], hT[:, ks, :], ACT.Copy).then_inc(s_hh, 1)

                @block.tensor
                def _(pe):
                    pe.wait_ge(s_silrep, 1)
                    with pe.Fori(0, SH_CHUNKS // 2) as n:
                        for j in range(2):
                            pe.wait_ge(s_wa[j], 16 * n + 16)
                            pe.wait_ge(s_ada_ev, 2 * n + j + 1)
                            for k in range(KT):
                                last = pe.matmul(PS[:, j, :], silA[:, k, :], wr[:, j, k, :], start=(k == 0), stop=(k == KT - 1))
                            last.then_inc(s_ada_pe, 1)
                    pe.wait_ge(s_ada_ev, SH_CHUNKS + 2)
                    for j in range(2 * KT):
                        last = pe.matmul(PS[:, 2, 2 * j:2 * j + 2], R[:, j * P:(j + 1) * P], ident[:, 0:65:64], start=True, stop=True)
                    last.then_inc(s_modT, 1)
                    for k in range(KT):
                        if k % 4 == 0:
                            pe.wait_ge(s_mod, k // 4 + 1)
                        pe.matmul(PS[0:32, 3, :], wg[:, k, :], hT[:, k, 0:SEQ], start=(k == 0), stop=(k == KT - 1))
                        last = pe.matmul(PS[0:32, 4, 0:CTX], wg[:, k, :], hT[:, k, SEQ:T], start=(k == 0), stop=(k == KT - 1))
                    last.then_inc(s_gate_pe, 1)

                @block.gpsimd
                def _(pool):
                    for q in range(4):
                        ks = slice(q * QK, (q + 1) * QK)
                        pool.wait_ge(s_hh, q + 1)
                        pool.tensor_tensor(hL[:, ks, :], hT[:, ks, :], hH[:, ks, :].bitcast(f32), ALU.subtract)

                @block.vector
                def _(dve):
                    for _ in range(2):
                        dve.drain().then_inc(s_ada_ev, 1)
                    dve.wait_ge(s_sil, 1)
                    for a in range(2):
                        last = dve.tensor_copy(silA[:, :, 64 * a:64 * a + 64], silc[:, a, :].unsqueeze(2).to_broadcast([P, KT, 64]))
                    last.then_inc(s_silrep, 1)
                    dve.tensor_tensor(lamp[:], lam4[:, 0:4:2, :], lam4[:, 1:4:2, :], ALU.mult)
                    dve.drain()
                    dve.tensor_reduce(lamd[:], lamp[:], AX.X, ALU.add).then_inc(s_lamd, 1)
                    dve.wait_ge(s_lame, 1)
                    dve.tensor_tensor(neglam[:], lame[:, 1:2], lame[:, 0:1], ALU.subtract)
                    dve.tensor_scalar(gains[:, 0:1], gains[:, 0:1], 1.0 - LAM_INIT, None, ALU.mult)
                    dve.drain()
                    dve.tensor_scalar(neglam[:], neglam[:], -LAM_INIT, None, ALU.add)
                    dve.wait_ge(s_modT, 1)
                    dve.tensor_tensor(mods[:], PS[:, 2, 0:4 * KT].rearrange("p (k a) -> p k a", a=2),
                                      bc[:].unsqueeze(2).to_broadcast([P, 2 * KT, 2]), ALU.add)
                    dve.drain()
                    dve.tensor_scalar(mods[:, KT:2 * KT, :], mods[:, KT:2 * KT, :], 1.0, None, ALU.add)
                    dve.drain()
                    dve.wait_ge(s_x, 32)
                    for k in range(KT):
                        for a, (t0, t1) in enumerate(((0, SEQ), (SEQ, T))):
                            last = dve.tensor_scalar(hT[:, k, t0:t1], hT[:, k, t0:t1], mods[:, KT + k, a:a + 1],
                                                     mods[:, k, a:a + 1], ALU.mult, ALU.add)
                        if k % 4 == 3:
                            last.then_inc(s_mod, 1)
                    dve.wait_ge(s_gate_pe, 1)
                    dve.tensor_scalar(gts[:, 0:SEQ], PS[0:32, 3, :], gb[:, 0:1], None, ALU.add)
                    dve.tensor_scalar(gts[:, SEQ:T], PS[0:32, 4, 0:CTX], gb[:, 0:1], None, ALU.add).then_inc(s_gate_ev, 1)

        w_loaded = [sem(f"proj_weights_loaded{i}") for i in range(WBUF)]
        s_tab = sem("tables_loaded")
        pe_qtr, act_evac, pool_w = sem("proj_quarters_summed"), sem("proj_kept"), sem("proj_weights_split")
        ml_stored, at_stored = sem("ml_out_stored"), sem("at_out_stored")
        dve_conv, act_silu = sem("conv_done"), sem("conv_silu_done")
        pe_m1, act_m1, dve_m1 = sem("ml_v_turned"), sem("ml_v_kept"), sem("ml_ctx_keys_weighted")
        pe_m2, act_g, act_d = sem("ml_state_and_max_summed"), sem("ml_state_decay"), sem("ml_decay")
        pool_d, pe_st, dve_sd = sem("ml_decay_masked"), sem("ml_scores"), sem("ml_scores_decayed")
        dve_qg, pe_n, dve_n = sem("ml_queries_decayed"), sem("ml_sums"), sem("ml_divided")
        dve_ss, act_rs, dve_hn = sem("ml_squares"), sem("ml_rms"), sem("ml_normed")
        pe_m5, dve_mlout = sem("ml_out_turned"), sem("ml_out_kept")
        pe_rot, act_v = sem("rotated"), sem("values_kept")
        dve_rope, pe_s, dve_max = sem("rope_done"), sem("scores"), sem("scores_max")
        act_exp, dve_w, pe_t = sem("scores_exp"), sem("weights"), sem("weights_turned")
        act_wt, pe_p, dve_pn = sem("weights_kept"), sem("values_summed"), sem("attention_kept")
        dve_as, act_as, dve_an = sem("at_squares"), sem("at_rms"), sem("at_normed")
        pe_o, dve_dout = sem("at_out_turned"), sem("at_out_kept")
        s_zero, s_zeroed = sem("zeros_ready"), sem("dense_gates_cleared")

        ring = over("ring", "hH", [P, 2, KT, CHUNK])
        s_wb = [sem("chunk_loaded0"), sem("chunk_loaded1")]
        with phase_a:
            WR = sb_at("WR", [P, WBUF, QK, P], ctx=phase_a)
            WL = over("WL", "WR", [P, WBUF, QK, P], f32r)
            WH = sb("WH", [P, WBUF, QK, P], f32r, ctx=phase_a)
            zeros = sb("zeros", [P, 256], ctx=phase_a)
            mst = sb("mst", [P, 2, SEQ], ctx=phase_a)
            rp = sb("rp", [P, 2, SEQ], ctx=phase_a)
            cw = sb("cw", [P, 2 * H, CONV], ctx=phase_a)
            cb = sb("cb", [P, 2 * H], ctx=phase_a)
            rawq = sb("rawq", [P, SEQ + 2 * PAD], ctx=phase_a)
            rawk = sb("rawk", [P, SEQ + 2 * PAD], ctx=phase_a)
            rawc = sb("rawc", [P, CTX + 2 * PAD], ctx=phase_a)
            mq = sb("mq", [P, SEQ], ctx=phase_a)
            mk = sb("mk", [P, T], ctx=phase_a)
            mvT = sb("mvT", [P, T], ctx=phase_a)
            sig = sb("sig", [P, SEQ], ctx=phase_a)
            vaug = sb("vaug", [P, LT + CT, HD + 2], ctx=phase_a)
            kw = sb("kw", [P, 2, CT, HD], ctx=phase_a)
            onesH = sb("onesH", [H, P], ctx=phase_a)
            C0 = sb("C0", [P, 2, HD + 1], ctx=phase_a)
            Mh = sb("Mh", [H, 2, SEQ], ctx=phase_a)
            G = sb_at("G", [P, 2, SEQ], ctx=phase_a)
            DM = sb("DM", [P, 2, 2, SEQ], ctx=phase_a)
            SD = sb("SD", [P, 2, LT, SEQ], ctx=phase_a)
            gI = over("gI", "G", [H, 2, T])
            gF = over("gF", "G", [H, 2, T], skip=8 * T)
            gA = over("gA", "G", [H, 2, T], skip=16 * T)
            gE = over("gE", "G", [H, 2, T], skip=24 * T)
            ones8 = over("ones8", "G", [H, T], skip=32 * T)
            m0 = over("m0", "G", [H, 2], skip=36 * T)
            mc = over("mc", "G", [H, 2], skip=36 * T + 32)
            dm0 = over("dm0", "G", [H, 2, H], skip=36 * T + 64)
            den = sb("den", [P, 2], ctx=phase_a)
            hf = sb("hf", [P, HD], ctx=phase_a)
            hn = sb("hn", [P, LT, HD], ctx=phase_a)
            sqd = sb("sqd", [P, HD], ctx=phase_a)
            ss = sb("ss", [P, 2, LT], ctx=phase_a)
            rawdq = sb("rawdq", [P, SEQ], ctx=phase_a)
            rawdk = sb("rawdk", [P, SEQ], ctx=phase_a)
            qz = sb("qz", [P, 2, SEQ], ctx=phase_a)
            kk = sb("kk", [P, T], ctx=phase_a)
            dvT = mvT
            V = sb("V", [P, LT + CT, HD], ctx=phase_a)
            dmflat = DM[:].rearrange("p a b t -> p (a b t)")
            E = dmflat[:, 0:2 * T].rearrange("p (a t) -> p a t", a=2)
            Wt = sb("Wt", [P, T], ctx=phase_a)
            WT = sb("WT", [P, LT + CT, P], ctx=phase_a)
            tq, tr = E[:, 0, 0:SEQ], E[:, 1, 0:SEQ]
            mx = sb("mx", [P, 4], ctx=phase_a)
            nm = sb("nm", [P, 2], ctx=phase_a)
            Z = sb("Z", [P, 2, 2], ctx=phase_a)
            rz = sb("rz", [P, 2], ctx=phase_a)
            on = sb("on", [P, LT, HD], ctx=phase_a)

            MLK, DFK = ("mq", "mk", "mv", "mo"), ("dq", "dk", "dv")
            HAS_CTX = {"mk", "mv", "dk", "dv"}
            BANK = {"mq": 0, "mk": 1, "mv": 0, "mo": 1, "dq": 0, "dk": 1, "dv": 0}
            TILE = {k: i for i, k in enumerate(MLK + DFK)}
            CTXBANK = 2

            def spans(d, st):
                return (st * P, SEQ) if d == 0 else (0, (st + 1) * P)

            with nc.Block() as block:
                @block.sync
                def _(sp):
                    for g, dst in enumerate((gI[:, 0, :], gF[:, 0, :], gI[:, 1, :], gF[:, 1, :])):
                        sp.dma_start(dst, gts_dram[g * H:(g + 1) * H, :]).then_inc(s_gate_mv, 16)
                    sp.dma_start(rp[:].rearrange("p a t -> p (a t)"), rope).then_inc(s_tab, 16)
                    sp.dma_start(cw[:].rearrange("p a t -> p (a t)"), convw).then_inc(s_tab, 16)
                    sp.dma_start(cb[:], convb).then_inc(s_tab, 16)
                    for b in range(WBUF):
                        sp.dma_start(WR[:, b, :, :], wseq[b]).then_inc(w_loaded[b], 16)
                    def weights(r):
                        for b in range(WBUF):
                            sp.wait_ge(pe_qtr, WBUF * r + b - WBUF + 1)
                            sp.dma_start(WR[:, b, :, :], wseq[WBUF * r + b]).then_inc(w_loaded[b], 16)

                    gz = gates_dram.rearrange("(p a) t -> p (a t)", p=P).rearrange("p (b c d) -> p b c d", b=ZPIECES, d=256)
                    sp.wait_ge(s_zero, 1)
                    with sp.Fori(1, ZPIECES + 1) as r:
                        weights(r)
                        sp.dma_start(gz[:, bass.ds(r - 1, 1), :, :].rearrange("p a c d -> p (a c) d"),
                                     zeros[:].unsqueeze(1).to_broadcast([P, NKEYS * DTOK // (ZPIECES * 256), 256])).then_inc(s_zeroed, 16)
                    with sp.Fori(ZPIECES + 1, QUARTERS // WBUF) as r:
                        weights(r)
                    sp.wait_ge(s_zeroed, 16 * ZPIECES)
                    wv = wada.rearrange("(k p) (n c) -> p k n c", p=P, c=CHUNK)
                    sp.wait_ge(pe_qtr, QUARTERS)
                    for j in range(2):
                        sp.dma_start(ring[:, j, :, :], wv[:, :, SH_CHUNKS + j, :]).then_inc(s_wb[j], 16)

                @block.tensor
                def _(pe):
                    B = lambda i: PS[:, i, :]

                    def half(h, kind, j):
                        tile = TILE[kind]
                        bank = BANK[kind]
                        if j == 0:
                            before = {"mq": 0, "mk": 0, "mv": 1, "mo": 2, "dq": 3, "dk": 4, "dv": 5}[kind]
                            if before or not isinstance(h, int):
                                pe.wait_ge(act_evac, 7 * h + before)
                        for q in (2 * j, 2 * j + 1):
                            pe.wait_ge(pool_w, 4 * NPROJ * h + 4 * tile + q + 1)

                            def product(dst, t0, t1):
                                for k in range(QK):
                                    kk_ = QK * q + k
                                    pe.matmul(dst, WH[:, q, k, :], hH[:, kk_, t0:t1], start=(kk_ == 0), stop=False)
                                    pe.matmul(dst, WH[:, q, k, :], hL[:, kk_, t0:t1], start=False, stop=False)
                                    last = pe.matmul(dst, WL[:, q, k, :], hH[:, kk_, t0:t1], start=False, stop=(kk_ == KT - 1))
                                return last

                            last = product(B(bank), 0, SEQ)
                            if kind in HAS_CTX:
                                if q == 0 and kind in ("mv", "dv"):
                                    pe.wait_ge(act_evac, 7 * h + TILE[kind])
                                last = product(PS[:, CTXBANK, 0:CTX], SEQ, T)
                            last.then_inc(pe_qtr, 1)

                    def m1(h):
                        pe.wait_ge(dve_dout, h + 1)
                        pe.wait_ge(act_evac, 7 * h + 3)
                        pe.wait_ge(act_silu, 2 * h + 2)
                        for t in range(LT):
                            pe.transpose(PS[:, 6, t * P:(t + 1) * P], mvT[:, t * P:(t + 1) * P], ident)
                        for t in range(CT):
                            pe.transpose(PS[:, 7, t * P:(t + 1) * P], mvT[:, SEQ + t * P:SEQ + (t + 1) * P], ident)
                            last = pe.transpose(PS[:, 7, (2 + t) * P:(3 + t) * P], mk[:, SEQ + t * P:SEQ + (t + 1) * P], ident)
                        last.then_inc(pe_m1, 1)

                    def m2(h):
                        pe.wait_ge(dve_m1, h + 1)
                        for d in range(2):
                            for t in range(CT):
                                pe.matmul(PS[:, 5, 256 * d:256 * d + HD + 1], kw[:, d, t, :], vaug[:, LT + t, 0:HD + 1],
                                          start=(t == 0), stop=(t == CT - 1))
                        for d in range(2):
                            last = pe.matmul(B(3 + d), onesH[:], Mh[:, d, :], start=True, stop=True)
                        last.then_inc(pe_m2, 1)

                    def st(h, t):
                        if t == 0:
                            pe.wait_ge(act_m1, h + 1)
                        elif t >= 2:
                            pe.wait_ge(dve_sd, 4 * h + t - 1)
                        pe.matmul(B(6 + t % 2), mk[:, t * P:(t + 1) * P], mq[:], start=True, stop=True).then_inc(pe_st, 1)

                    def nsum(h, t):
                        if t == 0:
                            pe.wait_ge(dve_sd, 4 * h + 4)
                            pe.wait_ge(dve_qg, h + 1)
                        elif t == 1:
                            pe.wait_ge(act_d, 4 * h + 4)
                        else:
                            pe.wait_ge(dve_n, 4 * h + t - 1)
                        bank = 5 if t % 2 == 0 else 3
                        for d in range(2):
                            o = PS[:, bank, 256 * d:256 * d + HD + 1]
                            for n, s in enumerate(range(0, t + 1) if d == 0 else range(t, LT)):
                                pe.matmul(o, SD[:, d, s, t * P:(t + 1) * P], vaug[:, s, 0:HD + 1], start=(n == 0), stop=False)
                            last = pe.matmul(o, G[:, d, t * P:(t + 1) * P], C0[:, d, :], start=False, stop=True)
                        last.then_inc(pe_n, 1)

                    def m5(h):
                        pe.wait_ge(dve_hn, h + 1)
                        for t in range(LT):
                            last = pe.transpose(PS[:, 4, t * P:(t + 1) * P], hn[:, t, :], ident)
                        last.then_inc(pe_m5, 1)

                    def rot(h):
                        pe.wait_ge(dve_mlout, h + 1)
                        pe.wait_ge(act_evac, 7 * h + 7)
                        pe.matmul(B(3), rotm, rawdq[:], start=True, stop=True)
                        pe.matmul(B(4), rotm, rawdk[:], start=True, stop=True)
                        for t in range(LT):
                            pe.transpose(PS[:, 6, t * P:(t + 1) * P], dvT[:, t * P:(t + 1) * P], ident)
                        for t in range(CT):
                            last = pe.transpose(PS[:, 7, t * P:(t + 1) * P], dvT[:, SEQ + t * P:SEQ + (t + 1) * P], ident)
                        last.then_inc(pe_rot, 1)

                    def scores(h, q):
                        if q == 0:
                            pe.wait_ge(dve_rope, h + 1)
                        else:
                            pe.wait_ge(act_exp, 4 * h + q)
                        for a in range(2):
                            pe.matmul(B(3 + a), qz[:, a, q * P:(q + 1) * P], kk[:, 0:SEQ], start=True, stop=True)
                            last = pe.matmul(PS[:, 5, a * CTX:(a + 1) * CTX], qz[:, a, q * P:(q + 1) * P], kk[:, SEQ:T], start=True, stop=True)
                        last.then_inc(pe_s, 1)

                    def turn(h, q):
                        pe.wait_ge(dve_w, 4 * h + q + 1)
                        if q == 0:
                            pe.wait_ge(act_v, h + 1)
                        else:
                            pe.wait_ge(dve_pn, 4 * h + q)
                        for t in range(LT + CT):
                            last = pe.transpose(PS[:, 6 + t // 4, (t % 4) * P:(t % 4 + 1) * P], Wt[:, t * P:(t + 1) * P], ident)
                        last.then_inc(pe_t, 1)

                    def pv(h, q):
                        pe.wait_ge(act_wt, 4 * h + q + 1)
                        for t in range(LT + CT):
                            last = pe.matmul(PS[:, 7, 256:384], WT[:, t, :], V[:, t, :], start=(t == 0), stop=(t == LT + CT - 1))
                        last.then_inc(pe_p, 1)

                    def outT(h):
                        pe.wait_ge(dve_an, h + 1)
                        for t in range(LT):
                            last = pe.transpose(PS[:, 6, t * P:(t + 1) * P], on[:, t, :], ident)
                        last.then_inc(pe_o, 1)

                    def stage_a(h):
                        half(h, "dq", 0); m1(h); half(h, "dq", 1); m2(h)
                        half(h, "dk", 0); st(h, 0); st(h, 1); half(h, "dk", 1); st(h, 2); st(h, 3)
                        half(h, "dv", 0); nsum(h, 0); nsum(h, 1); half(h, "dv", 1); nsum(h, 2); nsum(h, 3)
                        m5(h)

                    def stage_b(h, proj):
                        g = h + 1
                        if proj: half(g, "mq", 0)
                        rot(h)
                        if proj: half(g, "mq", 1)
                        scores(h, 0)
                        if proj: half(g, "mk", 0)
                        turn(h, 0); scores(h, 1)
                        if proj: half(g, "mk", 1)
                        pv(h, 0)
                        if proj: half(g, "mv", 0)
                        turn(h, 1); scores(h, 2)
                        if proj: half(g, "mv", 1)
                        pv(h, 1)
                        if proj: half(g, "mo", 0)
                        turn(h, 2); scores(h, 3)
                        if proj: half(g, "mo", 1)
                        pv(h, 2); turn(h, 3); pv(h, 3); outT(h)

                    pe.wait_ge(s_tab, 48 + 1)
                    for kind in MLK:
                        half(0, kind, 0)
                        half(0, kind, 1)
                    pe.wait_ge(s_ex, 1)
                    for d in range(2):
                        for t in range(LT):
                            pe.transpose(PS[:, 5, (d * LT + t) * H:(d * LT + t + 1) * H], gI[:, d, t * P:(t + 1) * P], ident[0:H, 0:H])
                            pe.transpose(PS[:, 5, (8 + d * LT + t) * H:(9 + d * LT + t) * H], gE[:, d, t * P:(t + 1) * P], ident[0:H, 0:H])
                        for t in range(CT):
                            pe.transpose(PS[:, 5, (16 + d * CT + t) * H:(17 + d * CT + t) * H],
                                         gE[:, d, SEQ + t * P:SEQ + (t + 1) * P], ident[0:H, 0:H])
                    pe.wait_ge(s_dm, 1)
                    pe.matmul(PS[:, 6, 0:2 * H], ones8[:, 0:P], dm0[:].rearrange("p a b -> p (a b)"), start=True, stop=True).then_inc(s_col, 1)
                    with pe.Fori(0, H - 1) as h:
                        stage_a(h)
                        stage_b(h, True)
                    stage_a(H - 1)
                    stage_b(H - 1, False)

                @block.scalar
                def _(act):
                    def keep_mq(h):
                        act.wait_ge(pe_qtr, 28 * h + 4)
                        if not (isinstance(h, int) and h == 0):
                            act.wait_ge(dve_mlout, h)
                        else:
                            act.wait_ge(s_tab, 48 + 1)
                        act.activation(rawq[:, PAD:PAD + SEQ], PS[:, 0, :], ACT.Copy).then_inc(act_evac, 1)

                    def keep_mk(h):
                        act.wait_ge(pe_qtr, 28 * h + 8)
                        act.activation(rawk[:, PAD:PAD + SEQ], PS[:, 1, :], ACT.Copy)
                        act.activation(rawc[:, PAD:PAD + CTX], PS[:, 2, 0:CTX], ACT.Copy).then_inc(act_evac, 1)

                    def keep_mv(h):
                        act.wait_ge(pe_qtr, 28 * h + 12)
                        act.activation(mvT[:, 0:SEQ], PS[:, 0, :], ACT.Copy)
                        act.activation(mvT[:, SEQ:T], PS[:, 2, 0:CTX], ACT.Copy).then_inc(act_evac, 1)

                    def keep_mo(h):
                        act.wait_ge(pe_qtr, 28 * h + 16)
                        act.activation(sig[:], PS[:, 1, :], ACT.Sigmoid).then_inc(act_evac, 1)

                    def silu_q(h):
                        act.wait_ge(dve_conv, 2 * h + 1)
                        act.activation(mq[:], mq[:], ACT.Silu).then_inc(act_silu, 1)

                    def silu_k(h):
                        act.wait_ge(dve_conv, 2 * h + 2)
                        act.activation(mk[:], mk[:], ACT.Silu).then_inc(act_silu, 1)

                    def keep_v(h):
                        act.wait_ge(pe_m1, h + 1)
                        act.activation(vaug[:, 0:LT, 0:HD], PS[:, 6, :].rearrange("p (t c) -> p t c", c=HD), ACT.Copy).then_inc(act_m1, 1)

                    def state_decay(h):
                        act.wait_ge(pe_m2, h + 1)
                        act.activation(C0[:], PS[:, 5, :].rearrange("p (d c) -> p d c", d=2)[:, :, 0:HD + 1], ACT.Copy)
                        for d in range(2):
                            last = act.activation(G[:, d, :], PS[:, 3 + d, :], ACT.Exp, scale=-1.0, bias=m0b[:, d, bass.ds(h, 1)])
                        last.then_inc(act_g, 1)

                    def decay(h, t):
                        if t >= 2:
                            act.wait_ge(dve_sd, 4 * h + t - 1)
                        for d in range(2):
                            l0, l1 = spans(d, t)
                            last = act.activation(DM[:, t % 2, d, l0:l1], PS[:, 3 + d, l0:l1], ACT.Exp, scale=-1.0,
                                                  bias=colv[:, d * LT + t, bass.ds(h, 1)])
                        last.then_inc(act_d, 1)

                    def rms(i, ready, n, done):
                        act.wait_ge(ready, n)
                        act.activation(ss[:, i, :], ss[:, i, :], ACT.Ln)
                        act.drain()
                        act.activation(ss[:, i, :], ss[:, i, :], ACT.Exp, scale=-0.5).then_inc(done, 1)

                    def keep_dq(h):
                        act.wait_ge(pe_qtr, 28 * h + 20)
                        act.wait_ge(dve_dout, h + 1)
                        act.activation(rawdq[:], PS[:, 0, :], ACT.Copy).then_inc(act_evac, 1)

                    def keep_dk(h):
                        act.wait_ge(pe_qtr, 28 * h + 24)
                        act.activation(rawdk[:], PS[:, 1, :], ACT.Copy)
                        act.activation(kk[:, SEQ:T], PS[:, 2, 0:CTX], ACT.Copy).then_inc(act_evac, 1)

                    def keep_dv(h):
                        act.wait_ge(pe_qtr, 28 * h + 28)
                        act.activation(dvT[:, 0:SEQ], PS[:, 0, :], ACT.Copy)
                        act.activation(dvT[:, SEQ:T], PS[:, 2, 0:CTX], ACT.Copy).then_inc(act_evac, 1)

                    def keep_values(h):
                        act.wait_ge(pe_rot, h + 1)
                        act.activation(V[:, 0:LT, :], PS[:, 6, :].rearrange("p (t c) -> p t c", c=HD), ACT.Copy)
                        act.activation(V[:, LT:LT + CT, :], PS[:, 7, 0:CTX].rearrange("p (t c) -> p t c", c=HD), ACT.Copy).then_inc(act_v, 1)

                    def store(h, kind, done):
                        act.wait_ge((dve_mlout, dve_dout)[kind], h + 1 + kind)
                        rows = mix_dram.rearrange("(k p) t -> p k t", p=P)[:, bass.ds(h + H * (1 - kind), 1), :]
                        act.dma_start(rows, mst[:, kind:kind + 1, :]).then_inc(done, 16)

                    def exps(h, q):
                        act.wait_ge(dve_max, 4 * h + q + 1)
                        for a in range(2):
                            act.activation(E[:, a, 0:SEQ], PS[:, 3 + a, :], ACT.Exp, scale=HALF ** -0.5, bias=nm[:, a:a + 1],
                                           accum_out=Z[:, 0, a:a + 1])
                            last = act.activation(E[:, a, SEQ:T], PS[:, 5, a * CTX:(a + 1) * CTX], ACT.Exp, scale=HALF ** -0.5,
                                                  bias=nm[:, a:a + 1], accum_out=Z[:, 1, a:a + 1])
                        last.then_inc(act_exp, 1)

                    def keep_wt(h, q):
                        act.wait_ge(pe_t, 4 * h + q + 1)
                        act.activation(WT[:].rearrange("p t c -> p (t c)"), PS[:, 6:8, :].rearrange("p b c -> p (b c)")[:, 0:T], ACT.Copy).then_inc(act_wt, 1)

                    def stage_a(h):
                        keep_v(h); keep_dq(h); state_decay(h); decay(h, 0); decay(h, 1); decay(h, 2); decay(h, 3)
                        keep_dk(h); keep_dv(h); rms(0, dve_ss, h + 1, act_rs)

                    def stage_b(h, proj):
                        g = h + 1
                        keep_values(h)
                        store(h, 0, ml_stored)
                        if proj: keep_mq(g)
                        exps(h, 0)
                        keep_wt(h, 0)
                        exps(h, 1)
                        if proj: keep_mk(g); silu_q(g)
                        keep_wt(h, 1)
                        exps(h, 2)
                        if proj: keep_mv(g)
                        keep_wt(h, 2)
                        exps(h, 3)
                        if proj: silu_k(g); keep_mo(g)
                        keep_wt(h, 3)
                        rms(1, dve_as, h + 1, act_as)
                        store(h, 1, at_stored)

                    act.wait_ge(s_abs, 1)
                    act.activation(gE[:], gE[:], ACT.Exp, scale=-1.0)
                    act.drain()
                    act.activation(gE[:], gE[:], ACT.Ln, bias=1.0).then_inc(s_lf1, 1)
                    keep_mq(0); keep_mk(0); silu_q(0); keep_mv(0)
                    act.wait_ge(s_scan, 1)
                    act.activation(gE[:], gA[:], ACT.Exp).then_inc(s_ex, 1)
                    silu_k(0); keep_mo(0)
                    with act.Fori(0, H - 1) as h:
                        stage_a(h)
                        stage_b(h, True)
                    stage_a(H - 1)
                    stage_b(H - 1, False)
                    act.wait_ge(ml_stored, 16 * H + 1)
                    act.wait_ge(at_stored, 16 * H + 1)

                @block.gpsimd
                def _(pool):
                    def mask(h, t):
                        pool.wait_ge(act_d, 4 * h + t + 1)
                        pool.sem_inc(s_passed)
                        for d, sign in ((0, 1), (1, -1)):
                            blk = DM[:, t % 2, d, t * P:(t + 1) * P]
                            last = pool.affine_select(out=blk, in_=blk, pattern=[[sign, P]], compare_op=ALU.is_ge, fill=0.0,
                                                      base=0, channel_multiplier=-sign)
                        last.then_inc(pool_d, 1)

                    def split(h, kind):
                        for q in range(4):
                            split_quarter(h, kind, q)

                    def split_quarter(h, kind, q):
                        pool.wait_ge(w_loaded[q], 16 * (NPROJ * h + TILE[kind] + 1))
                        pool.sem_inc(s_passed)
                        pool.tensor_copy(WH[:, q, :, :], WR[:, q, :, :])
                        pool.drain()
                        pool.tensor_tensor(WL[:, q, :, :], WR[:, q, :, :], WH[:, q, :, :].bitcast(f32), ALU.subtract).then_inc(pool_w, 1)

                    def stage(h, proj):
                        split(h, "dq")
                        for q in range(3):
                            split_quarter(h, "dk", q)
                        mask(h, 0); mask(h, 1)
                        split_quarter(h, "dk", 3); split_quarter(h, "dv", 0)
                        mask(h, 2); mask(h, 3)
                        for q in range(1, 4):
                            split_quarter(h, "dv", q)
                        if proj:
                            for kind in MLK:
                                split(h + 1, kind)

                    for kind in MLK:
                        split(0, kind)
                    with pool.Fori(0, H - 1) as h:
                        stage(h, True)
                    stage(H - 1, False)

                @block.vector
                def _(dve):
                    def conv(o, raw, n, c):
                        dve.tensor_scalar(o, raw[:, 0:n], cw[:, c, 0:1], cb[:, bass.ds(c, 1)], ALU.mult, ALU.add)
                        for j in range(1, CONV):
                            dve.drain()
                            last = dve.scalar_tensor_tensor(o, raw[:, j:j + n], cw[:, c, j:j + 1], o, ALU.mult, ALU.add)
                        return last

                    def conv_q(h):
                        dve.wait_ge(act_evac, 7 * h + 1)
                        conv(mq[:], rawq, SEQ, h).then_inc(dve_conv, 1)

                    def conv_k(h):
                        dve.wait_ge(act_evac, 7 * h + 2)
                        conv(mk[:, 0:SEQ], rawk, SEQ, h + H)
                        conv(mk[:, SEQ:T], rawc, CTX, h + H).then_inc(dve_conv, 1)

                    def ctx_keys(h):
                        dve.tensor_scalar(Mh[:].rearrange("p d t -> p (d t)"), Mrow[:].rearrange("p d t -> p (d t)"),
                                          ident[0:H, bass.ds(h, 1)], None, ALU.mult)
                        dve.wait_ge(pe_m1, h + 1)
                        dve.tensor_copy(vaug[:, LT:LT + CT, 0:HD], PS[:, 7, 0:CTX].rearrange("p (t c) -> p t c", c=HD))
                        for d in range(2):
                            for t in range(CT):
                                last = dve.tensor_scalar(kw[:, d, t, :], PS[:, 7, (2 + t) * P:(3 + t) * P],
                                                         colv[:, 16 + d * CT + t, bass.ds(h, 1)], HD ** -0.5, ALU.mult, ALU.mult)
                        last.then_inc(dve_m1, 1)

                    def decayed_queries(h):
                        dve.wait_ge(act_g, h + 1)
                        for d in range(2):
                            last = dve.tensor_tensor(G[:, d, :], G[:, d, :], mq[:], ALU.mult)
                        last.then_inc(dve_qg, 1)

                    def decayed_scores(h, t):
                        dve.wait_ge(pool_d, 4 * h + t + 1)
                        dve.wait_ge(pe_st, 4 * h + t + 1)
                        for d in range(2):
                            l0, l1 = spans(d, t)
                            last = dve.scalar_tensor_tensor(SD[:, d, t, l0:l1], PS[:, 6 + t % 2, l0:l1], HD ** -0.5, DM[:, t % 2, d, l0:l1],
                                                            ALU.mult, ALU.mult)
                        last.then_inc(dve_sd, 1)

                    def squares(o, src):
                        dve.scalar_tensor_tensor(sqd[:], src, 1.0, src, ALU.mult, ALU.mult, accum_out=o)

                    def mean_eps(i):
                        dve.drain()
                        dve.tensor_scalar(ss[:, i, :], ss[:, i, :], 1.0 / HD, RMS_EPS, ALU.mult, ALU.add)

                    def divide(h, t):
                        dve.wait_ge(pe_n, 4 * h + t + 1)
                        bank = PS[:, 5 if t % 2 == 0 else 3, :].rearrange("p (d c) -> p d c", d=2)
                        dsum = bank[:, :, HD:HD + 1].rearrange("p d c -> p (d c)")
                        floor = colv[:, 8 + t:8 + t + LT + 1:LT, bass.ds(h, 1)].rearrange("p d c -> p (d c)")
                        dve.scalar_tensor_tensor(den[:], dsum, -1.0, floor, ALU.mult, ALU.max)
                        dve.drain()
                        dve.tensor_tensor(den[:], dsum, den[:], ALU.max)
                        dve.drain()
                        dve.reciprocal(den[:], den[:])
                        dve.drain()
                        dve.tensor_scalar(hf[:], bank[:, 0, 0:HD], den[:, 0:1], None, ALU.mult)
                        dve.drain()
                        dve.scalar_tensor_tensor(hn[:, t, :], bank[:, 1, 0:HD], den[:, 1:2], hf[:], ALU.mult, ALU.add).then_inc(dve_n, 1)
                        dve.drain()
                        squares(ss[:, 0, t:t + 1], hn[:, t, :])

                    def ml_norm(h):
                        mean_eps(0)
                        dve.drain().then_inc(dve_ss, 1)
                        dve.wait_ge(act_rs, h + 1)
                        dve.tensor_tensor(hn[:], hn[:], ss[:, 0, :].unsqueeze(2).to_broadcast([P, LT, HD]), ALU.mult).then_inc(dve_hn, 1)
                        dve.wait_ge(pe_m5, h + 1)
                        dve.wait_ge(ml_stored, 16 * h + 1)
                        dve.scalar_tensor_tensor(mst[:, 0, :], PS[:, 4, :], gains[:, 1:2], sig[:], ALU.mult, ALU.mult).then_inc(dve_mlout, 1)

                    def rope_qk(h):
                        dve.wait_ge(pe_rot, h + 1)
                        for raw, bank in ((rawdq, 3), (rawdk, 4)):
                            dve.tensor_tensor(tq, raw[:], rp[:, 0, :], ALU.mult)
                            dve.tensor_tensor(tr, PS[:, bank, :], rp[:, 1, :], ALU.mult)
                            dve.drain()
                            if bank == 3:
                                for a in range(2):
                                    r = slice(HALF * a, HALF * (a + 1))
                                    last = dve.tensor_tensor(qz[r, a, :], tq[r, :], tr[r, :], ALU.add)
                            else:
                                last = dve.tensor_tensor(kk[:, 0:SEQ], tq, tr, ALU.add)
                            dve.drain()
                        dve.drain().then_inc(dve_rope, 1)

                    def maxima(h, q):
                        dve.wait_ge(pe_s, 4 * h + q + 1)
                        dve.tensor_reduce(mx[:, 0:2], PS[:, 3:5, :], AX.X, ALU.max)
                        dve.tensor_reduce(mx[:, 2:4], PS[:, 5, :].rearrange("p (a c) -> p a c", a=2), AX.X, ALU.max)
                        dve.drain()
                        dve.tensor_tensor(nm[:], mx[:, 0:2], mx[:, 2:4], ALU.max)
                        dve.drain()
                        dve.tensor_scalar(nm[:], nm[:], -HALF ** -0.5, None, ALU.mult).then_inc(dve_max, 1)

                    def weights(h, q):
                        dve.wait_ge(act_exp, 4 * h + q + 1)
                        dve.tensor_tensor(rz[:], Z[:, 0, :], Z[:, 1, :], ALU.add)
                        dve.drain()
                        dve.reciprocal(rz[:], rz[:])
                        dve.drain()
                        dve.tensor_tensor(rz[:, 1:2], rz[:, 1:2], neglam[:], ALU.mult)
                        if q:
                            dve.wait_ge(pe_t, 4 * h + q)
                        dve.tensor_scalar(Wt[:], E[:, 0, :], rz[:, 0:1], None, ALU.mult)
                        dve.drain()
                        dve.scalar_tensor_tensor(Wt[:], E[:, 1, :], rz[:, 1:2], Wt[:], ALU.mult, ALU.add).then_inc(dve_w, 1)

                    def keep_att(h, q):
                        dve.wait_ge(pe_p, 4 * h + q + 1)
                        dve.tensor_copy(on[:, q, :], PS[:, 7, 256:384]).then_inc(dve_pn, 1)
                        dve.drain()
                        squares(ss[:, 1, q:q + 1], on[:, q, :])

                    def att_norm(h):
                        mean_eps(1)
                        dve.drain().then_inc(dve_as, 1)
                        dve.wait_ge(act_as, h + 1)
                        dve.tensor_tensor(on[:], on[:], ss[:, 1, :].unsqueeze(2).to_broadcast([P, LT, HD]), ALU.mult).then_inc(dve_an, 1)
                        dve.wait_ge(pe_o, h + 1)
                        dve.wait_ge(at_stored, 16 * h + 1)
                        dve.tensor_scalar(mst[:, 1, :], PS[:, 6, :], gains[:, 0:1], None, ALU.mult).then_inc(dve_dout, 1)

                    def stage_a(h):
                        ctx_keys(h); decayed_queries(h)
                        for t in range(LT):
                            decayed_scores(h, t)
                        for t in range(LT):
                            divide(h, t)
                        ml_norm(h)

                    def stage_b(h, proj):
                        g = h + 1
                        rope_qk(h); maxima(h, 0)
                        if proj: conv_q(g)
                        weights(h, 0); maxima(h, 1); weights(h, 1); keep_att(h, 0)
                        if proj: conv_k(g)
                        maxima(h, 2); weights(h, 2); keep_att(h, 1)
                        maxima(h, 3); weights(h, 3); keep_att(h, 2); keep_att(h, 3)
                        att_norm(h)

                    dve.memset(zeros[:], 0.0).then_inc(s_zero, 1)
                    for pad in (rawq[:, 0:PAD], rawq[:, PAD + SEQ:], rawk[:, 0:PAD], rawk[:, PAD + SEQ:], rawc[:, 0:PAD], rawc[:, PAD + CTX:]):
                        dve.memset(pad, 0.0)
                    dve.memset(vaug[:, :, HD:HD + 2], 1.0)
                    dve.memset(onesH[:], 1.0)
                    dve.memset(qz[HALF:P, 0, :], 0.0)
                    dve.memset(qz[0:HALF, 1, :], 0.0)
                    dve.drain().then_inc(s_tab, 1)
                    for s in (ml_stored, at_stored):
                        dve.drain().then_inc(s, 1)
                    dve.memset(ones8[:], 1.0)
                    dve.wait_ge(s_gate_mv, 64)
                    dve.scalar_tensor_tensor(gE[:], gF[:], -1.0, gF[:], ALU.mult, ALU.max).then_inc(s_abs, 1)
                    dve.wait_ge(s_tab, 49)
                    conv_q(0)
                    dve.tensor_scalar(gF[:], gF[:], 0.0, None, ALU.min)
                    dve.drain()
                    dve.wait_ge(s_lf1, 1)
                    dve.tensor_tensor(gF[:], gF[:], gE[:], ALU.subtract)
                    dve.drain()
                    for d in range(2):
                        for t0, t1 in ((0, SEQ), (SEQ, T)):
                            o, i = gA[:, d, t0:t1], gF[:, d, t0:t1]
                            if d:
                                o, i = o[:, ::-1], i[:, ::-1]
                            dve.tensor_tensor_scan(out=o, data0=ones8[:, 0:t1 - t0], data1=i, initial=0.0, op0=ALU.mult, op1=ALU.add)
                    dve.drain()
                    dve.tensor_tensor(gI[:], gI[:], gA[:], ALU.subtract)
                    dve.drain()
                    dve.tensor_reduce(mc[:], gI[:, :, SEQ:T], AX.X, ALU.max)
                    dve.drain()
                    dve.tensor_scalar(mc[:], mc[:], 0.0, None, ALU.max)
                    dve.drain()
                    dve.tensor_tensor(m0[:, 0:1], mc[:, 0:1], gA[:, 0, T - 1:T], ALU.add)
                    dve.tensor_tensor(m0[:, 1:2], mc[:, 1:2], gA[:, 1, SEQ:SEQ + 1], ALU.add)
                    dve.drain()
                    for d in range(2):
                        dve.tensor_scalar(dm0[:, d, :], ident[0:H, 0:H], m0[:, d:d + 1], None, ALU.mult)
                        o, i = Mrow[:, d, :], gI[:, d, 0:SEQ]
                        if d:
                            o, i = o[:, ::-1], i[:, ::-1]
                        dve.tensor_tensor_scan(out=o, data0=i, data1=i, initial=m0[:, d:d + 1], op0=ALU.max, op1=ALU.max)
                        dve.tensor_scalar(gA[:, d, SEQ:T], gI[:, d, SEQ:T], mc[:, d:d + 1], None, ALU.subtract)
                    dve.drain().then_inc(s_dm, 1)
                    dve.scalar_tensor_tensor(gA[:, :, 0:SEQ], gA[:, :, 0:SEQ], -1.0, Mrow[:], ALU.mult, ALU.subtract).then_inc(s_scan, 1)
                    conv_k(0)
                    dve.wait_ge(s_col, 1)
                    dve.tensor_copy(colv[:].rearrange("p a h -> p (a h)"), PS[:, 5, 0:20 * H])
                    dve.tensor_copy(m0b[:].rearrange("p a h -> p (a h)"), PS[:, 6, 0:2 * H])
                    dve.drain().then_inc(dve_dout, 1)
                    with dve.Fori(0, H - 1) as h:
                        stage_a(h)
                        stage_b(h, True)
                    stage_a(H - 1)
                    stage_b(H - 1, False)

        sb_at("ring_place", [P, 2, KT, CHUNK])
        assert at["ring_place"] == at["hH"]
        mixT = sb_at("mixT", [P, KT, SEQ])
        x1 = sb("x1", [P, LT, D])
        x1_dram = nc.dram_tensor("x1_dram", (SEQ, D), f32, kind="Internal").ap()
        vecs = sb_at("vecs", [P, 4, D])
        lng = sb("lng", [P, 2, D])
        eidx = sb("eidx", [P, NG, GROUP], u32)
        gate = sb("gate", [P, NG, GROUP])
        st6 = sb("st6", [P, LT, 4, 6])
        mv2 = sb("mv2", [P, LT, 2])
        rsd = sb("rsd", [P, LT])
        nmr = sb("nmr", [P, LT])
        h2 = mixT[:].rearrange("p k t -> p (k t)").rearrange("p (t d) -> p t d", t=LT)

        s_mix, s_mh = sem("mixer_output_loaded"), sem("mixer_output_high")
        s_o = [sem(f"out_unit_loaded{i}") for i in range(4)]
        s_oh, s_ol, s_ope = sem("out_unit_high"), sem("out_unit_low"), sem("out_units_multiplied")
        s_silg, s_g2w, s_g2pe, s_g2ev = sem("silu_spread_again"), sem("gate2_weights"), sem("gate2_summed"), sem("gate2_kept")
        s_nmr, s_z, s_zused, s_x1 = sem("ln_stats_final"), sem("rows_normalised"), sem("normalised_rows_used"), sem("residual_ready")
        s_ld3, s_x3 = sem("vectors_loaded"), sem("residual_and_ln1_loaded")
        s_rep = sem("silu_spread3")
        s_cpe, s_cev = sem("chunk_summed"), sem("chunk_kept")
        s_keys = sem("keys_loaded")
        s_wq = [sem("query_weights_loaded0"), sem("query_weights_loaded1")]
        s_stat, s_std = sem("ln_stats"), sem("ln_std")
        s_h2, s_hTpe, s_hTev = sem("peer_input"), sem("peer_input_turned"), sem("peer_input_turned_kept")
        s_qpe, s_qev = sem("queries_summed"), sem("queries_kept")
        s_spe, s_sev = sem("key_scores"), sem("key_scores_kept")
        s_top, s_gex = sem("chosen"), sem("chosen_exps")
        s_dense, s_scat = sem("dense_gates_ready"), sem("dense_gates_added")
        s_added = sem("heads_gates_added")
        s_xh, s_xl = sem("dense_input_high"), sem("dense_input_low")
        s_spill = sem("residual_stored")

        def row_stats(dve, tiles, sem_stat, sem_std, n):
            for t in tiles:
                dve.bn_aggr(mv2[:, t, :], st6[:, t, :, :].rearrange("p a b -> p (a b)"))
            ts = slice(tiles[0], tiles[-1] + 1)
            var = mv2[:, ts, 1:2].rearrange("p a b -> p (a b)")
            mean = mv2[:, ts, 0:1].rearrange("p a b -> p (a b)")
            dve.drain()
            dve.tensor_scalar(rsd[:, ts], var, LN_EPS, None, ALU.add).then_inc(sem_stat, 1)
            dve.wait_ge(sem_std, n)
            dve.reciprocal(rsd[:, ts], rsd[:, ts])
            dve.drain()
            return dve.scalar_tensor_tensor(nmr[:, ts], mean, -1.0, rsd[:, ts], ALU.mult, ALU.mult)

        xh = over("xh", "mixT", [P, KT, DTOK], f32r)
        xl = over("xl", "vecs", [P, KT, DTOK], f32r)

        UR = over("UR", "ring_place", [P, GROUP, KT, P])
        UL = over("UL", "ring_place", [P, GROUP, KT, P], f32r)
        UH = over("UH", "ring_place", [P, GROUP, KT, P], f32r, skip=4 * GROUP * KT * P)
        s_ut = [sem("ut_block_loaded0"), sem("ut_block_loaded1")]
        s_uh, s_ul = sem("u_high_parts"), sem("u_low_parts")
        s_pa, s_ge = sem("dense_dots"), sem("dense_gelu")

        def u_block(sp, n, j):
            sp.dma_start(UR[:, j, :, :], peer_ut[GROUP * n + j]).then_inc(s_ut[j], 16)

        def u_high(act, n, j):
            act.wait_ge(s_ut[j], 16 * n + 16)
            act.activation(UH[:, j, :, :], UR[:, j, :, :], ACT.Copy).then_inc(s_uh, 1)

        def u_low(dve, n, j):
            dve.wait_ge(s_uh, GROUP * n + j + 1)
            dve.tensor_tensor(UL[:, j, :, :], UR[:, j, :, :], UH[:, j, :, :].bitcast(f32), ALU.subtract).then_inc(s_ul, 1)

        def dense_dots(pe, n):
            for j in range(GROUP):
                pe.wait_ge(s_ul, GROUP * n + j + 1)
                if j == 0:
                    pe.wait_ge(s_ge, n + 1)
                for k in range(KT):
                    dst = PS[:, j, 0:DTOK]
                    pe.matmul(dst, UH[:, j, k, :], xh[:, k, :], start=(k == 0), stop=False)
                    pe.matmul(dst, UH[:, j, k, :], xl[:, k, :], start=False, stop=False)
                    last = pe.matmul(dst, UL[:, j, k, :], xh[:, k, :], start=False, stop=(k == KT - 1))
                last.then_inc(s_pa, 1)

        def dense_gelu(act, n):
            act.wait_ge(s_pa, GROUP * n + GROUP)
            act.activation(gl[:], PS[:, 0:GROUP, 0:DTOK], ACT.Gelu).then_inc(s_ge, 1)

        b3 = ExitStack()
        with b3:
            oR = over("oR", "ring_place", [P, 4, OUK, CHUNK])
            oL = over("oL", "ring_place", [P, 4, OUK, CHUNK], f32r)
            oH = over("oH", "ring_place", [P, 4, OUK, CHUNK], f32r, skip=4 * OUK * CHUNK * 4)
            mixH = over("mixH", "ring_place", [P, KT, SEQ], f32r, skip=KT * CHUNK * 4)
            mixL = over("mixL", "mixT", [P, KT, SEQ], f32r)
            wqb = sb("wqb", [P, 2, KT, P], ctx=b3)
            kys = sb_at("kys", [P, 2 * PH, NKEYS], ctx=b3)
            gl = over("gl", "kys", [P, GROUP, DTOK])
            silB = wqb[:, 0, :, :]
            g2w = x1[:].rearrange("p t d -> p (t d)")[:, 0:KT * G2C].rearrange("p (k c) -> p k c", k=KT)
            silG = lng[:, 0, :].rearrange("p (k m) -> p k m", k=KT)
            h2T = ring[:, 0, :, :]
            rest = ring[:, 1, :, :].rearrange("p k c -> p (k c)")
            def carve(at, shape, dt=f32, src=None):
                n = int(np.prod(shape[1:]))
                v = (rest if src is None else src)[:, at:at + n]
                if dt is not f32:
                    v = v.bitcast(dt)
                if len(shape) == 2:
                    return v
                names = "abcd"[:len(shape) - 1]
                return v.rearrange(f"p ({' '.join(names)}) -> p {' '.join(names)}", **dict(zip(names, shape[1:])))
            qT = carve(0, [P, 2, SEQ])
            sc = carve(1024, [P, LT, 2, NKEYS])
            s2 = carve(2048, [P, LT, 2, NKEYS])
            cand = carve(3072, [P, LT, TOPK * TOPK])
            cand2 = carve(4096, [P, LT, TOPK * TOPK])
            oh = carve(5120, [P, LT, TOPK, TOPK])
            vv = carve(6144, [P, LT, 2, TOPK])
            ii = carve(6272, [P, LT, 2, TOPK], u32)
            iif = carve(6400, [P, LT, 2, TOPK])
            tv = carve(6528, [P, LT, TOPK])
            tp = carve(6592, [P, LT, TOPK], u32)
            ab = carve(6656, [P, 2, LT, TOPK], u32)
            abf = carve(6784, [P, 2, LT, TOPK])
            sel = carve(6912, [P, 2, LT, TOPK])
            ef = carve(7040, [P, LT, TOPK])
            gx = carve(7104, [P, LT, TOPK])
            gs = carve(7168, [P, LT])
            dgate = carve(7172, [P, DT, TOPK])
            didx = carve(7172 + DT * TOPK, [P, DT, TOPK], u32)
            yg = carve(0, [P, LT, CHUNK], src=kys[:].rearrange("p a k -> p (a k)"))

            with nc.Block() as block:
                @block.sync
                def _(sp):
                    wv = wada.rearrange("(k p) (n c) -> p k n c", p=P, c=CHUNK)
                    ov = wout.rearrange("(k p) (n c) -> p k n c", p=P, c=CHUNK)
                    for i in range(4):
                        sp.dma_start(vecs[:, i, :], brow[i:i + 1, :].partition_broadcast(P)).then_inc(s_ld3, 16)
                    sp.dma_start(mixT[:], mix_dram.rearrange("(k p) t -> p k t", p=P)).then_inc(s_mix, 16)
                    with sp.Fori(1, REST_CHUNKS // 2) as n:
                        for j in range(2):
                            sp.wait_ge(s_cpe, 2 * n + j - 1)
                            sp.dma_start(ring[:, j, :, :], wv[:, :, SH_CHUNKS + 2 * n + j, :]).then_inc(s_wb[j], 16)
                    sp.dma_start(x1[:], x.rearrange("(t p) d -> p t d", p=P)).then_inc(s_x3, 16)
                    for i in range(2):
                        sp.dma_start(lng[:, i, :], lnv[i:i + 1, :].partition_broadcast(P)).then_inc(s_x3, 16)
                    def out_unit(c, u):
                        sp.dma_start(oR[:, u % 4, :, :], ov[:, u * OUK:(u + 1) * OUK, c, :]).then_inc(s_o[u % 4], 16)

                    sp.wait_ge(s_cpe, REST_CHUNKS - 1)
                    for u in range(OUNITS):
                        if u >= 4:
                            sp.wait_ge(s_ope, u - 3)
                        out_unit(0, u)
                    with sp.Fori(1, OUT_CHUNKS) as c:
                        for u in range(OUNITS):
                            sp.wait_ge(s_ope, OUNITS * c + u - 3)
                            out_unit(c, u)
                    for t in range(LT):
                        sp.wait_ge(s_x1, t + 1)
                        sp.dma_start(x1_dram[t * P:(t + 1) * P, :], x1[:, t, :]).then_inc(s_spill, 16)
                        if t == 0:
                            sp.dma_start(kys[:].rearrange("p a k -> p (a k)"), keysT).then_inc(s_keys, 16)
                    for j in range(2):
                        sp.dma_start(wqb[:, j, :, :], wq[j]).then_inc(s_wq[j], 16)
                    gv = wada.rearrange("(k p) (n c) -> p k n c", p=P, c=G2C)
                    g2_at = 5 * D // G2C
                    sp.wait_ge(s_spill, 16 * LT)
                    sp.dma_start(g2w, gv[:, :, g2_at, :]).then_inc(s_g2w, 16)
                    with sp.Fori(1, PH) as n:
                        for j in range(2):
                            sp.wait_ge(s_qpe, 2 * n + j - 1)
                            sp.dma_start(wqb[:, j, :, :], wq[2 * n + j]).then_inc(s_wq[j], 16)
                        sp.wait_ge(s_g2pe, n)
                        sp.dma_start(g2w, gv[:, :, n + g2_at, :]).then_inc(s_g2w, 16)
                    sp.wait_ge(s_qpe, 2 * PH)
                    sp.wait_ge(s_xl, 1)
                    u_block(sp, 0, 0); u_block(sp, 0, 1)
                    for j in range(GROUP):
                        sp.wait_ge(s_pa, j + 1)
                        u_block(sp, 1, j)

                @block.tensor
                def _(pe):
                    pe.wait_ge(s_rep, 1)
                    with pe.Fori(0, REST_CHUNKS // 2) as n:
                        for j in range(2):
                            pe.wait_ge(s_wb[j], 16 * n + 16)
                            pe.wait_ge(s_cev, 2 * n + j + 1)
                            for k in range(KT):
                                last = pe.matmul(PS[:, j, :], silB[:, k, :], ring[:, j, k, :], start=(k == 0), stop=(k == KT - 1))
                            last.then_inc(s_cpe, 1)
                    pe.wait_ge(s_cev, REST_CHUNKS + 2)
                    with pe.Fori(0, OUT_CHUNKS // 2) as n:
                        for j in range(2):
                            c = 2 * n + j
                            pe.wait_ge(s_cev, c + REST_CHUNKS + 1)
                            for u in range(OUNITS):
                                pe.wait_ge(s_ol, OUNITS * c + u + 1)
                                for t in range(LT):
                                    tok, dst = slice(t * P, (t + 1) * P), PS[:, 4 * j + t, :]
                                    for i in range(OUK):
                                        k = OUK * u + i
                                        pe.matmul(dst, mixH[:, k, tok], oH[:, u % 4, i, :], start=(k == 0), stop=False)
                                        pe.matmul(dst, mixL[:, k, tok], oH[:, u % 4, i, :], start=False, stop=False)
                                        last = pe.matmul(dst, mixH[:, k, tok], oL[:, u % 4, i, :], start=False, stop=(k == KT - 1))
                                last.then_inc(s_ope, 1)
                    for t in range(LT):
                        pe.wait_ge(s_h2, t + 1)
                        for q in range(4):
                            n = 4 * t + q
                            if n >= 4:
                                pe.wait_ge(s_hTev, n - 3)
                            for i in range(4):
                                k = 4 * q + i
                                last = pe.transpose(PS[:, n % 4, i * P:(i + 1) * P], h2[:, t, k * P:(k + 1) * P], ident)
                            last.then_inc(s_hTpe, 1)
                    pe.wait_ge(s_hTev, 16)
                    pe.wait_ge(s_keys, 16)

                    def queries(m, j):
                        pe.wait_ge(s_wq[j], 16 * m + 16)
                        pe.wait_ge(s_qev, 2 * m + j + 1)
                        for k in range(KT):
                            last = pe.matmul(PS[:, j, :], wqb[:, j, k, :], h2T[:, k, :], start=(k == 0), stop=(k == KT - 1))
                        last.then_inc(s_qpe, 1)

                    def key_scores(m, j):
                        pe.wait_ge(s_qev, 2 * m + j + 3)
                        pe.wait_ge(s_sev, 2 * m + j + 1)
                        for t in range(LT):
                            last = pe.matmul(PS[:, 2 + j, t * NKEYS:(t + 1) * NKEYS], qT[:, j, t * P:(t + 1) * P],
                                             kys[:, bass.ds(2 * m + j, 1), :].rearrange("p a k -> p (a k)"), start=True, stop=True)
                        last.then_inc(s_spe, 1)

                    def gate2(m):
                        pe.wait_ge(s_g2w, 16 * m + 16)
                        pe.wait_ge(s_g2ev, m + 1)
                        for k in range(KT):
                            last = pe.matmul(PS[:, 4, 0:G2C], silG[:, k, :], g2w[:, k, :], start=(k == 0), stop=(k == KT - 1))
                        last.then_inc(s_g2pe, 1)

                    queries(0, 0)
                    pe.wait_ge(s_silg, 1)
                    with pe.Fori(0, PH - 1) as m:
                        queries(m, 1); key_scores(m, 0); queries(m + 1, 0); key_scores(m, 1); gate2(m)
                    queries(PH - 1, 1); key_scores(PH - 1, 0); key_scores(PH - 1, 1); gate2(PH - 1)
                    pe.wait_ge(s_xh, 1)
                    pe.wait_ge(s_xl, 1)
                    dense_dots(pe, 0)

                @block.gpsimd
                def _(pool):
                    cells = gates_dram.rearrange("e (t o) -> (e t) o", o=1)
                    def out_low(c, u):
                        pool.wait_ge(s_oh, OUNITS * c + u + 1)
                        pool.sem_inc(s_passed)
                        pool.tensor_tensor(oL[:, u % 4, :, :], oR[:, u % 4, :, :], oH[:, u % 4, :, :].bitcast(f32), ALU.subtract).then_inc(s_ol, 1)

                    for u in range(OUNITS):
                        ks = slice(u * OUK, (u + 1) * OUK)
                        pool.wait_ge(s_mh, u + 1)
                        pool.tensor_tensor(mixL[:, ks, :], mixT[:, ks, :], mixH[:, ks, :].bitcast(f32), ALU.subtract)
                        pool.drain()
                        out_low(0, u)
                    with pool.Fori(1, OUT_CHUNKS) as c:
                        for u in range(OUNITS):
                            out_low(c, u)
                    for t in range(LT):
                        pool.wait_ge(s_zused, t + 1)
                        pool.tensor_tensor(x1[:, t, :], x1[:, t, :], lng[:, 0, :], ALU.mult)
                        pool.drain()
                        pool.tensor_tensor(x1[:, t, :], x1[:, t, :], lng[:, 1, :], ALU.add).then_inc(s_x1, 1)
                    pool.drain()
                    pool.tensor_copy(silG, silc[:, 0, :].unsqueeze(2).to_broadcast([P, KT, P])).then_inc(s_silg, 1)
                    pool.wait_ge(s_xh, 1)
                    pool.tensor_tensor(xl[:], h2T[:, :, 0:DTOK], xh[:].bitcast(f32), ALU.subtract).then_inc(s_xl, 1)
                    with pool.Fori(0, PH) as m:
                        pool.wait_ge(s_dense, m + 1)
                        pool.sem_inc(s_passed)
                        for t in range(DT):
                            for k in range(TOPK):
                                pool.indirect_dma_start(out=cells, out_offset=bass.IndirectOffsetOnAxis(ap=didx[:, t, k:k + 1], axis=0),
                                                        in_=dgate[:, t, k:k + 1], in_offset=None, compute_op=ALU.add).then_inc(s_scat, 16)
                        pool.wait_ge(s_scat, (16 * DT * TOPK) * m + 16 * DT * TOPK)
                        pool.sem_inc(s_added)

                @block.scalar
                def _(act):
                    def out_high(c, u):
                        act.wait_ge(s_o[u % 4], 16 * (2 * c + u // 4) + 16)
                        act.activation(oH[:, u % 4, :, :], oR[:, u % 4, :, :], ACT.Copy).then_inc(s_oh, 1)

                    act.wait_ge(s_mix, 16)
                    act.wait_ge(s_cpe, REST_CHUNKS)
                    for u in range(OUNITS):
                        ks = slice(u * OUK, (u + 1) * OUK)
                        act.activation(mixH[:, ks, :], mixT[:, ks, :], ACT.Copy).then_inc(s_mh, 1)
                        out_high(0, u)
                    with act.Fori(1, OUT_CHUNKS) as c:
                        for u in range(OUNITS):
                            out_high(c, u)
                    act.wait_ge(s_stat, 1)
                    act.activation(rsd[:], rsd[:], ACT.Sqrt).then_inc(s_std, 1)

                    def normalise(t):
                        act.activation(x1[:, t, :], x1[:, t, :], ACT.Identity, scale=rsd[:, t:t + 1], bias=nmr[:, t:t + 1]).then_inc(s_z, 1)

                    act.wait_ge(s_nmr, 1)
                    normalise(0)
                    for t in range(LT):
                        if t < LT - 1:
                            normalise(t + 1)
                        for q in range(4):
                            n = 4 * t + q
                            act.wait_ge(s_hTpe, n + 1)
                            act.activation(h2T[:, 4 * q:4 * q + 4, t * P:(t + 1) * P],
                                           PS[:, n % 4, :].rearrange("p (i c) -> p i c", i=4), ACT.Copy).then_inc(s_hTev, 1)

                    def keep_queries(m):
                        for j in range(2):
                            act.wait_ge(s_qpe, 2 * m + j + 1)
                            act.wait_ge(s_spe, 2 * m + j + 1)
                            act.activation(qT[:, j, :], PS[:, j, :], ACT.Copy).then_inc(s_qev, 1)

                    def keep_scores(m):
                        act.wait_ge(s_top, m + 1)
                        for j in range(2):
                            act.wait_ge(s_spe, 2 * m + j + 3)
                            act.activation(sc[:, :, j, :], PS[:, 2 + j, :].rearrange("p (t k) -> p t k", k=NKEYS), ACT.Copy).then_inc(s_sev, 1)

                    def gate_exps(m):
                        act.wait_ge(s_top, m + 2)
                        act.activation(gx, gx, ACT.Exp).then_inc(s_gex, 1)

                    keep_queries(0)
                    act.activation(xh[:], h2T[:, :, 0:DTOK], ACT.Copy).then_inc(s_xh, 1)
                    keep_scores(0)
                    with act.Fori(1, PH) as m:
                        keep_queries(m); gate_exps(m - 1); keep_scores(m)
                    gate_exps(PH - 1)
                    u_high(act, 0, 0); u_high(act, 0, 1)
                    u_high(act, 1, 0)
                    dense_gelu(act, 0)
                    u_high(act, 1, 1)

                @block.vector
                def _(dve):
                    for i in range(2):
                        for s in (s_cev, s_qev, s_sev, s_spe):
                            dve.drain().then_inc(s, 1)
                    for s in (s_top, s_g2ev, s_ge):
                        dve.drain().then_inc(s, 1)
                    dve.tensor_copy(silB, silc[:, 0, :].unsqueeze(2).to_broadcast([P, KT, P])).then_inc(s_rep, 1)
                    dve.wait_ge(s_ld3, 4 * 16)
                    vflat = vecs[:].rearrange("p a d -> p (a d)")
                    with dve.Fori(0, REST_CHUNKS // 2) as n:
                        for j in range(2):
                            dve.wait_ge(s_cpe, 2 * n + j + 1)
                            part = vflat[:, bass.ds((2 * n + j) * CHUNK, CHUNK)]
                            dve.tensor_tensor(part, PS[:, j, :], part, ALU.add).then_inc(s_cev, 1)
                    dve.drain()
                    dve.tensor_scalar(vecs[:, 2, :], vecs[:, 2, :], 1.0, None, ALU.add)
                    dve.wait_ge(s_x3, 16 * 3)
                    tmp = kys[:].rearrange("p a k -> p (a k)")
                    dve.drain()
                    dve.tensor_tensor(tmp, lng[:, 1, :], vecs[:, 2, :], ALU.mult)
                    dve.drain()
                    dve.tensor_tensor(vecs[:, 1, :], vecs[:, 1, :], tmp, ALU.add)
                    dve.tensor_tensor(vecs[:, 2, :], vecs[:, 2, :], lng[:, 0, :], ALU.mult)
                    dve.drain()
                    with dve.Fori(0, OUT_CHUNKS // 2) as n:
                        for j in range(2):
                            c = 2 * n + j
                            dve.wait_ge(s_ope, OUNITS * c + OUNITS)
                            cols = bass.ds(c * CHUNK, CHUNK)
                            for t in range(LT):
                                last = dve.tensor_tensor(yg[:, t, :], PS[:, 4 * j + t, :], vecs[:, 0, cols], ALU.mult)
                            last.then_inc(s_cev, 1)
                            dve.drain()
                            for t in range(LT):
                                dve.scalar_tensor_tensor(x1[:, t, cols], x1[:, t, cols], ALPHA, yg[:, t, :], ALU.mult, ALU.add)
                            dve.drain()
                            for t in range(LT):
                                dve.bn_stats(st6[:, t, bass.ds(c, 1), :].rearrange("p a b -> p (a b)"), x1[:, t, cols])
                            dve.drain()
                    row_stats(dve, list(range(LT)), s_stat, s_std, 1).then_inc(s_nmr, 1)
                    for t in range(LT):
                        dve.wait_ge(s_z, t + 1)
                        dve.tensor_tensor(h2[:, t, :], x1[:, t, :], vecs[:, 2, :], ALU.mult).then_inc(s_zused, 1)
                        dve.drain()
                        dve.tensor_tensor(h2[:, t, :], h2[:, t, :], vecs[:, 1, :], ALU.add).then_inc(s_h2, 1)

                    def top16(groups):
                        for src, tmp, v, i in groups:
                            dve.max(v[:, 0:8], src)
                        dve.drain()
                        for src, tmp, v, i in groups:
                            dve.max_index(i[:, 0:8], v[:, 0:8], src)
                            dve.match_replace(out=tmp, in_to_replace=v[:, 0:8], in_values=src, imm_value=NEG)
                        dve.drain()
                        for src, tmp, v, i in groups:
                            dve.max(v[:, 8:16], tmp)
                        dve.drain()
                        for src, tmp, v, i in groups:
                            dve.max_index(i[:, 8:16], v[:, 8:16], tmp)
                        dve.drain()

                    eview = eidx[:].rearrange("p (t m a) b -> p t m (a b)", t=LT - DT, m=PH)
                    gview = gate[:].rearrange("p (t m a) b -> p t m (a b)", t=LT - DT, m=PH)
                    flat = lambda v: v.rearrange("p a b -> p (a b)")
                    dve.drain().then_inc(s_added, 1)
                    with dve.Fori(0, PH) as m:
                        dve.wait_ge(s_sev, 2 * m + 4)
                        dve.memset(gs, 0.0)
                        top16([(sc[:, t, j, :], s2[:, t, j, :], vv[:, t, j, :], ii[:, t, j, :]) for t in range(LT) for j in range(2)])
                        for t in range(LT):
                            dve.tensor_tensor(cand[:, t, :].rearrange("p (a b) -> p a b", a=TOPK),
                                              vv[:, t, 0, :].unsqueeze(2).to_broadcast([P, TOPK, TOPK]),
                                              vv[:, t, 1, :].unsqueeze(1).to_broadcast([P, TOPK, TOPK]), ALU.add)
                        dve.tensor_copy(iif, ii)
                        dve.drain()
                        top16([(cand[:, t, :], cand2[:, t, :], tv[:, t, :], tp[:, t, :]) for t in range(LT)])
                        dve.tensor_tensor(gx, tv, tv[:, :, 0:1].to_broadcast([P, LT, TOPK]), ALU.subtract).then_inc(s_top, 1)
                        dve.tensor_scalar(flat(ab[:, 0, :, :]), flat(tp), 4, None, ALU.logical_shift_right)
                        dve.tensor_scalar(flat(ab[:, 1, :, :]), flat(tp), TOPK - 1, None, ALU.bitwise_and)
                        dve.drain()
                        dve.tensor_copy(abf, ab)
                        dve.drain()
                        for j in range(2):
                            dve.tensor_tensor(oh.rearrange("p t k i -> p (t k) i"), flat(abf[:, j, :, :]).unsqueeze(2).to_broadcast([P, LT * TOPK, TOPK]),
                                              iota16.unsqueeze(1).to_broadcast([P, LT * TOPK, TOPK]), ALU.is_equal)
                            dve.drain()
                            dve.tensor_tensor(oh, oh, iif[:, :, j, :].unsqueeze(2).to_broadcast([P, LT, TOPK, TOPK]), ALU.mult)
                            dve.drain()
                            dve.tensor_reduce(sel[:, j, :, :], oh, AX.X, ALU.add)
                            dve.drain()
                        dve.scalar_tensor_tensor(ef, sel[:, 0, :, :], float(NKEYS), sel[:, 1, :, :], ALU.mult, ALU.add)
                        dve.wait_ge(s_gex, m + 1)
                        dve.tensor_reduce(gs, gx, AX.X, ALU.add)
                        dve.drain()
                        dve.reciprocal(gs, gs)
                        dve.tensor_copy(eview[:, :, bass.ds(m, 1), :].rearrange("p t m k -> p t (m k)"), ef[:, DT:LT, :])
                        dve.drain()
                        dve.wait_ge(s_added, m + 1)
                        dve.scalar_tensor_tensor(didx, ef[:, 0:DT, :], float(DTOK), tokid.unsqueeze(2).to_broadcast([P, DT, TOPK]), ALU.mult, ALU.add)
                        dve.tensor_tensor(gview[:, :, bass.ds(m, 1), :].rearrange("p t m k -> p t (m k)"), gx[:, DT:LT, :],
                                          gs[:, DT:LT].unsqueeze(2).to_broadcast([P, LT - DT, TOPK]), ALU.mult)
                        dve.tensor_tensor(dgate, gx[:, 0:DT, :], gs[:, 0:DT].unsqueeze(2).to_broadcast([P, DT, TOPK]), ALU.mult)
                        dve.drain().then_inc(s_dense, 1)
                        dve.wait_ge(s_g2pe, m + 1)
                        part = vecs[:, 3, bass.ds(m * G2C, G2C)]
                        dve.tensor_tensor(part, PS[:, 4, 0:G2C], part, ALU.add).then_inc(s_g2ev, 1)
                    for n in range(2):
                        for j in range(GROUP):
                            u_low(dve, n, j)

        b4 = ExitStack()
        s_u = [sem(f"u_rows{i}") for i in range(GROUP)]
        s_v = [sem(f"v_rows{i}") for i in range(GROUP)]
        s_idx = sem("indices_staged")
        s_udone, s_vdone = sem("u_rows_used"), sem("v_rows_used")
        s_act, s_dgelu = sem("dots_done"), sem("dots_gelu")
        s_vb = [sem(f"v_chunk_loaded{c}") for c in range(OUT_CHUNKS)]
        s_gb = sem("gate_blocks_loaded")
        s_vh, s_vl = sem("v_high_parts"), sem("v_low_parts")
        s_po, s_m, s_add = sem("dense_outputs"), sem("dense_gated"), sem("dense_added")
        s_gdone = sem("sums_done")
        s_ln4, s_back = sem("ln2_loaded"), [sem(f"residual_back{t}") for t in range(LT)]
        s_nmr4, s_z4, s_gained = sem("ln2_stats_final"), sem("ln2_rows_normalised"), sem("ln2_rows_gained")
        s_stat4, s_std4 = sem("ln2_stats"), sem("ln2_std")
        s_y, s_out = sem("rows_finished"), sem("rows_stored")
        with b4:
            Ub = lng
            Vb = sb("Vb", [P, GROUP, D], ctx=b4)
            VR = over("VR", "ring_place", [P, GROUP, D], skip=8 * GROUP * D)
            VL = over("VL", "ring_place", [P, GROUP, D], f32r, skip=8 * GROUP * D)
            VH = over("VH", "ring_place", [P, GROUP, D], f32r, skip=12 * GROUP * D)
            sb_at("gl_place", [P, GROUP, DTOK], ctx=b4)
            assert at["gl_place"] == at["kys"]
            GB = sb("GB", [P, GROUP, DTOK], ctx=b4)
            AH = sb("AH", [P, GROUP, DTOK], f32r, ctx=b4)
            AL = sb("AL", [P, GROUP, DTOK], f32r, ctx=b4)
            stage = sb("stage", [P, 2, GROUP], u32, ctx=b4)
            dots = sb("dots", [P, GROUP], ctx=b4)
            coef = sb("coef", [P, GROUP], ctx=b4)
            VHf, AHf = VH[:].bitcast(f32), AH[:].bitcast(f32)
            NOUT = OUT_CHUNKS * DT
            OB = 6
            chunk = [slice(c * CHUNK, (c + 1) * CHUNK) for c in range(OUT_CHUNKS)]

            with nc.Block() as block:
                @block.sync
                def _(sp):
                    gd = gates_dram.rearrange("(n b p) t -> p n b t", b=GROUP, p=P)
                    vd = peer_v.rearrange("(n b p) d -> p n b d", b=GROUP, p=P)

                    def v_chunk(n, c):
                        sp.dma_start(VR[:, :, chunk[c]], vd[:, bass.ds(n, 1), :, chunk[c]].rearrange("p a b d -> p (a b) d")).then_inc(s_vb[c], 16)

                    def g_block(n):
                        sp.dma_start(GB[:], gd[:, bass.ds(n, 1), :, :].rearrange("p a b t -> p (a b) t")).then_inc(s_gb, 16)

                    def turn(n, more):
                        if more:
                            for j in range(GROUP):
                                sp.wait_ge(s_pa, GROUP * n + j + GROUP + 1)
                                u_block(sp, n + 2, j)
                        sp.wait_ge(s_m, n + 1)
                        g_block(n + 1)
                        for c in range(OUT_CHUNKS):
                            sp.wait_ge(s_po, NOUT * n + DT * (c + 1))
                            v_chunk(n + 1, c)

                    g_block(0)
                    for c in range(OUT_CHUNKS):
                        v_chunk(0, c)
                    with sp.Fori(0, NG - 2) as n:
                        turn(n, True)
                    turn(NG - 2, False)
                    sp.wait_ge(s_pa, GROUP * NG)
                    for t in range(DT):
                        sp.dma_start(h2[:, t, :], x1_dram[t * P:(t + 1) * P, :]).then_inc(s_back[t], 16)
                    sp.wait_ge(s_udone, GROUP * NG + GROUP)
                    for i in range(2):
                        sp.dma_start(lng[:, i, :], lnv[2 + i:3 + i, :].partition_broadcast(P)).then_inc(s_ln4, 16)
                    for t in range(DT, LT):
                        sp.dma_start(h2[:, t, :], x1_dram[t * P:(t + 1) * P, :]).then_inc(s_back[t], 16)
                    for t in range(LT):
                        sp.wait_ge(s_y, t + 1)
                        sp.dma_start(out[t * P:(t + 1) * P, :], h2[:, t, :]).then_inc(s_out, 16)
                    sp.wait_ge(s_out, 16 * LT)

                @block.gpsimd
                def _(pool):
                    def rows(table, buf, slot, ready, par, e):
                        pool.indirect_dma_start(out=buf[:, slot, :], out_offset=None, in_=table,
                                                in_offset=bass.IndirectOffsetOnAxis(ap=stage[:, par, e:e + 1], axis=0)).then_inc(ready[slot], 16)

                    def u_rows(n, par, e):
                        pool.wait_ge(s_udone, GROUP * n + e + 1)
                        pool.sem_inc(s_passed)
                        rows(peer_u, Ub, e, s_u, par, e)

                    def v_rows(n, par, e):
                        pool.wait_ge(s_vdone, GROUP * n + e + 1)
                        pool.sem_inc(s_passed)
                        rows(peer_v, Vb, e, s_v, par, e)

                    def stage_in(n, par):
                        pool.tensor_copy(stage[:, par, :], eidx[:, bass.ds(n, 1), :].rearrange("p a b -> p (a b)")).then_inc(s_idx, 1)
                        pool.wait_ge(s_idx, n + 1)
                        pool.sem_inc(s_passed)

                    def turn(n, i, more):
                        v_rows(n, i, 0); v_rows(n, i, 1)
                        if more:
                            stage_in(n + 1, 1 - i)
                            u_rows(n + 1, 1 - i, 0); u_rows(n + 1, 1 - i, 1)

                    stage_in(0, 0)
                    for e in range(GROUP):
                        u_rows(0, 0, e)
                    with pool.Fori(0, NG // 2 - 1) as r:
                        turn(2 * r, 0, True)
                        turn(2 * r + 1, 1, True)
                    turn(NG - 2, 0, True)
                    turn(NG - 1, 1, False)
                    for t in range(LT):
                        pool.wait_ge(s_gained, t + 1)
                        pool.tensor_tensor(h2[:, t, :], h2[:, t, :], lng[:, 1, :], ALU.add).then_inc(s_y, 1)

                @block.tensor
                def _(pe):
                    def dense_out(n):
                        pe.wait_ge(s_m, n + 1)
                        for o in range(NOUT):
                            c, t = o // DT, o % DT
                            if t == 0:
                                pe.wait_ge(s_vl, OUT_CHUNKS * n + c + 1)
                            pe.wait_ge(s_add, NOUT * n + o + 1)
                            dst, tok = PS[:, 2 + o % OB, :], slice(t * P, (t + 1) * P)
                            for j in range(GROUP):
                                pe.matmul(dst, AH[:, j, tok], VH[:, j, chunk[c]], start=(j == 0), stop=False)
                                pe.matmul(dst, AH[:, j, tok], VL[:, j, chunk[c]], start=False, stop=False)
                                last = pe.matmul(dst, AL[:, j, tok], VH[:, j, chunk[c]], start=False, stop=(j == GROUP - 1))
                            last.then_inc(s_po, 1)

                    with pe.Fori(0, NG - 1) as n:
                        dense_dots(pe, n + 1); dense_out(n)
                    dense_out(NG - 1)

                @block.scalar
                def _(act):
                    def v_high(n, c):
                        act.wait_ge(s_vb[c], 16 * n + 16)
                        act.activation(VH[:, :, chunk[c]], VR[:, :, chunk[c]], ACT.Copy).then_inc(s_vh, 1)

                    def turn(n, more, last=False):
                        for c in range(OUT_CHUNKS):
                            v_high(n, c)
                        if more:
                            u_high(act, n + 2, 0)
                        act.wait_ge(s_act, n + 1)
                        act.activation(dots[:], dots[:], ACT.Gelu).then_inc(s_dgelu, 1)
                        if not last:
                            act.wait_ge(s_m, n + 1)
                            dense_gelu(act, n + 1)
                        if more:
                            u_high(act, n + 2, 1)

                    with act.Fori(0, NG - 2) as n:
                        turn(n, True)
                    turn(NG - 2, False); turn(NG - 1, False, True)
                    for t in range(LT):
                        act.wait_ge(s_stat4, t + 1)
                        act.activation(rsd[:, t:t + 1], rsd[:, t:t + 1], ACT.Sqrt).then_inc(s_std4, 1)
                        act.wait_ge(s_nmr4, t + 1)
                        act.activation(h2[:, t, :], h2[:, t, :], ACT.Identity, scale=rsd[:, t:t + 1], bias=nmr[:, t:t + 1]).then_inc(s_z4, 1)

                @block.vector
                def _(dve):
                    def v_low(n, c):
                        dve.wait_ge(s_vh, OUT_CHUNKS * n + c + 1)
                        dve.tensor_tensor(VL[:, :, chunk[c]], VR[:, :, chunk[c]], VHf[:, :, chunk[c]], ALU.subtract).then_inc(s_vl, 1)

                    def gated(n):
                        dve.wait_ge(s_ge, n + 2)
                        dve.wait_ge(s_gb, 16 * n + 16)
                        dve.tensor_tensor(gl[:], gl[:], GB[:], ALU.mult)
                        dve.drain()
                        dve.tensor_copy(AH[:], gl[:])
                        dve.drain()
                        dve.tensor_tensor(AL[:], gl[:], AHf, ALU.subtract).then_inc(s_m, 1)

                    def add(n, o):
                        part = x1[:, o % DT, chunk[o // DT]]
                        dve.wait_ge(s_po, NOUT * n + o + 1)
                        dve.tensor_tensor(part, PS[:, 2 + o % OB, :], part, ALU.add).then_inc(s_add, 1)

                    def u_dot(n, e):
                        dve.wait_ge(s_u[e], 16 * n + 16)
                        dve.scalar_tensor_tensor(Ub[:, e, :], Ub[:, e, :], 1.0, h2[:, DT, :], ALU.mult, ALU.mult,
                                                 accum_out=dots[:, e:e + 1]).then_inc(s_udone, 1)

                    def v_sum(n, e):
                        dve.wait_ge(s_v[e], 16 * n + 16)
                        dve.scalar_tensor_tensor(x1[:, DT, :], Vb[:, e, :], coef[:, e:e + 1], x1[:, DT, :], ALU.mult, ALU.add).then_inc(s_vdone, 1)

                    def turn(n, more):
                        gated(n)
                        for c in range(OUT_CHUNKS):
                            v_low(n, c)
                        u_dot(n, 0); u_dot(n, 1)
                        dve.drain().then_inc(s_act, 1)
                        if more:
                            u_low(dve, n + 2, 0)
                        add(n, 0); add(n, 1)
                        dve.wait_ge(s_dgelu, n + 1)
                        dve.tensor_tensor(coef[:], dots[:], gate[:, bass.ds(n, 1), :].rearrange("p a b -> p (a b)"), ALU.mult)
                        add(n, 2); add(n, 3)
                        if more:
                            u_low(dve, n + 2, 1)
                        add(n, 4); add(n, 5); add(n, 6)
                        dve.drain()
                        v_sum(n, 0)
                        add(n, 7); add(n, 8); add(n, 9)
                        dve.drain()
                        v_sum(n, 1)
                        add(n, 10); add(n, 11)
                        dve.drain()

                    for s, credits in ((s_udone, GROUP), (s_vdone, GROUP), (s_add, OB)):
                        for _ in range(credits):
                            dve.drain().then_inc(s, 1)
                    for t in range(LT):
                        dve.memset(x1[:, t, :], 0.0)
                    with dve.Fori(0, NG - 2) as n:
                        turn(n, True)
                    turn(NG - 2, False); turn(NG - 1, False)
                    dve.drain().then_inc(s_gdone, 1)
                    def gained(t):
                        dve.wait_ge(s_z4, t + 1)
                        if t == 0:
                            dve.wait_ge(s_ln4, 32)
                        dve.tensor_tensor(h2[:, t, :], h2[:, t, :], lng[:, 0, :], ALU.mult).then_inc(s_gained, 1)

                    for t in range(LT):
                        dve.tensor_tensor(x1[:, t, :], x1[:, t, :], vecs[:, 3, :], ALU.mult)
                        dve.drain()
                        dve.wait_ge(s_back[t], 16)
                        dve.scalar_tensor_tensor(h2[:, t, :], h2[:, t, :], ALPHA, x1[:, t, :], ALU.mult, ALU.add)
                        dve.drain()
                        for i in range(4):
                            dve.bn_stats(st6[:, t, i, :], h2[:, t, i * 512:(i + 1) * 512])
                        dve.drain()
                        row_stats(dve, [t], s_stat4, s_std4, t + 1).then_inc(s_nmr4, 1)
                        if t:
                            gained(t - 1)
                    gained(LT - 1)


def constants():
    turn = np.zeros((P, P), np.float32)
    nf = HALF // 4
    for m in range(P):
        if m % (2 * nf) < nf:
            turn[m + nf, m] = -1.0
        else:
            turn[m - nf, m] = 1.0
    iota = np.tile(np.arange(TOPK, dtype=np.float32), (P, 1))
    inv = (np.float32(10000.0) ** (-np.arange(nf, dtype=np.float32) / np.float32(nf))).astype(np.float32)
    tok = np.arange(SEQ)
    pos = np.stack([tok // GRID_W, tok % GRID_W]).astype(np.float32)
    f = np.arange(P)
    ang = pos[(f % HALF) // (HALF // 2)] * inv[f % nf][:, None]
    rope = np.concatenate([np.cos(ang), np.sin(ang)], 1).astype(np.float32)
    token = (np.arange(P)[:, None] + P * np.arange(DT)[None, :]).astype(np.float32)
    return np.concatenate([np.eye(P, dtype=np.float32), turn, iota, token], 1), rope


def kernel(x, c, ctx, c_ctx, w_ada, b_ada, w_in, conv_w, conv_b, gate_b, diff_lambda, diff_norm_g,
           mlstm_norm_g, w_out, ln1_g, ln1_b, ln2_g, ln2_b, peer_wq, peer_keys, peer_u, peer_v):
    import concourse.bacc as bacc
    from concourse.bass_utils import run_bass_kernel_spmd

    con = np.ascontiguousarray
    w_in = np.asarray(w_in)[0]
    b_ada = np.asarray(b_ada)[0]
    w = w_in[:, :NPROJ * H * HD].reshape(4, QK, P, NPROJ, H, HD)[:, :, :, [3, 4, 5, 6, 0, 1, 2]]
    consts, rope = constants()
    arrays = {
        "xT": con(np.asarray(x)[0].T), "x": con(np.asarray(x)[0]), "cxT": con(np.asarray(ctx)[0].T),
        "ccol": con(np.concatenate([np.asarray(c)[0].reshape(KT, P).T, np.asarray(c_ctx).reshape(KT, P).T], 1)),
        "wada": con(np.asarray(w_ada)[0]), "bcol": con(b_ada[:2 * D].reshape(2 * KT, P).T), "brow": con(b_ada[2 * D:].reshape(4, D)),
        "wseq": con(w.transpose(4, 3, 0, 2, 1, 5).reshape(QUARTERS, P, QK, P)),
        "wgate": con(w_in[:, 7 * H * HD:]), "gbias": con(np.asarray(gate_b)[0].reshape(NGATES * H, 1)),
        "convw": con(np.asarray(conv_w)[0].reshape(CONV, 2 * H, HD).transpose(2, 1, 0).reshape(P, 2 * H * CONV)),
        "convb": con(np.asarray(conv_b)[0].reshape(2 * H, HD).T),
        "lamv": con(np.asarray(diff_lambda)[0].reshape(1, 4 * HALF)),
        "gcol": con(np.stack([np.asarray(diff_norm_g)[0], np.asarray(mlstm_norm_g)[0]], 1)),
        "wout": con(np.asarray(w_out)[0]),
        "lnv": con(np.stack([np.asarray(a)[0] for a in (ln1_g, ln1_b, ln2_g, ln2_b)])),
        "wq": con(np.asarray(peer_wq)[0].reshape(KT, P, 2 * PH, P).transpose(2, 1, 0, 3)),
        "keysT": con(np.asarray(peer_keys)[0].transpose(3, 1, 0, 2).reshape(P, 2 * PH * NKEYS)),
        "peer_u": con(np.asarray(peer_u)[0]), "peer_v": con(np.asarray(peer_v)[0]),
        "peer_ut": con(np.asarray(peer_u)[0].reshape(NEB, P, KT, P).transpose(0, 3, 2, 1)),
        "consts": consts, "rope": rope,
    }
    nc = bacc.Bacc("TRN2", target_bir_lowering=False, num_devices=1)
    aps = {n: nc.dram_tensor(n, a.shape, mybir.dt.from_np(a.dtype), kind="ExternalInput").ap() for n, a in arrays.items()}
    aps["out"] = nc.dram_tensor("out", (SEQ, D), mybir.dt.float32, kind="ExternalOutput").ap()
    program(nc, **aps)
    r = run_bass_kernel_spmd(nc, [arrays], core_ids=[0])
    return r.results[0]["out"].reshape(1, SEQ, D)
```
